# Optimizing a Trainium2 kernel written in Bass

```python
import jax
import jax.numpy as jnp
from jax import lax
import numpy as np

D_MODEL = 1024
BATCH = 1
SEQ = 2048
DEPTH = 1
DEC_BATCH = 1
DEC_SEQ = 1024
PAST_LEN = 128

N_HEADS_A = 8
D_A = D_MODEL // 2
HEAD_DIM = D_A // N_HEADS_A
N_GROUPS_B = 4
D_B = D_MODEL // 4
GROUP_DIM_B = D_B // N_GROUPS_B
N_HEADS_C = 4
D_C = D_MODEL // 4
HEAD_DIM_C = D_C // N_HEADS_C
D_MIX = D_A + D_B + D_C
D_IN = 3 * D_A + 2 * D_B + D_C
DILATED_PATTERNS = ((128, 1), (512, 4), (2048, 16))
Q_BLOCK = 128
CHUNK_B = 128
N_MEM = 256
N_EXPERTS = 16
EC_CAPACITY_FACTOR = 2
D_EXPERT = D_MODEL
ROPE_THETA = 10000.0
EPS = 1e-6
NEG_INF = -1e30

kernel_name = 'hybrid_dilated_gmlp_ec_encoder'

def rmsnorm(x, g):
    xf = x.astype(jnp.float32)
    y = xf * lax.rsqrt(jnp.mean(xf * xf, axis=-1, keepdims=True) + EPS)
    return (y * g.astype(jnp.float32)).astype(x.dtype)

def layernorm(x, g, b):
    xf = x.astype(jnp.float32)
    mu = jnp.mean(xf, axis=-1, keepdims=True)
    var = jnp.mean(jnp.square(xf - mu), axis=-1, keepdims=True)
    y = (xf - mu) * lax.rsqrt(var + EPS)
    return (y * g.astype(jnp.float32) + b.astype(jnp.float32)).astype(x.dtype)

def rope(x):
    s, dh = x.shape[1], x.shape[-1]
    half = dh // 2
    inv_freq = jnp.power(ROPE_THETA, -jnp.arange(half, dtype=jnp.float32) * 2.0 / dh)
    ang = jnp.arange(s, dtype=jnp.float32)[:, None] * inv_freq[None, :]
    cos = jnp.cos(ang)[None, :, None, :]
    sin = jnp.sin(ang)[None, :, None, :]
    xf = x.astype(jnp.float32)
    x1, x2 = xf[..., :half], xf[..., half:]
    return jnp.concatenate([x1 * cos - x2 * sin, x2 * cos + x1 * sin], axis=-1).astype(x.dtype)

def banded_attention(q, k, v, radius):
    n, l, h, dh = q.shape
    nb = -(-l // Q_BLOCK)
    lp = nb * Q_BLOCK
    qb = jnp.pad(q, ((0, 0), (0, lp - l), (0, 0), (0, 0))).reshape(n, nb, Q_BLOCK, h, dh)
    kv_pad = ((0, 0), (radius, lp + Q_BLOCK - l - radius), (0, 0), (0, 0))
    kp = jnp.pad(k, kv_pad).reshape(n, nb + 1, Q_BLOCK, h, dh)
    vp = jnp.pad(v, kv_pad).reshape(n, nb + 1, Q_BLOCK, h, dh)
    kb = jnp.concatenate([kp[:, :-1], kp[:, 1:]], axis=2)
    vb = jnp.concatenate([vp[:, :-1], vp[:, 1:]], axis=2)
    t = jnp.arange(Q_BLOCK)[:, None]
    s = jnp.arange(2 * Q_BLOCK)[None, :]
    kpos = jnp.arange(nb)[:, None, None] * Q_BLOCK + s[None] - radius
    mask = (jnp.abs(s - radius - t)[None] <= radius) & (kpos >= 0) & (kpos < l)
    scores = jnp.einsum('nbqhd,nbkhd->nbhqk', qb, kb, preferred_element_type=jnp.float32) * (dh ** -0.5)
    scores = jnp.where(mask[None, :, None], scores, NEG_INF)
    m = jnp.max(scores, axis=-1, keepdims=True)
    p = jnp.exp(scores - m)
    den = jnp.sum(p, axis=-1)
    o = jnp.einsum('nbhqk,nbkhd->nbqhd', p.astype(v.dtype), vb, preferred_element_type=jnp.float32)
    o = o / jnp.swapaxes(den, -1, -2)[..., None]
    lse = jnp.swapaxes(m[..., 0] + jnp.log(den), -1, -2)
    return o.reshape(n, lp, h, dh)[:, :l], lse.reshape(n, lp, h)[:, :l]

def dilated_attention(q, k, v):
    b, s, h, dh = q.shape
    outs, lses = [], []
    for window, dil in DILATED_PATTERNS:
        radius = window // (2 * dil)
        sub = s // dil
        def by_residue(t):
            return t.reshape(b, sub, dil, h, dh).transpose(0, 2, 1, 3, 4).reshape(b * dil, sub, h, dh)
        o, lse = banded_attention(by_residue(q), by_residue(k), by_residue(v), radius)
        outs.append(o.reshape(b, dil, sub, h, dh).transpose(0, 2, 1, 3, 4).reshape(b, s, h, dh))
        lses.append(lse.reshape(b, dil, sub, h).transpose(0, 2, 1, 3).reshape(b, s, h))
    w = jax.nn.softmax(jnp.stack(lses), axis=0)
    return jnp.einsum('pbsh,pbshd->bshd', w, jnp.stack(outs))

def spatial_gating(uv, ln_g, ln_b, w_s, b_s):
    b, s, _ = uv.shape
    uv = jax.nn.gelu(uv)
    u, v = uv[..., :D_B], uv[..., D_B:]
    v = layernorm(v, ln_g, ln_b).reshape(b, s // CHUNK_B, CHUNK_B, N_GROUPS_B, GROUP_DIM_B)
    v = jnp.einsum('gts,bcsgd->bctgd', w_s, v) + b_s.T[None, None, :, :, None]
    return u * v.reshape(b, s, D_B)

def memory_attention(q, mem, g_mem, w_kv):
    b, s, _ = q.shape
    m = mem.shape[1]
    kv = rmsnorm(mem, g_mem) @ w_kv
    k = kv[..., :D_C].reshape(b, m, N_HEADS_C, HEAD_DIM_C)
    v = kv[..., D_C:].reshape(b, m, N_HEADS_C, HEAD_DIM_C)
    q = q.reshape(b, s, N_HEADS_C, HEAD_DIM_C)
    scores = jnp.einsum('bshd,bmhd->bhsm', q, k, preferred_element_type=jnp.float32) * (HEAD_DIM_C ** -0.5)
    p = jax.nn.softmax(scores, axis=-1)
    o = jnp.einsum('bhsm,bmhd->bshd', p.astype(v.dtype), v)
    return o.reshape(b, s, D_C)

def expert_choice(xn, w_router, w_gate, w_up, w_down):
    shp = xn.shape
    xt = xn.reshape(-1, shp[-1])
    t = xt.shape[0]
    cap = EC_CAPACITY_FACTOR * t // N_EXPERTS
    aff = jax.nn.softmax((xt @ w_router).astype(jnp.float32), axis=-1)
    g, idx = lax.top_k(aff.T, cap)
    xe = xt[idx]
    hdn = jax.nn.silu(jnp.einsum('ecd,edf->ecf', xe, w_gate)) * jnp.einsum('ecd,edf->ecf', xe, w_up)
    ye = jnp.einsum('ecf,efd->ecd', hdn, w_down)
    ye = ye * g[..., None].astype(ye.dtype)
    y = jnp.zeros_like(xt).at[idx.reshape(-1)].add(ye.reshape(-1, shp[-1]))
    return y.reshape(shp)

def encoder(x, mem, g_mix, w_in, ln_b_g, ln_b_b, w_spatial, b_spatial, g_mem, w_mem_kv,
            g_out, w_out, g_ffn, w_router, w_gate, w_up, w_down, g_final):
    b, s, _ = x.shape
    for l in range(DEPTH):
        h = rmsnorm(x, g_mix[l])
        z = h @ w_in[l]
        q_a = rope(z[..., :D_A].reshape(b, s, N_HEADS_A, HEAD_DIM))
        k_a = rope(z[..., D_A:2 * D_A].reshape(b, s, N_HEADS_A, HEAD_DIM))
        v_a = z[..., 2 * D_A:3 * D_A].reshape(b, s, N_HEADS_A, HEAD_DIM)
        uv_b = z[..., 3 * D_A:3 * D_A + 2 * D_B]
        q_c = z[..., 3 * D_A + 2 * D_B:]
        o_a = dilated_attention(q_a, k_a, v_a).astype(x.dtype).reshape(b, s, D_A)
        o_b = spatial_gating(uv_b, ln_b_g[l], ln_b_b[l], w_spatial[l], b_spatial[l])
        o_c = memory_attention(q_c, mem, g_mem[l], w_mem_kv[l])
        go = g_out[l]
        o = jnp.concatenate([rmsnorm(o_a, go[:D_A]),
                             rmsnorm(o_b, go[D_A:D_A + D_B]),
                             rmsnorm(o_c, go[D_A + D_B:])], axis=-1)
        x = x + o @ w_out[l]
        x = x + expert_choice(rmsnorm(x, g_ffn[l]), w_router[l], w_gate[l], w_up[l], w_down[l])
    return rmsnorm(x, g_final)

def setup_inputs(seed: int = 0) -> dict:
    key = jax.random.key(seed)
    ks = jax.random.split(key, 20)
    f32 = jnp.float32

    def nrm(k, shape, scale):
        return jax.random.normal(k, shape, f32) * scale

    def gain(k, shape):
        return 1.0 + 0.05 * jax.random.normal(k, shape, f32)

    return {
        'x_prompt': nrm(ks[0], (BATCH, SEQ, D_MODEL), 1.0),
        'x_sample': nrm(ks[1], (DEC_BATCH, DEC_SEQ, D_MODEL), 1.0),
        'mem_prompt': nrm(ks[2], (BATCH, N_MEM, D_MODEL), 1.0),
        'mem_sample': nrm(ks[3], (DEC_BATCH, N_MEM, D_MODEL), 1.0),
        'g_mix': gain(ks[4], (DEPTH, D_MODEL)),
        'w_in': nrm(ks[5], (DEPTH, D_MODEL, D_IN), D_MODEL ** -0.5),
        'ln_b_g': gain(ks[6], (DEPTH, D_B)),
        'ln_b_b': nrm(ks[7], (DEPTH, D_B), 0.02),
        'w_spatial': nrm(ks[8], (DEPTH, N_GROUPS_B, CHUNK_B, CHUNK_B), CHUNK_B ** -0.5),
        'b_spatial': gain(ks[9], (DEPTH, N_GROUPS_B, CHUNK_B)),
        'g_mem': gain(ks[10], (DEPTH, D_MODEL)),
        'w_mem_kv': nrm(ks[11], (DEPTH, D_MODEL, 2 * D_C), D_MODEL ** -0.5),
        'g_out': gain(ks[12], (DEPTH, D_MIX)),
        'w_out': nrm(ks[13], (DEPTH, D_MIX, D_MODEL), D_MIX ** -0.5),
        'g_ffn': gain(ks[14], (DEPTH, D_MODEL)),
        'w_router': nrm(ks[15], (DEPTH, D_MODEL, N_EXPERTS), D_MODEL ** -0.5),
        'w_gate': nrm(ks[16], (DEPTH, N_EXPERTS, D_MODEL, D_EXPERT), D_MODEL ** -0.5),
        'w_up': nrm(ks[17], (DEPTH, N_EXPERTS, D_MODEL, D_EXPERT), D_MODEL ** -0.5),
        'w_down': nrm(ks[18], (DEPTH, N_EXPERTS, D_EXPERT, D_MODEL), D_EXPERT ** -0.5),
        'g_final': gain(ks[19], (D_MODEL,)),
    }

def reference(x_prompt, x_sample, mem_prompt, mem_sample, g_mix, w_in, ln_b_g, ln_b_b,
              w_spatial, b_spatial, g_mem, w_mem_kv, g_out, w_out, g_ffn, w_router,
              w_gate, w_up, w_down, g_final):
    y_prompt = encoder(x_prompt, mem_prompt, g_mix, w_in, ln_b_g, ln_b_b, w_spatial, b_spatial,
                       g_mem, w_mem_kv, g_out, w_out, g_ffn, w_router, w_gate, w_up, w_down, g_final)
    y_sample = encoder(x_sample, mem_sample, g_mix, w_in, ln_b_g, ln_b_b, w_spatial, b_spatial,
                       g_mem, w_mem_kv, g_out, w_out, g_ffn, w_router, w_gate, w_up, w_down, g_final)
    return (y_prompt, y_sample)


_drawn_inputs = setup_inputs


def setup_inputs(seed=0):
    import zlib

    import numpy as np

    out = dict(_drawn_inputs(seed))
    spreads = {}
    factors = {'ln_b_g': 3.589, 'ln_b_b': 7.028, 'b_spatial': 4.054, 'g_ffn': 2.901}
    for name, (base, spread) in spreads.items():
        noise = np.random.default_rng([zlib.crc32(name.encode()), seed]).standard_normal(out[name].shape)
        drawn = base * np.exp(spread * noise) if base else spread * noise
        out[name] = jnp.asarray(drawn.astype(out[name].dtype))
    for name, factor in factors.items():
        out[name] = (out[name] * factor).astype(out[name].dtype)
    return out
```

```python
from contextlib import ExitStack

import numpy as np

import concourse.bass as bass
from concourse import mybir

F32 = mybir.dt.float32
F32R = mybir.dt.float32r
BF16 = mybir.dt.bfloat16
I32 = mybir.dt.int32
U32 = mybir.dt.uint32
ACT = mybir.ActivationFunctionType
ALU = mybir.AluOpType
AX_X = mybir.AxisListType.X

P = 128
D = 1024
KC = D // P
SEQS = (2048, 1024)
TOK = sum(SEQS)
NT = TOK // P
NTP = SEQS[0] // P
PAIRS = NT // 2
PAIRS_P = NTP // 2
HA, HD = 8, 64
D_A = HA * HD
D_B = 256
GB, GD = 4, 64
HC = 4
D_C = HC * HD
D_IN = 3 * D_A + 2 * D_B + D_C
MEM = 256
NE = 16
EPS = 1e-6
SCALE = HD ** -0.5
NEG = -1e30
PAD = 256
KV_ROWS = sum(s + 2 * PAD for s in SEQS)
KV_BASE = (PAD, SEQS[0] + 3 * PAD)
O_COLS = D_A + 2 * HA
XN_COLS = D + NE
CAPS = tuple(2 * s // NE for s in SEQS)
ST = sum(CAPS) // P
BITS = 30
GELU_C = 2.0 * (2.0 / np.pi) ** 0.5


def ge(eng, sem, value):
    if isinstance(value, int) and value <= 0:
        return
    eng.wait_ge(sem, value)


def bank_of(h):
    return h % 2 * 2 + h // 2


class Phase:

    def __init__(self, nc, name):
        self.nc, self.name, self.ctx, self.sems = nc, name, ExitStack(), []

    def __enter__(self):
        return self

    def __exit__(self, *e):
        self.ctx.close()
        if self.sems:
            self.nc.clear_and_free_semaphores(self.sems)
            self.nc.all_engine_barrier()

    def sb(self, name, shape, dt=F32):
        return self.ctx.enter_context(self.nc.sbuf_tensor(f"{self.name}_{name}", shape, dt))

    def psum(self, name, shape):
        return self.ctx.enter_context(self.nc.psum_tensor(f"{self.name}_{name}", shape, F32))

    def sem(self, name):
        self.sems.append(self.nc.alloc_semaphore(f"{self.name}_{name}"))
        return self.sems[-1]


def memory_phase(nc, A, kmT, vm):
    NM = 2 * MEM // P
    with Phase(nc, "mem") as ph:
        ident = ph.sb("ident", [P, P])
        m = ph.sb("rows", [P, NM, D])
        w = ph.sb("w", [P, KC, 2 * D_C])
        g = ph.sb("g", [P, KC])
        junk = ph.sb("junk", [P, D], BF16)
        ss = ph.sb("ss", [P, NM])
        ms = ph.sb("ms", [P, NM])
        rstd = ph.sb("rstd", [P, NM])
        half = ph.sb("half", [P, NM])
        mT = ph.sb("mT", [P, KC, P])
        kt = ph.sb("k", [P, D_C])
        zero = ph.sb("zero", [P, D])
        psT = ph.psum("psT", [P, KC, P])
        psKV = ph.psum("psKV", [P, 2 * D_C])
        psK = ph.psum("psK", [P, 4, P])
        loaded, zeroed, padded = ph.sem("loaded"), ph.sem("zeroed"), ph.sem("padded")
        squared, meaned, powered, scaled = (ph.sem(x) for x in ("squared", "meaned", "powered", "scaled"))
        w_scaled, turned, turned_sb, kv_ps = (ph.sem(x) for x in ("w_scaled", "turned", "turned_sb", "kv_ps"))
        k_sb, v_sb, kT_ps, kT_sb, half_set = (ph.sem(x) for x in ("k_sb", "v_sb", "kT_ps", "kT_sb", "half_set"))
        with nc.Block() as block:
            @block.sync
            def _(sp):
                sp.dma_start(m[:], A["mem"].rearrange("(n p) d -> p n d", p=P)).then_inc(loaded, 16)
                sp.dma_start(w[:], A["w_mem_kv"].rearrange("(n p) d -> p n d", p=P)).then_inc(loaded, 16)
                sp.dma_start(g[:], A["g_mem"]).then_inc(loaded, 16)
                sp.dma_start(ident[:], A["ident"]).then_inc(loaded, 16)
                sp.wait_ge(zeroed, 1)
                row = 0
                pads = 0
                for s in SEQS:
                    for r in (row, row + PAD + s):
                        for j in range(0, PAD, P):
                            sp.dma_start(A["kv"][r + j:r + j + P, :], zero[:]).then_inc(padded, 16)
                            pads += 1
                    row += s + 2 * PAD
                sp.wait_ge(padded, 16 * pads)

            @block.gpsimd
            def _(pool):
                nc.gpsimd.memset(half[:], -0.5).then_inc(half_set, 1)
                pool.wait_ge(half_set, 1)
                pool.wait_ge(meaned, 1)
                nc.gpsimd.tensor_tensor(rstd[:], ms[:], half[:], ALU.pow).then_inc(powered, 1)

            @block.scalar
            def _(act):
                act.wait_ge(loaded, 64)
                for n in range(NM):
                    if n:
                        act.wait_ge(squared, n)
                    nc.scalar.activation(junk[:], m[:, n, :], ACT.Square, accum_out=ss[:, n:n + 1]).then_inc(squared, 1)
                act.wait_ge(powered, 1)
                for n in range(NM):
                    nc.scalar.activation(m[:, n, :], m[:, n, :], ACT.Copy, scale=rstd[:, n:n + 1]).then_inc(scaled, 1)
                for n in range(NM):
                    act.wait_ge(kv_ps, n + 1)
                    if n:
                        act.wait_ge(kT_ps, n)
                    nc.scalar.activation(kt[:], psKV[:, 0:D_C], ACT.Copy).then_inc(k_sb, 1)
                    nc.scalar.activation(vm[:, n // 2, n % 2, :], psKV[:, D_C:], ACT.Copy).then_inc(v_sb, 1)

            @block.vector
            def _(dve):
                nc.vector.memset(zero[:], 0.0).then_inc(zeroed, 1)
                dve.wait_ge(loaded, 64)
                for k in range(KC):
                    nc.vector.tensor_scalar(w[:, k, :], w[:, k, :], g[:, k:k + 1], None, ALU.mult).then_inc(w_scaled, 1)
                dve.wait_ge(squared, NM)
                nc.vector.tensor_scalar(ms[:], ss[:], 1.0 / D, EPS, ALU.mult, ALU.add).then_inc(meaned, 1)
                for n in range(NM):
                    dve.wait_ge(turned, n + 1)
                    if n:
                        dve.wait_ge(kv_ps, n)
                    nc.vector.tensor_copy(mT[:], psT[:]).then_inc(turned_sb, 1)
                    dve.wait_ge(kT_ps, n + 1)
                    nc.vector.tensor_copy(kmT[:, n // 2, :, (n % 2) * P:(n % 2 + 1) * P], psK[:, 0:2, :]).then_inc(kT_sb, 1)

            @block.tensor
            def _(pe):
                pe.wait_ge(w_scaled, KC)
                for n in range(NM):
                    pe.wait_ge(scaled, n + 1)
                    for k in range(KC):
                        last = nc.tensor.transpose(psT[:, k, :], m[:, n, k * P:(k + 1) * P], ident[:])
                    last.then_inc(turned, 1)
                    pe.wait_ge(turned_sb, n + 1)
                    if n:
                        pe.wait_ge(k_sb, n)
                        pe.wait_ge(v_sb, n)
                    for k in range(KC):
                        last = nc.tensor.matmul(psKV[:], mT[:, k, :], w[:, k, :], start=(k == 0), stop=(k == KC - 1))
                    last.then_inc(kv_ps, 1)
                    pe.wait_ge(k_sb, n + 1)
                    if n:
                        pe.wait_ge(kT_sb, n)
                    for j in range(2):
                        last = nc.tensor.transpose(psK[:, j, :], kt[:, j * P:(j + 1) * P], ident[:])
                    last.then_inc(kT_ps, 1)


def split_weights(nc, ph, dram, g, g_loaded, w_hi, w_lo, cols):
    with Phase(nc, ph.name + "_split") as sp_:
        stage = sp_.sb("stage", [P, 2, cols])
        loaded = [sp_.sem(f"loaded{i}") for i in range(2)]
        hi_done, lo_done = sp_.sem("hi_done"), sp_.sem("lo_done")
        with nc.Block() as block:
            @block.sync
            def _(sp):
                for k in range(KC):
                    ge(sp, lo_done, k - 1)
                    sp.dma_start(stage[:, k % 2, :], dram[k * P:(k + 1) * P, :]).then_inc(loaded[k % 2], 16)

            @block.scalar
            def _(act):
                act.wait_ge(g_loaded, 16)
                for k in range(KC):
                    act.wait_ge(loaded[k % 2], 16 * (k // 2 + 1))
                    nc.scalar.activation(w_hi[:, k, :], stage[:, k % 2, :], ACT.Copy, scale=g[:, k:k + 1]).then_inc(hi_done, 1)

            @block.vector
            def _(dve):
                for k in range(KC):
                    dve.wait_ge(hi_done, k + 1)
                    nc.vector.scalar_tensor_tensor(out=w_lo[:, k, :], in0=stage[:, k % 2, :], scalar=g[:, k:k + 1],
                                                   in1=w_hi[:, k, :].bitcast(F32), op0=ALU.mult,
                                                   op1=ALU.subtract).then_inc(lo_done, 1)


def project_phase(nc, A, kmT, vm):
    with Phase(nc, "prj") as ph:
        ident = ph.sb("ident", [P, P])
        w_hi = ph.sb("w_hi", [P, KC, D_IN], F32R)
        w_lo = ph.sb("w_lo", [P, KC, D_IN], F32R)
        g = ph.sb("g", [P, KC])
        consts = ph.sem("consts")
        g_loaded = ph.sem("g_loaded")
        with nc.Block() as block:
            @block.sync
            def _(sp):
                sp.dma_start(g[:], A["g_mix"]).then_inc(g_loaded, 16)
                sp.dma_start(ident[:], A["ident"]).then_inc(consts, 16)
                sp.wait_ge(consts, 16)
                sp.wait_ge(g_loaded, 16)
        split_weights(nc, ph, A["w_in"], g, g_loaded, w_hi, w_lo, D_IN)

        x = ph.sb("x", [P, 2, D])
        cs = ph.sb("cs", [P, 2, 4, HD // 2])
        hT_hi = ph.sb("hT_hi", [P, 2, KC, P], F32R)
        hT_lo = ph.sb("hT_lo", [P, 2, KC, P], F32R)
        qkv = ph.sb("qkv", [P, 3, D_A])
        obc = ph.sb("obc", [P, D_B + D_C])
        uv_a = ph.sb("uv_a", [P, 2 * D_B])
        uv_b = ph.sb("uv_b", [P, 2 * D_B])
        rot_b = ph.sb("rot_b", [P, D_A])
        vln = ph.sb("vln", [P, D_B])
        ob = uv_b[:, 0:D_B]
        oc = ph.sb("oc", [P, D_C])
        qc = ph.sb("qc", [P, D_C])
        qcT = ph.sb("qcT", [P, 2, P])
        prob = ph.sb("prob", [P, HC, MEM])
        probT = ph.sb("probT", [P, 2 * HC, P])
        wsT = ph.sb("wsT", [P, GB, P])
        bs = ph.sb("bs", [P, GB])
        ln_g = ph.sb("ln_g", [P, D_B])
        ln_b = ph.sb("ln_b", [P, D_B])
        stat = ph.sb("stat", [P, 64])
        half = ph.sb("half", [P, 2])
        ssx, msx, rsx = stat[:, 0:1], stat[:, 1:2], stat[:, 2:3]
        bn6, mv, vev, rsv = stat[:, 4:10], stat[:, 10:12], stat[:, 12:13], stat[:, 13:14]
        mx, nmx, den, rden = stat[:, 16:20], stat[:, 20:24], stat[:, 24:28], stat[:, 28:32]
        ssb, ssc, msbc, rsbc = stat[:, 32:33], stat[:, 33:34], stat[:, 34:36], stat[:, 36:38]

        ps_x = ph.psum("ps_x", [P, 8, P])
        ps_a = ph.psum("ps_a", [P, 512])
        ps_b = ph.psum("ps_b", [P, 512])
        ps_c = ph.psum("ps_c", [P, 512])
        ps_s = ph.psum("ps_s", [P, HC, MEM])
        ps_o = ph.psum("ps_o", [P, 512])

        names = """squared_x meaned_x powered_x scaled_x z_qc z_uv z_q z_k z_v qc_sb qcT_ps qcT_sb sc_ps xT
            hi_sb lo_sb uv_sq inner0 inner g_exp g_exp1 g_rec guv bn_a bn_b var_eps rstd_v vn vn_g vln_sb sp_ps ob_sb
            rotq_a rotq rotq_sb rotk_a rotk rotk_sb maxed nmx_sb p_sb pT_ps pT_a pT_b v_sb pv_ps rden_sb oc_sb
            sq_b sq_c ms_bc rs_bc ob_out oc_out half_set""".split()
        s = {n: ph.sem(n) for n in names}
        x_loaded = [ph.sem(f"x_loaded{u}") for u in range(2)]
        q_stored, kv_stored, obc_stored = ph.sem("q_stored"), ph.sem("kv_stored"), ph.sem("obc_stored")

        def loop(eng, body, start=None):
            if start:
                start()
            with eng.Fori(0, PAIRS_P) as i:
                body(i, 0, False)
            with eng.Fori(PAIRS_P, PAIRS - 1) as i:
                body(i, 1, False)
            body(PAIRS - 1, 1, True)

        with nc.Block() as block:
            @block.sync
            def _(sp):
                for dst, src in ((wsT, "w_sT"), (bs, "b_sT"), (ln_g, "ln_g"), (ln_b, "ln_b")):
                    sp.dma_start(dst[:], A[src]).then_inc(consts, 16)

                def load(t, u):
                    sp.dma_start(x[:, u, :], A["x"][bass.ds(t * P, P), :]).then_inc(x_loaded[u], 16)
                    sp.dma_start(cs[:, u, :, :], A["cossin"][bass.ds(t * P, P), :]).then_inc(x_loaded[u], 16)

                def body(i, seq, last):
                    for u in range(2):
                        t = 2 * i + u
                        row = KV_BASE[seq] - (SEQS[0] if seq else 0)
                        sp.wait_ge(s["rotq_sb"], t + 1)
                        sp.dma_start(A["q"][bass.ds(t * P, P), :], qkv[:, 0, :]).then_inc(q_stored, 16)
                        sp.wait_ge(s["rotk_sb"], t + 1)
                        if not last:
                            sp.wait_ge(s["xT"], t + 1)
                            load(t + 2, u)
                        sp.wait_ge(s["v_sb"], t + 1)
                        sp.dma_start(A["kv"][bass.ds(t * P + row, P), :], qkv[:, 1:3, :]).then_inc(kv_stored, 16)
                        sp.wait_ge(s["ob_out"], t + 1)
                        sp.wait_ge(s["oc_out"], t + 1)
                        sp.dma_start(A["obc"][bass.ds(t * P, P), :], obc[:]).then_inc(obc_stored, 16)

                def start():
                    load(0, 0)
                    load(1, 1)
                loop(sp, body, start)
                for stored in (q_stored, kv_stored, obc_stored):
                    sp.wait_ge(stored, 16 * NT)

            @block.gpsimd
            def _(pool):
                nc.gpsimd.memset(half[:], -0.5).then_inc(s["half_set"], 1)
                pool.wait_ge(s["half_set"], 1)

                def prep(t):
                    pool.wait_ge(s["meaned_x"], t + 1)
                    ge(pool, s["scaled_x"], t)
                    nc.gpsimd.tensor_tensor(rsx, msx, half[:, 0:1], ALU.pow).then_inc(s["powered_x"], 1)

                def body(i, seq, last):
                    for u in range(2):
                        t = 2 * i + u
                        if not (last and u):
                            prep(t + 1)
                        pool.wait_ge(s["var_eps"], t + 1)
                        ge(pool, s["vn"], t)
                        nc.gpsimd.tensor_tensor(rsv, vev, half[:, 0:1], ALU.pow).then_inc(s["rstd_v"], 1)
                        pool.wait_ge(s["rotq"], t + 1)
                        nc.gpsimd.tensor_tensor(qkv[:, 0, :], qkv[:, 0, :], rot_b[:], ALU.add).then_inc(s["rotq_sb"], 1)
                        pool.wait_ge(s["rotk"], t + 1)
                        nc.gpsimd.tensor_tensor(qkv[:, 1, :], qkv[:, 1, :], rot_b[:], ALU.add).then_inc(s["rotk_sb"], 1)
                        pool.wait_ge(s["ms_bc"], t + 1)
                        ge(pool, s["oc_out"], t)
                        nc.gpsimd.tensor_tensor(rsbc, msbc, half[:], ALU.pow).then_inc(s["rs_bc"], 1)
                loop(pool, body, lambda: prep(0))

            @block.scalar
            def _(act):
                act.wait_ge(consts, 16 * 5)

                def square_x(t, u, n):
                    act.wait_ge(x_loaded[u], 32 * n)
                    ge(act, s["meaned_x"], t)
                    ge(act, s["pv_ps"], t - 1)
                    nc.scalar.activation(probT[:], x[:, u, :].rearrange("p (k c) -> p k c", c=P), ACT.Square, accum_out=ssx).then_inc(s["squared_x"], 1)

                def scale_x(t, u):
                    act.wait_ge(s["powered_x"], t + 1)
                    nc.scalar.activation(x[:, u, :], x[:, u, :], ACT.Copy, scale=rsx).then_inc(s["scaled_x"], 1)

                def hi_x(t, u):
                    act.wait_ge(s["xT"], t + 1)
                    ge(act, s["z_v"], t - 1)
                    nc.scalar.activation(hT_hi[:, u, :, :], ps_x[:], ACT.Copy).then_inc(s["hi_sb"], 1)

                def body(i, seq, last):
                    for u in range(2):
                        t = 2 * i + u
                        more = not (last and u)
                        n = i + 1 + u
                        act.wait_ge(s["z_qc"], t + 1)
                        ge(act, s["qcT_ps"], t)
                        nc.scalar.activation(qc[:], ps_a[:, 0:D_C], ACT.Copy).then_inc(s["qc_sb"], 1)
                        if more:
                            square_x(t + 1, 1 - u, n)
                        act.wait_ge(s["z_uv"], t + 1)
                        ge(act, s["guv"], t)
                        nc.scalar.activation(uv_a[:], ps_b[:], ACT.Square).then_inc(s["uv_sq"], 1)
                        act.wait_ge(s["qcT_ps"], t + 1)
                        ge(act, s["sc_ps"], t)
                        nc.scalar.activation(qcT[:], ps_s[:, 0, :], ACT.Copy).then_inc(s["qcT_sb"], 1)
                        if more:
                            scale_x(t + 1, 1 - u)
                        act.wait_ge(s["inner"], t + 1)
                        nc.scalar.activation(uv_a[:], uv_b[:], ACT.Exp, scale=-GELU_C).then_inc(s["g_exp"], 1)
                        if more:
                            hi_x(t + 1, 1 - u)
                        act.wait_ge(s["nmx_sb"], t + 1)
                        ge(act, s["pT_ps"], t)
                        ge(act, s["rden_sb"], t)
                        for h in range(HC):
                            j = bank_of(h)
                            last_exp = nc.scalar.activation(prob[:, h, :], ps_s[:, j, :], ACT.Exp, bias=nmx[:, j:j + 1],
                                                            scale=SCALE, accum_out=den[:, h:h + 1])
                        last_exp.then_inc(s["p_sb"], 1)
                        act.wait_ge(s["ob_sb"], t + 1)
                        ge(act, s["ms_bc"], t)
                        nc.scalar.activation(qc[:], ob, ACT.Square, accum_out=ssb).then_inc(s["sq_b"], 1)
                        act.wait_ge(s["pT_ps"], t + 1)
                        ge(act, s["pv_ps"], t)
                        nc.scalar.activation(probT[:, 0:HC, :], ps_x[:, 0:HC, :], ACT.Copy).then_inc(s["pT_a"], 1)
                        act.wait_ge(s["z_v"], t + 1)
                        ge(act, kv_stored, 16 * t)
                        nc.scalar.activation(qkv[:, 2, :], ps_b[:], ACT.Copy).then_inc(s["v_sb"], 1)
                        act.wait_ge(s["oc_sb"], t + 1)
                        act.wait_ge(s["sq_b"], t + 1)
                        nc.scalar.activation(qc[:], oc[:], ACT.Square, accum_out=ssc).then_inc(s["sq_c"], 1)
                        act.wait_ge(s["rs_bc"], t + 1)
                        ge(act, obc_stored, 16 * t)
                        nc.scalar.activation(obc[:, 0:D_B], ob, ACT.Copy, scale=rsbc[:, 0:1]).then_inc(s["ob_out"], 1)
                        nc.scalar.activation(obc[:, D_B:], oc[:], ACT.Copy, scale=rsbc[:, 1:2]).then_inc(s["oc_out"], 1)

                def start():
                    square_x(0, 0, 1)
                    scale_x(0, 0)
                    hi_x(0, 0)
                loop(act, body, start)

            @block.vector
            def _(dve):
                dve.wait_ge(consts, 16 * 5)

                def mean_x(t):
                    dve.wait_ge(s["squared_x"], t + 1)
                    ge(dve, s["powered_x"], t)
                    nc.vector.tensor_scalar(msx, ssx, 1.0 / D, EPS, ALU.mult, ALU.add).then_inc(s["meaned_x"], 1)

                def lo_x(t, u):
                    dve.wait_ge(s["hi_sb"], t + 1)
                    nc.vector.tensor_tensor(hT_lo[:, u, :, :], ps_x[:], hT_hi[:, u, :, :].bitcast(F32),
                                            ALU.subtract).then_inc(s["lo_sb"], 1)

                def rotate(z, out, u, first, second):
                    zh = z.rearrange("p (h two c) -> p h two c", h=HA, two=2)
                    ah = out.rearrange("p (h two c) -> p h two c", h=HA, two=2)
                    bh = rot_b[:].rearrange("p (h two c) -> p h two c", h=HA, two=2)
                    for j in range(2):
                        cos = cs[:, u, j:j + 1, :].broadcast_to([P, HA, HD // 2])
                        last_a = nc.vector.tensor_tensor(ah[:, :, j, :], zh[:, :, j, :], cos, ALU.mult)
                    last_a.then_inc(first, 1)
                    for j in range(2):
                        sin = cs[:, u, 2 + j:3 + j, :].broadcast_to([P, HA, HD // 2])
                        last_b = nc.vector.tensor_tensor(bh[:, :, j, :], zh[:, :, 1 - j, :], sin, ALU.mult)
                    last_b.then_inc(second, 1)

                def body(i, seq, last):
                    for u in range(2):
                        t = 2 * i + u
                        more = not (last and u)
                        if more:
                            mean_x(t + 1)
                        dve.wait_ge(s["uv_sq"], t + 1)
                        ge(dve, s["ob_out"], t)
                        nc.vector.tensor_scalar(uv_b[:], uv_a[:], 0.044715, 1.0, ALU.mult, ALU.add).then_inc(s["inner0"], 1)
                        dve.wait_ge(s["inner0"], t + 1)
                        nc.vector.tensor_tensor(uv_b[:], uv_b[:], ps_b[:], ALU.mult).then_inc(s["inner"], 1)
                        dve.wait_ge(s["g_exp"], t + 1)
                        nc.vector.tensor_scalar(uv_a[:], uv_a[:], 1.0, None, ALU.add).then_inc(s["g_exp1"], 1)
                        dve.wait_ge(s["g_exp1"], t + 1)
                        nc.vector.reciprocal(uv_a[:], uv_a[:]).then_inc(s["g_rec"], 1)
                        dve.wait_ge(s["g_rec"], t + 1)
                        nc.vector.tensor_tensor(uv_b[:], uv_a[:], ps_b[:], ALU.mult).then_inc(s["guv"], 1)
                        dve.wait_ge(s["guv"], t + 1)
                        nc.vector.bn_stats(bn6, uv_b[:, D_B:]).then_inc(s["bn_a"], 1)
                        dve.wait_ge(s["bn_a"], t + 1)
                        nc.vector.memset(stat[:, 40:41], 0.0)
                        nc.vector.bn_aggr(mv, bn6).then_inc(s["bn_b"], 1)
                        dve.wait_ge(s["bn_b"], t + 1)
                        ge(dve, s["rstd_v"], t)
                        nc.vector.tensor_scalar(vev, mv[:, 1:2], EPS, None, ALU.add).then_inc(s["var_eps"], 1)
                        dve.wait_ge(s["z_q"], t + 1)
                        ge(dve, s["rotk_sb"], t)
                        ge(dve, q_stored, 16 * t)
                        rotate(ps_c[:], qkv[:, 0, :], u, s["rotq_a"], s["rotq"])
                        dve.wait_ge(s["rstd_v"], t + 1)
                        ge(dve, s["sp_ps"], t)
                        nc.vector.tensor_scalar(vln[:], uv_b[:, D_B:], mv[:, 0:1], rsv, ALU.subtract, ALU.mult).then_inc(s["vn"], 1)
                        dve.wait_ge(s["vn"], t + 1)
                        nc.vector.tensor_tensor(vln[:], vln[:], ln_g[:], ALU.mult).then_inc(s["vn_g"], 1)
                        dve.wait_ge(s["vn_g"], t + 1)
                        nc.vector.tensor_tensor(vln[:], vln[:], ln_b[:], ALU.add).then_inc(s["vln_sb"], 1)
                        dve.wait_ge(s["sc_ps"], t + 1)
                        nc.vector.tensor_reduce(mx, ps_s[:], AX_X, ALU.max).then_inc(s["maxed"], 1)
                        dve.wait_ge(s["maxed"], t + 1)
                        ge(dve, s["p_sb"], t)
                        nc.vector.tensor_scalar(nmx, mx, -SCALE, None, ALU.mult).then_inc(s["nmx_sb"], 1)
                        if more:
                            lo_x(t + 1, 1 - u)
                        dve.wait_ge(s["z_k"], t + 1)
                        dve.wait_ge(s["rotq_sb"], t + 1)
                        ge(dve, kv_stored, 16 * t)
                        rotate(ps_a[:], qkv[:, 1, :], u, s["rotk_a"], s["rotk"])
                        dve.wait_ge(s["sp_ps"], t + 1)
                        for gi in range(GB):
                            c = slice(gi * GD, (gi + 1) * GD)
                            gated = nc.vector.scalar_tensor_tensor(
                                out=ob[:, c], in0=ps_o[:, D_C + gi * GD:D_C + (gi + 1) * GD], scalar=bs[:, gi:gi + 1],
                                in1=uv_b[:, c], op0=ALU.add, op1=ALU.mult)
                        gated.then_inc(s["ob_sb"], 1)
                        dve.wait_ge(s["pT_ps"], t + 1)
                        ge(dve, s["pv_ps"], t)
                        nc.vector.tensor_copy(probT[:, HC:, :], ps_x[:, HC:, :]).then_inc(s["pT_b"], 1)
                        dve.wait_ge(s["p_sb"], t + 1)
                        ge(dve, s["oc_sb"], t)
                        nc.vector.reciprocal(rden, den).then_inc(s["rden_sb"], 1)
                        dve.wait_ge(s["rden_sb"], t + 1)
                        dve.wait_ge(s["pv_ps"], t + 1)
                        ge(dve, s["oc_out"], t)
                        nc.vector.tensor_tensor(oc[:].rearrange("p (h c) -> p h c", h=HC),
                                                ps_o[:, 0:D_C].rearrange("p (h c) -> p h c", h=HC),
                                                rden.rearrange("p (h one) -> p h one", one=1).broadcast_to([P, HC, HD]),
                                                ALU.mult).then_inc(s["oc_sb"], 1)
                        dve.wait_ge(s["sq_b"], t + 1)
                        dve.wait_ge(s["sq_c"], t + 1)
                        ge(dve, s["rs_bc"], t)
                        nc.vector.tensor_scalar(msbc, stat[:, 32:34], 1.0 / D_B, EPS, ALU.mult, ALU.add).then_inc(s["ms_bc"], 1)

                def start():
                    mean_x(0)
                    lo_x(0, 0)
                loop(dve, body, start)

            @block.tensor
            def _(pe):
                pe.wait_ge(consts, 16 * 5)

                def turn(t, u):
                    pe.wait_ge(s["scaled_x"], t + 1)
                    ge(pe, s["pT_a"], t - 1)
                    ge(pe, s["pT_b"], t - 1)
                    for k in range(KC):
                        last = nc.tensor.transpose(ps_x[:, k, :], x[:, u, k * P:(k + 1) * P], ident[:])
                    last.then_inc(s["xT"], 1)

                def product(ps, u, col, width):
                    n = 0
                    for k in range(KC):
                        for a, b in ((hT_lo, w_hi), (hT_hi, w_lo), (hT_hi, w_hi)):
                            last = nc.tensor.matmul(ps[:, 0:width], a[:, u, k, :], b[:, k, col:col + width],
                                                    start=(n == 0), stop=(n == 3 * KC - 1))
                            n += 1
                    return last

                def body(i, seq, last):
                    for u in range(2):
                        t = 2 * i + u
                        pe.wait_ge(s["lo_sb"], t + 1)
                        ge(pe, s["rotk"], t)
                        product(ps_a, u, 3 * D_A + 2 * D_B, D_C).then_inc(s["z_qc"], 1)
                        ge(pe, s["v_sb"], t)
                        product(ps_b, u, 3 * D_A, 2 * D_B).then_inc(s["z_uv"], 1)
                        pe.wait_ge(s["qc_sb"], t + 1)
                        ge(pe, s["p_sb"], t)
                        for j in range(2):
                            x_ = nc.tensor.transpose(ps_s[:, 0, j * P:(j + 1) * P], qc[:, j * P:(j + 1) * P], ident[:])
                        x_.then_inc(s["qcT_ps"], 1)
                        ge(pe, s["rotq"], t)
                        product(ps_c, u, 0, D_A).then_inc(s["z_q"], 1)
                        pe.wait_ge(s["qcT_sb"], t + 1)
                        for h in range(HC):
                            lane = slice((h % 2) * HD, (h % 2 + 1) * HD)
                            x_ = nc.tensor.matmul(ps_s[:, bank_of(h), :], qcT[lane, h // 2, :], kmT[lane, seq, h // 2, :],
                                                  start=True, stop=True)
                        x_.then_inc(s["sc_ps"], 1)
                        if not (last and u):
                            turn(t + 1, 1 - u)
                        pe.wait_ge(s["qc_sb"], t + 1)
                        product(ps_a, u, D_A, D_A).then_inc(s["z_k"], 1)
                        pe.wait_ge(s["vln_sb"], t + 1)
                        ge(pe, s["ob_sb"], t)
                        for gi in range(GB):
                            x_ = nc.tensor.matmul(ps_o[:, D_C + gi * GD:D_C + (gi + 1) * GD], wsT[:, gi, :],
                                                  vln[:, gi * GD:(gi + 1) * GD], start=True, stop=True)
                        x_.then_inc(s["sp_ps"], 1)
                        pe.wait_ge(s["p_sb"], t + 1)
                        if not (last and u):
                            pe.wait_ge(s["lo_sb"], t + 2)
                        for h in range(HC):
                            for c in range(2):
                                x_ = nc.tensor.transpose(ps_x[:, 2 * h + c, :], prob[:, h, c * P:(c + 1) * P], ident[:])
                        x_.then_inc(s["pT_ps"], 1)
                        pe.wait_ge(s["guv"], t + 1)
                        product(ps_b, u, 2 * D_A, D_A).then_inc(s["z_v"], 1)
                        pe.wait_ge(s["pT_a"], t + 1)
                        pe.wait_ge(s["pT_b"], t + 1)
                        ge(pe, s["oc_sb"], t)
                        for h in range(HC):
                            for c in range(2):
                                x_ = nc.tensor.matmul(ps_o[:, h * HD:(h + 1) * HD], probT[:, 2 * h + c, :],
                                                      vm[:, seq, c, h * HD:(h + 1) * HD], start=(c == 0), stop=(c == 1))
                        x_.then_inc(s["pv_ps"], 1)
                loop(pe, body, lambda: turn(0, 0))


class Pattern:

    def __init__(self, seq, which, dil, before):
        self.seq, self.which, self.dil, self.before = seq, which, dil, before
        self.whole = dil == 16
        sub = SEQS[seq] // dil
        self.per = max(1, P // sub)
        self.blocks = SEQS[seq] // P
        self.chunks = 1 if self.whole else 2
        n = self.blocks // 2
        if self.whole:
            m = 3 + seq
            self.first, self.middle, self.last = (m, m), [(1, n - 1, (m, m))], (m, m)
        elif dil == 1:
            self.first, self.middle, self.last = (0, 1), [(1, n - 1, (1, 1))], (1, 2)
        else:
            self.first, self.last = (0, 0), (2, 2)
            self.middle = [(1, 2, (0, 0)), (2, n - 2, (1, 1)), (n - 2, n - 1, (2, 2))]

    def run(self, eng, body, masks=False):
        n = self.blocks // 2
        body(0, self.first, True, False)
        for lo, hi, m in self.middle if masks else [(1, n - 1, None)]:
            if hi - lo == 1:
                body(lo, m, False, False)
            elif hi > lo:
                with eng.Fori(lo, hi) as i:
                    body(i, m, False, False)
        body(n - 1, self.last, False, True)

    def place(self, i, u):
        if self.dil == 1:
            return (2 * i + u) * P, 0
        if self.whole:
            return 0, (2 * i + u) * self.per
        return i // 2 * P, i % 2 * 2 + u

    def rows(self, dram, i, u, j):
        base = self.seq * SEQS[0]
        v = dram[base:base + SEQS[self.seq], :].rearrange("(n d) c -> n d c", d=self.dil)
        n, r = self.place(i, u)
        return v[bass.ds(n, P // self.per), bass.ds(r + j, 1), :].rearrange("n d c -> n (d c)")

    def keys(self, dram, i, u, j, cols):
        base = KV_BASE[self.seq] - PAD
        v = dram[base:base + SEQS[self.seq] + 2 * PAD, cols].rearrange("(n d) c -> n d c", d=self.dil)
        n, r = self.place(i, u)
        if self.whole:
            return v[PAD // self.dil:PAD // self.dil + P // self.per, bass.ds(r + j, 1), :]
        v = v[bass.ds(n + PAD // self.dil - 64, 2 * P), bass.ds(r, 1), :]
        return v.rearrange("(c p) d e -> p c (d e)", p=P)


def attend_phase(nc, A):
    G = HA // 2
    with Phase(nc, "att") as ph:
        ident = ph.sb("ident", [P, P])
        masks = ph.sb("masks", [P, 5, 2 * P])
        qin = ph.sb("qin", [P, 2, D_A])
        kin = ph.sb("kin", [P, 2, 2, D_A])
        vin = ph.sb("vin", [P, 2, 2, D_A])
        qT = ph.sb("qT", [P, 2, 4, P])
        kT = ph.sb("kT", [P, 2, 4, 2 * P])
        score = ph.sb("score", [P, 2, G, 2 * P])
        prob = ph.sb("prob", [P, 2, G, 2 * P])
        probT = ph.sb("probT", [P, 2, 2 * G, P])
        o = ph.sb("o", [P, 2, O_COLS])
        nmx = ph.sb("nmx", [P, HA])
        spare = ph.sb("spare", [P, 1])
        ps_s = [ph.psum(f"ps_s{g}", [P, G, 2 * P]) for g in range(2)]
        ps_p = ph.psum("ps_p", [P, 2 * G, P])
        ps_o = ph.psum("ps_o", [P, D_A])
        ps_t = ph.psum("ps_t", [P, 4, P])
        consts = ph.sem("consts")
        qk_loaded = [ph.sem(f"qk_loaded{u}") for u in range(2)]
        v_loaded = [ph.sem(f"v_loaded{u}") for u in range(2)]
        o_stored = [ph.sem(f"o_stored{u}") for u in range(2)]
        turned, turned_sb = ph.sem("turned"), ph.sem("turned_sb")
        scored = [ph.sem(f"scored{g}") for g in range(2)]
        masked = [ph.sem(f"masked{g}") for g in range(2)]
        nmx_sb = [ph.sem(f"nmx_sb{g}") for g in range(2)]
        p_sb = [ph.sem(f"p_sb{g}") for g in range(2)]
        pT_ps = [ph.sem(f"pT_ps{g}") for g in range(2)]
        pT_sb = [ph.sem(f"pT_sb{g}") for g in range(2)]
        pv_ps = [ph.sem(f"pv_ps{g}") for g in range(2)]
        o_sb = ph.sem("o_sb")

        patterns = []
        for seq in range(2):
            for which, dil in enumerate((1, 4, 16)):
                patterns.append(Pattern(seq, which, dil, sum(q.blocks for q in patterns)))

        with nc.Block() as block:
            @block.sync
            def _(sp):
                sp.dma_start(ident[:], A["ident"]).then_inc(consts, 16)
                sp.dma_start(masks[:], A["masks"]).then_inc(consts, 16)
                for pt in patterns:
                    part = P // pt.per

                    def load_qk(i, u):
                        c = pt.before + 2 * i + u
                        ge(sp, turned, 3 * (c - 1))
                        for j in range(pt.per):
                            at = slice(j * part, (j + 1) * part)
                            sp.dma_start(qin[at, u, :], pt.rows(A["q"], i, u, j)).then_inc(qk_loaded[u], 32 // pt.per)
                            sp.dma_start(kin[at, u, 0:pt.chunks, :], pt.keys(A["kv"], i, u, j, slice(0, D_A)))\
                                .then_inc(qk_loaded[u], 32 // pt.per)

                    def load_v(i, u):
                        c = pt.before + 2 * i + u
                        ge(sp, pv_ps[1], c - 1)
                        for j in range(pt.per):
                            at = slice(j * part, (j + 1) * part)
                            sp.dma_start(vin[at, u, 0:pt.chunks, :], pt.keys(A["kv"], i, u, j, slice(D_A, 2 * D_A)))\
                                .then_inc(v_loaded[u], 32 // pt.per)

                    def store(i, u):
                        sp.wait_ge(o_sb, pt.before + 2 * i + u + 1)
                        sp.wait_ge(p_sb[1], pt.before + 2 * i + u + 1)
                        for j in range(pt.per):
                            at = slice(j * part, (j + 1) * part)
                            sp.dma_start(pt.rows(A[f"o{pt.which}"], i, u, j), o[at, u, :])\
                                .then_inc(o_stored[u], 32 // pt.per)

                    def body(i, m, first, last):
                        for u in range(2):
                            if not last:
                                load_qk(i + 1, u)
                            if not (first and u == 0):
                                store(i - 1 + u, 1 - u)
                            if not (last and u):
                                load_v(i + u, 1 - u)
                    load_qk(0, 0)
                    load_qk(0, 1)
                    load_v(0, 0)
                    pt.run(sp, body)
                    store(pt.blocks // 2 - 1, 1)
                for u in range(2):
                    sp.wait_ge(o_stored[u], 32 * sum(pt.blocks // 2 for pt in patterns))

            @block.tensor
            def _(pe):
                pe.wait_ge(consts, 32)
                for pt in patterns:
                    W = pt.chunks * P

                    def turn(i, u, r):
                        c = pt.before + 2 * i + u
                        if r == 0:
                            pe.wait_ge(qk_loaded[u], 64 * (pt.before // 2 + i + 1))
                        if r <= pt.chunks:
                            ge(pe, turned_sb, 3 * c + r)
                            for j in range(4):
                                src = qin[:, u, j * P:(j + 1) * P] if r == 0 else kin[:, u, r - 1, j * P:(j + 1) * P]
                                x_ = nc.tensor.transpose(ps_t[:, j, :], src, ident[:])
                            x_.then_inc(turned, 1 if r < pt.chunks else 3 - pt.chunks)

                    def scores(c, u, g):
                        if g == 0:
                            pe.wait_ge(turned_sb, 3 * c + 3)
                        ge(pe, masked[g], c)
                        for h in range(g * G, (g + 1) * G):
                            lane = slice(h % 2 * HD, h % 2 * HD + HD)
                            x_ = nc.tensor.matmul(ps_s[g][:, bank_of(h % G), 0:W], qT[lane, u, h // 2, :],
                                                  kT[lane, u, h // 2, 0:W], start=True, stop=True)
                        x_.then_inc(scored[g], 1)

                    def turn_p(c, g):
                        pe.wait_ge(p_sb[g], c + 1)
                        if g:
                            pe.wait_ge(pT_sb[0], c + 1)
                        else:
                            ge(pe, pT_sb[1], c)
                        for h in range(G):
                            for k in range(pt.chunks):
                                x_ = nc.tensor.transpose(ps_p[:, pt.chunks * h + k, :], prob[:, g, h, k * P:(k + 1) * P], ident[:])
                        x_.then_inc(pT_ps[g], 1)

                    def values(c, i, u, g):
                        pe.wait_ge(pT_sb[g], c + 1)
                        if g == 0:
                            pe.wait_ge(v_loaded[u], 32 * (pt.before // 2 + i + 1))
                            ge(pe, o_sb, c)
                        for h in range(G):
                            for k in range(pt.chunks):
                                col = (g * G + h) * HD
                                x_ = nc.tensor.matmul(ps_o[:, col:col + HD], probT[:, g, pt.chunks * h + k, :],
                                                      vin[:, u, k, col:col + HD], start=(k == 0), stop=(k == pt.chunks - 1))
                        x_.then_inc(pv_ps[g], 1)

                    def body(i, m, first, last):
                        for u in range(2):
                            c = pt.before + 2 * i + u
                            more = not (last and u)
                            scores(c, u, 0)
                            if not (first and u == 0):
                                turn_p(c - 1, 1)
                            if more:
                                turn(i + u, 1 - u, 0)
                            if not (first and u == 0):
                                values(c - 1, i - 1 + u, 1 - u, 1)
                            scores(c, u, 1)
                            if more:
                                turn(i + u, 1 - u, 1)
                            turn_p(c, 0)
                            if more:
                                turn(i + u, 1 - u, 2)
                            values(c, i, u, 0)
                    for r in range(3):
                        turn(0, 0, r)
                    pt.run(pe, body)
                    n = pt.blocks // 2 - 1
                    turn_p(pt.before + 2 * n + 1, 1)
                    values(pt.before + 2 * n + 1, n, 1, 1)

            @block.scalar
            def _(act):
                for pt in patterns:
                    W = pt.chunks * P

                    def out(i, u, r):
                        c = pt.before + 2 * i + u
                        if r <= pt.chunks:
                            act.wait_ge(turned, 3 * c + r + 1)
                            if r == 0:
                                ge(act, scored[1], c - 1)
                            dst = qT[:, u, :, :] if r == 0 else kT[:, u, :, (r - 1) * P:r * P]
                            nc.scalar.activation(dst, ps_t[:], ACT.Copy).then_inc(turned_sb, 1 if r < pt.chunks else 3 - pt.chunks)

                    def exps(c, u, g, slot_uses):
                        act.wait_ge(nmx_sb[g], c + 1)
                        ge(act, pT_ps[g], c)
                        if g == 0:
                            ge(act, o_stored[u], 32 * slot_uses)
                        for h in range(G):
                            n = g * G + h
                            x_ = nc.scalar.activation(prob[:, g, h, 0:W], score[:, g, h, 0:W], ACT.Exp, bias=nmx[:, n:n + 1],
                                                      scale=SCALE, accum_out=o[:, u, D_A + HA + n:D_A + HA + n + 1])
                        x_.then_inc(p_sb[g], 1)

                    def body(i, m, first, last):
                        for u in range(2):
                            c = pt.before + 2 * i + u
                            more = not (last and u)
                            if more:
                                out(i + u, 1 - u, 0)
                            exps(c, u, 0, pt.before // 2 + i)
                            if more:
                                out(i + u, 1 - u, 1)
                                out(i + u, 1 - u, 2)
                            exps(c, u, 1, pt.before // 2 + i)
                    for r in range(3):
                        out(0, 0, r)
                    pt.run(act, body)

            @block.vector
            def _(dve):
                dve.wait_ge(consts, 32)
                for pt in patterns:
                    W = pt.chunks * P

                    def mask(c, u, g, m, slot_uses):
                        dve.wait_ge(scored[g], c + 1)
                        ge(dve, p_sb[g], c)
                        if g == 0:
                            ge(dve, o_stored[u], 32 * slot_uses)
                        nc.vector.memset(spare[:], 0.0)
                        for h in range(G):
                            n = g * G + h
                            x_ = nc.vector.tensor_tensor_reduce(
                                out=score[:, g, h, 0:W], in0=ps_s[g][:, bank_of(h), 0:W], in1=masks[:, m, 0:W], scale=1.0,
                                scalar=-3e38, op0=ALU.add, op1=ALU.max, accum_out=o[:, u, D_A + n:D_A + n + 1])
                        x_.then_inc(masked[g], 1)
                        dve.wait_ge(masked[g], c + 1)
                        nc.vector.tensor_scalar(nmx[:, g * G:(g + 1) * G], o[:, u, D_A + g * G:D_A + (g + 1) * G], -SCALE, None,
                                                ALU.mult).then_inc(nmx_sb[g], 1)

                    def out_p(c, g):
                        dve.wait_ge(pT_ps[g], c + 1)
                        ge(dve, pv_ps[g], c)
                        nc.vector.tensor_copy(probT[:, g, 0:pt.chunks * G, :], ps_p[:, 0:pt.chunks * G, :]).then_inc(pT_sb[g], 1)

                    def out_o(c, u):
                        dve.wait_ge(pv_ps[1], c + 1)
                        nc.vector.tensor_copy(o[:, u, 0:D_A], ps_o[:]).then_inc(o_sb, 1)

                    def body(i, m, first, last):
                        for u in range(2):
                            c = pt.before + 2 * i + u
                            uses = pt.before // 2 + i
                            mask(c, u, 0, m[u], uses)
                            if not (first and u == 0):
                                out_p(c - 1, 1)
                                out_o(c - 1, 1 - u)
                            mask(c, u, 1, m[u], uses)
                            out_p(c, 0)
                    pt.run(dve, body, masks=True)
                    out_p(pt.before + pt.blocks - 1, 1)
                    out_o(pt.before + pt.blocks - 1, 1)


def mix_phase(nc, A, affinity):
    with Phase(nc, "mix") as ph:
        ident = ph.sb("ident", [P, P])
        w_hi = ph.sb("w_hi", [P, KC, D], F32R)
        w_lo = ph.sb("w_lo", [P, KC, D], F32R)
        w_r = ph.sb("w_r", [P, KC, NE])
        g = ph.sb("g", [P, KC])
        g_ffn = ph.sb("g_ffn", [P, D])
        consts, g_loaded = ph.sem("consts"), ph.sem("g_loaded")
        with nc.Block() as block:
            @block.sync
            def _(sp):
                sp.dma_start(g[:], A["g_out"]).then_inc(g_loaded, 16)
                sp.dma_start(ident[:], A["ident"]).then_inc(consts, 16)
                sp.dma_start(g_ffn[:], A["g_ffn"]).then_inc(consts, 16)
                sp.dma_start(w_r[:], A["w_router"].rearrange("(k p) e -> p k e", p=P)).then_inc(consts, 16)
                sp.wait_ge(consts, 48)
                sp.wait_ge(g_loaded, 16)
        split_weights(nc, ph, A["w_out"], g, g_loaded, w_hi, w_lo, D)

        o3 = ph.sb("o3", [P, 2, 3, O_COLS])
        obc = ph.sb("obc", [P, 2, D_B + D_C])
        oa = ph.sb("oa", [P, 2, D_A])
        cT_hi = ph.sb("cT_hi", [P, 2, KC, P], F32R)
        cT_lo = ph.sb("cT_lo", [P, 2, KC, P], F32R)
        x = ph.sb("x", [P, 2, D])
        xn = ph.sb("xn", [P, 2, XN_COLS])
        xnT = ph.sb("xnT", [P, KC, P])
        junk = ph.sb("junk", [P, D], BF16)
        stat = ph.sb("stat", [P, 160])
        half = ph.sb("half", [P, 1])
        top, wts, wden = stat[:, 0:8], stat[:, 8:32], stat[:, 32:56]
        tot, rtot, wfin = stat[:, 56:64], stat[:, 64:72], stat[:, 72:96]
        ss_a, ms_a, rs_a = stat[:, 96:97], stat[:, 97:98], stat[:, 98:99]
        ss_y, ms_y, rs_y = stat[:, 100:101], stat[:, 101:102], stat[:, 102:103]
        rmax, rneg, rden, rrec, rexp = stat[:, 104:105], stat[:, 105:106], stat[:, 106:107], stat[:, 107:108], stat[:, 112:128]
        ps_c = ph.psum("ps_c", [P, KC, P])
        ps_y = ph.psum("ps_y", [P, 2, 512])
        ps_n = ph.psum("ps_n", [P, KC, P])
        ps_r = ph.psum("ps_r", [P, 512])
        names = """topped shifted weighted wden_sb tot_sb rtot_sb wfin_sb scaled3 added_a added_b sq_a ms_a rs_a
            oa_out cT_ps hi_sb lo_sb y_a y_b x1_a x1_b sq_y ms_y rs_y xn_sb nT_ps nT_sb r_ps rmax_sb rneg_sb
            rexp_sb rrec_sb aff_a aff_b half_set""".split()
        s = {n: ph.sem(n) for n in names}
        o_loaded = [ph.sem(f"o_loaded{u}") for u in range(2)]
        x_loaded = [ph.sem(f"x_loaded{u}") for u in range(2)]
        y_stored = [ph.sem(f"y_stored{u}") for u in range(2)]
        xn_stored = [ph.sem(f"xn_stored{u}") for u in range(2)]

        def loop(eng, body):
            body(0, True, False)
            with eng.Fori(1, PAIRS - 1) as i:
                body(i, False, False)
            body(PAIRS - 1, False, True)

        with nc.Block() as block:
            @block.sync
            def _(sp):
                def load_o(t, u):
                    ge(sp, s["added_b"], t - 1)
                    ge(sp, s["cT_ps"], t - 1)
                    for j in range(3):
                        sp.dma_start(o3[:, u, j, :], A[f"o{j}"][bass.ds(t * P, P), :]).then_inc(o_loaded[u], 16)
                    sp.dma_start(obc[:, u, :], A["obc"][bass.ds(t * P, P), :]).then_inc(o_loaded[u], 16)

                def load_x(t, u, n):
                    ge(sp, y_stored[u], 16 * n)
                    ge(sp, s["xn_sb"], t - 1)
                    sp.dma_start(x[:, u, :], A["x"][bass.ds(t * P, P), :]).then_inc(x_loaded[u], 16)

                def store(t, u):
                    sp.wait_ge(s["x1_b"], t + 1)
                    sp.dma_start(A["y"][bass.ds(t * P, P), :], x[:, u, :]).then_inc(y_stored[u], 16)
                    sp.wait_ge(s["aff_a"], t + 1)
                    sp.dma_start(A["xn"][bass.ds(t * P, P), :], xn[:, u, :]).then_inc(xn_stored[u], 16)

                def body(i, first, last):
                    for u in range(2):
                        t = 2 * i + u
                        if not last:
                            load_o(t + 2, u)
                        if not (first and u == 0):
                            store(t - 1, 1 - u)
                        if not (last and u):
                            load_x(t + 1, 1 - u, i + u)
                load_o(0, 0)
                load_o(1, 1)
                load_x(0, 0, 0)
                loop(sp, body)
                store(NT - 1, 1)
                for u in range(2):
                    sp.wait_ge(y_stored[u], 16 * PAIRS)
                    sp.wait_ge(xn_stored[u], 16 * PAIRS)

            @block.gpsimd
            def _(pool):
                nc.gpsimd.memset(half[:], -0.5).then_inc(s["half_set"], 1)
                pool.wait_ge(s["half_set"], 1)

                def join(t, u):
                    pool.wait_ge(s["scaled3"], t + 1)
                    ge(pool, s["oa_out"], t)
                    a, b, c = (o3[:, u, j, 0:D_A] for j in range(3))
                    nc.gpsimd.tensor_tensor(a, a, b, ALU.add).then_inc(s["added_a"], 1)
                    pool.wait_ge(s["added_a"], t + 1)
                    ge(pool, s["cT_ps"], t - 1)
                    nc.gpsimd.tensor_tensor(oa[:, u, :], a, c, ALU.add).then_inc(s["added_b"], 1)
                    pool.wait_ge(s["ms_a"], t + 1)
                    nc.gpsimd.tensor_tensor(rs_a, ms_a, half[:], ALU.pow).then_inc(s["rs_a"], 1)

                def norm(t):
                    pool.wait_ge(s["ms_y"], t + 1)
                    ge(pool, s["xn_sb"], t)
                    nc.gpsimd.tensor_tensor(rs_y, ms_y, half[:], ALU.pow).then_inc(s["rs_y"], 1)

                def body(i, first, last):
                    for u in range(2):
                        t = 2 * i + u
                        if not (first and u == 0):
                            norm(t - 1)
                        if not last:
                            join(t + 2, u)
                join(0, 0)
                join(1, 1)
                loop(pool, body)
                norm(NT - 1)

            @block.scalar
            def _(act):
                act.wait_ge(consts, 48)

                def join(t, u):
                    act.wait_ge(s["shifted"], t + 1)
                    nc.scalar.activation(wts, wts, ACT.Exp, scale=SCALE).then_inc(s["weighted"], 1)
                    act.wait_ge(s["added_b"], t + 1)
                    ge(act, s["ms_a"], t)
                    nc.scalar.activation(junk[:, 0:D_A], oa[:, u, :], ACT.Square, accum_out=ss_a).then_inc(s["sq_a"], 1)
                    act.wait_ge(s["rs_a"], t + 1)
                    nc.scalar.activation(oa[:, u, :], oa[:, u, :], ACT.Copy, scale=rs_a).then_inc(s["oa_out"], 1)

                def hi(t, u):
                    act.wait_ge(s["cT_ps"], t + 1)
                    ge(act, s["y_b"], t - 1)
                    nc.scalar.activation(cT_hi[:, u, :, :], ps_c[:], ACT.Copy).then_inc(s["hi_sb"], 1)

                def square(t, u):
                    act.wait_ge(s["x1_b"], t + 1)
                    ge(act, s["ms_y"], t)
                    nc.scalar.activation(junk[:], x[:, u, :], ACT.Square, accum_out=ss_y).then_inc(s["sq_y"], 1)

                def out_n(t):
                    act.wait_ge(s["nT_ps"], t + 1)
                    ge(act, s["r_ps"], t)
                    nc.scalar.activation(xnT[:], ps_n[:], ACT.Copy).then_inc(s["nT_sb"], 1)

                def softmax(t):
                    act.wait_ge(s["rneg_sb"], t + 1)
                    ge(act, s["aff_b"], t)
                    nc.scalar.activation(rexp, ps_r[:, 0:NE], ACT.Exp, bias=rneg, accum_out=rden).then_inc(s["rexp_sb"], 1)

                def body(i, first, last):
                    for u in range(2):
                        t = 2 * i + u
                        past = not (first and u == 0)
                        if past:
                            square(t - 1, 1 - u)
                            out_n(t - 1)
                        if not (last and u):
                            hi(t + 1, 1 - u)
                        if not last:
                            join(t + 2, u)
                        if past:
                            softmax(t - 1)
                join(0, 0)
                hi(0, 0)
                join(1, 1)
                loop(act, body)
                square(NT - 1, 1)
                out_n(NT - 1)
                softmax(NT - 1)

            @block.vector
            def _(dve):
                dve.wait_ge(consts, 48)

                def heads(ap):
                    return ap.rearrange("p (j h) -> p j h", j=3)

                def over(ap):
                    return ap.rearrange("p (one h) -> p one h", one=1).broadcast_to([P, 3, HA])

                def join(t, u, n):
                    dve.wait_ge(o_loaded[u], 64 * n)
                    mj = o3[:, u, :, D_A:D_A + HA]
                    nc.vector.tensor_reduce(top, mj.rearrange("p j h -> p h j"), AX_X, ALU.max).then_inc(s["topped"], 1)
                    dve.wait_ge(s["topped"], t + 1)
                    ge(dve, s["wfin_sb"], t)
                    nc.vector.tensor_tensor(heads(wts), mj, over(top), ALU.subtract).then_inc(s["shifted"], 1)
                    dve.wait_ge(s["weighted"], t + 1)
                    nc.vector.tensor_tensor(heads(wden), heads(wts), o3[:, u, :, D_A + HA:], ALU.mult).then_inc(s["wden_sb"], 1)
                    dve.wait_ge(s["wden_sb"], t + 1)
                    nc.vector.tensor_reduce(tot, wden.rearrange("p (j h) -> p h j", j=3), AX_X, ALU.add).then_inc(s["tot_sb"], 1)
                    dve.wait_ge(s["tot_sb"], t + 1)
                    nc.vector.reciprocal(rtot, tot).then_inc(s["rtot_sb"], 1)
                    dve.wait_ge(s["rtot_sb"], t + 1)
                    nc.vector.tensor_tensor(heads(wfin), heads(wts), over(rtot), ALU.mult).then_inc(s["wfin_sb"], 1)
                    dve.wait_ge(s["wfin_sb"], t + 1)
                    for j in range(3):
                        v = o3[:, u, j, 0:D_A].rearrange("p (h c) -> p h c", h=HA)
                        by = wfin[:, j * HA:(j + 1) * HA].rearrange("p (h one) -> p h one", one=1).broadcast_to([P, HA, HD])
                        x_ = nc.vector.tensor_tensor(v, v, by, ALU.mult)
                    x_.then_inc(s["scaled3"], 1)
                    dve.wait_ge(s["sq_a"], t + 1)
                    ge(dve, s["oa_out"], t)
                    nc.vector.tensor_scalar(ms_a, ss_a, 1.0 / D_A, EPS, ALU.mult, ALU.add).then_inc(s["ms_a"], 1)

                def lo(t, u):
                    dve.wait_ge(s["hi_sb"], t + 1)
                    nc.vector.tensor_tensor(cT_lo[:, u, :, :], ps_c[:], cT_hi[:, u, :, :].bitcast(F32), ALU.subtract)\
                        .then_inc(s["lo_sb"], 1)

                def add_x(t, u, j, n):
                    if j == 0:
                        dve.wait_ge(x_loaded[u], 16 * n)
                    c = slice(j * 512, (j + 1) * 512)
                    dve.wait_ge(s["y_b" if j else "y_a"], t + 1)
                    nc.vector.tensor_tensor(x[:, u, c], x[:, u, c], ps_y[:, j, :], ALU.add).then_inc(s["x1_b" if j else "x1_a"], 1)

                def norm(t, u, n):
                    dve.wait_ge(s["sq_y"], t + 1)
                    ge(dve, s["rs_y"], t)
                    nc.vector.tensor_scalar(ms_y, ss_y, 1.0 / D, EPS, ALU.mult, ALU.add).then_inc(s["ms_y"], 1)
                    dve.wait_ge(s["rs_y"], t + 1)
                    ge(dve, xn_stored[u], 16 * n)
                    ge(dve, s["nT_ps"], t - 1)
                    nc.vector.scalar_tensor_tensor(out=xn[:, u, 0:D], in0=x[:, u, :], scalar=rs_y, in1=g_ffn[:],
                                                   op0=ALU.mult, op1=ALU.mult).then_inc(s["xn_sb"], 1)

                def softmax(t, u):
                    dve.wait_ge(s["r_ps"], t + 1)
                    nc.vector.tensor_reduce(rmax, ps_r[:, 0:NE], AX_X, ALU.max).then_inc(s["rmax_sb"], 1)
                    dve.wait_ge(s["rmax_sb"], t + 1)
                    ge(dve, s["rexp_sb"], t)
                    nc.vector.tensor_scalar(rneg, rmax, -1.0, None, ALU.mult).then_inc(s["rneg_sb"], 1)
                    dve.wait_ge(s["rexp_sb"], t + 1)
                    nc.vector.reciprocal(rrec, rden).then_inc(s["rrec_sb"], 1)
                    dve.wait_ge(s["rrec_sb"], t + 1)
                    nc.vector.tensor_scalar(xn[:, u, D:], rexp, rrec, None, ALU.mult).then_inc(s["aff_a"], 1)
                    nc.vector.tensor_scalar(affinity[:, bass.ds(t * NE, NE)], rexp, rrec, None, ALU.mult).then_inc(s["aff_b"], 1)

                def body(i, first, last):
                    for u in range(2):
                        t = 2 * i + u
                        past = not (first and u == 0)
                        if past:
                            add_x(t - 1, 1 - u, 1, None)
                            norm(t - 1, 1 - u, i - 1 + u)
                        add_x(t, u, 0, i + 1)
                        if not (last and u):
                            lo(t + 1, 1 - u)
                        if not last:
                            join(t + 2, u, i + 2)
                        if past:
                            softmax(t - 1, 1 - u)
                join(0, 0, 1)
                lo(0, 0)
                join(1, 1, 1)
                loop(dve, body)
                add_x(NT - 1, 1, 1, None)
                norm(NT - 1, 1, PAIRS - 1)
                softmax(NT - 1, 1)

            @block.tensor
            def _(pe):
                pe.wait_ge(consts, 48)

                def turn(t, u):
                    pe.wait_ge(s["oa_out"], t + 1)
                    ge(pe, s["lo_sb"], t)
                    for k in range(KC):
                        src = oa[:, u, k * P:(k + 1) * P] if k < 4 else obc[:, u, (k - 4) * P:(k - 3) * P]
                        x_ = nc.tensor.transpose(ps_c[:, k, :], src, ident[:])
                    x_.then_inc(s["cT_ps"], 1)

                def turn_n(t, u):
                    pe.wait_ge(s["xn_sb"], t + 1)
                    ge(pe, s["nT_sb"], t)
                    for k in range(KC):
                        x_ = nc.tensor.transpose(ps_n[:, k, :], xn[:, u, k * P:(k + 1) * P], ident[:])
                    x_.then_inc(s["nT_ps"], 1)

                def product(t, u, j):
                    ge(pe, s["x1_b" if j else "x1_a"], t)
                    n = 0
                    for k in range(KC):
                        for a, b in ((cT_lo, w_hi), (cT_hi, w_lo), (cT_hi, w_hi)):
                            x_ = nc.tensor.matmul(ps_y[:, j, :], a[:, u, k, :], b[:, k, j * 512:(j + 1) * 512],
                                                  start=(n == 0), stop=(n == 3 * KC - 1))
                            n += 1
                    x_.then_inc(s["y_b" if j else "y_a"], 1)

                def route(t):
                    pe.wait_ge(s["nT_sb"], t + 1)
                    ge(pe, s["rexp_sb"], t)
                    for k in range(KC):
                        x_ = nc.tensor.matmul(ps_r[:, 0:NE], xnT[:, k, :], w_r[:, k, :], start=(k == 0), stop=(k == KC - 1))
                    x_.then_inc(s["r_ps"], 1)

                def body(i, first, last):
                    for u in range(2):
                        t = 2 * i + u
                        past = not (first and u == 0)
                        pe.wait_ge(s["lo_sb"], t + 1)
                        product(t, u, 0)
                        if past:
                            turn_n(t - 1, 1 - u)
                        if not (last and u):
                            turn(t + 1, 1 - u)
                        product(t, u, 1)
                        if past:
                            route(t - 1)
                turn(0, 0)
                loop(pe, body)
                turn_n(NT - 1, 1)
                route(NT - 1)


def choose_phase(nc, A, affinity, slots):
    with Phase(nc, "top") as ph:
        load = ph.sb("load", [P, P + 2 * NT + CAPS[0]])
        bits = ph.sb("bits", [P, BITS], I32)
        ones = ph.sb("ones", [P, P], BF16)
        tri = ph.sb("tri", [P, P], BF16)
        ids = ph.sb("ids", [P, 2 * NT], BF16)
        slot_row = ph.sb("slot_row", [P, CAPS[0]], BF16)
        caps = ph.sb("caps", [P, 2, NE])
        thr = ph.sb("thr", [P, 2, NE], I32)
        cand = ph.sb("cand", [P, 2, NE], I32)
        kept = ph.sb("kept", [P, 2, NE], I32)
        hits = ph.sb("hits", [P, NT, NE], BF16)
        ties = ph.sb("ties", [P, NT, NE], BF16)
        chosen = ph.sb("chosen", [P, NT, NE], BF16)
        need = ph.sb("need", [P, 2, NE])
        before = ph.sb("before", [P, NT, NE])
        rank = ph.sb("rank", [P, NT, NE])
        slot = ph.sb("slot", [P, NT * NE])
        R = 8
        onehot = ph.sb("onehot", [P, R, CAPS[0]], BF16)
        ps_n = ph.psum("ps_n", [P, 2, 256])
        ps_w = ph.psum("ps_w", [P, 512])
        ps_s = ph.psum("ps_s", [P, 512])
        ps_i = [ph.psum(f"ps_i{j}", [P, 512]) for j in range(ST)]
        names = """loaded made cand_set hit counted kept_set thr_set gt eq n_gt pre_ps need_sb run rank_sb ok tied sel
            sel_ps slot_sb oh_set oh_used lists""".split()
        s = {n: ph.sem(n) for n in names}
        MADE = 8
        tiles = (slice(0, NTP), slice(NTP, NT))

        def per_tile(ap, seq):
            n = tiles[seq].stop - tiles[seq].start
            return ap[:, seq:seq + 1, :].broadcast_to([P, n, NE])

        with nc.Block() as block:
            @block.sync
            def _(sp):
                sp.dma_start(load[:, 0:P], A["tri"]).then_inc(s["loaded"], 16)
                sp.dma_start(load[:, P:P + 2 * NT], A["ids"]).then_inc(s["loaded"], 16)
                sp.dma_start(load[:, P + 2 * NT:], A["slot_row"]).then_inc(s["loaded"], 16)
                sp.dma_start(bits[:].bitcast(F32), A["bits"]).then_inc(s["loaded"], 16)

            @block.tensor
            def _(pe):
                pe.wait_ge(s["made"], MADE)

                def count(what):
                    for seq in range(2):
                        t0, t1 = tiles[seq].start, tiles[seq].stop
                        for t in range(t0, t1):
                            x_ = nc.tensor.matmul(ps_n[:, seq, 0:NE], ones[:], what[:, t, :], start=(t == t0), stop=(t == t1 - 1))
                    return x_

                def prefix(what, done):
                    nc.tensor.matmul(ps_w[:, 0:NT * NE], tri[:], what[:].rearrange("p t e -> p (t e)"), start=True, stop=True)
                    nc.tensor.matmul(ps_s[:, 0:NT * NE], ones[:], what[:].rearrange("p t e -> p (t e)"), start=True, stop=True)\
                        .then_inc(done, 1)
                with pe.Fori(0, BITS) as b:
                    pe.wait_ge(s["hit"], b + 1)
                    count(hits).then_inc(s["counted"], 1)
                pe.wait_ge(s["gt"], 1)
                count(hits).then_inc(s["n_gt"], 1)
                pe.wait_ge(s["eq"], 1)
                prefix(ties, s["pre_ps"])
                pe.wait_ge(s["sel"], 1)
                prefix(chosen, s["sel_ps"])
                with pe.Fori(0, NE) as e:
                    for t in range(NT):
                        seq = int(t >= NTP)
                        pe.wait_ge(s["oh_set"], e * NT + t + 1)
                        for j in range(CAPS[seq] // P):
                            x_ = nc.tensor.matmul(ps_i[2 * seq + j][:, bass.ds(2 * e, 2)], onehot[:, t % R, j * P:(j + 1) * P],
                                                  ids[:, 2 * t:2 * t + 2], start=(t in (0, NTP)), stop=(t in (NTP - 1, NT - 1)))
                        x_.then_inc(s["oh_used"], 1)

            @block.vector
            def _(dve):
                nc.vector.memset(ones[:], 1.0).then_inc(s["made"], 1)
                nc.vector.memset(thr[:], 0).then_inc(s["made"], 1)
                for seq in range(2):
                    nc.vector.memset(caps[:, seq, :], float(CAPS[seq])).then_inc(s["made"], 1)
                    nc.vector.memset(before[:, tiles[seq].start, :], 0.0).then_inc(s["made"], 1)
                dve.wait_ge(s["loaded"], 64)
                nc.vector.tensor_copy(tri[:], load[:, 0:P])
                nc.vector.tensor_copy(ids[:], load[:, P:P + 2 * NT]).then_inc(s["made"], 1)
                nc.vector.tensor_copy(slot_row[:], load[:, P + 2 * NT:]).then_inc(s["made"], 1)
                dve.wait_ge(s["made"], MADE)
                aff = affinity[:].rearrange("p (t e) -> p t e", e=NE)

                def compare(out, op, level):
                    for seq in range(2):
                        x_ = nc.vector.tensor_tensor(out[:, tiles[seq], :], aff[:, tiles[seq], :], per_tile(level, seq), op)
                    return x_

                with dve.Fori(0, BITS) as b:
                    ge(dve, s["thr_set"], b)
                    nc.vector.tensor_tensor(cand[:].rearrange("p s e -> p (s e)"), thr[:].rearrange("p s e -> p (s e)"),
                                            bits[:, bass.ds(b, 1)].broadcast_to([P, 2 * NE]), ALU.bitwise_or).then_inc(s["cand_set"], 1)
                    dve.wait_ge(s["cand_set"], b + 1)
                    ge(dve, s["counted"], b)
                    compare(hits, ALU.is_ge, cand[:].bitcast(F32)).then_inc(s["hit"], 1)
                    dve.wait_ge(s["counted"], b + 1)
                    nc.vector.tensor_tensor(kept[:], ps_n[:, :, 0:NE], caps[:], ALU.is_ge).then_inc(s["kept_set"], 1)
                    dve.wait_ge(s["kept_set"], b + 1)
                    nc.vector.memset(slot[:, 0:1], 0.0)
                    nc.vector.copy_predicated(thr[:], kept[:], cand[:]).then_inc(s["thr_set"], 1)

                dve.wait_ge(s["thr_set"], BITS)
                compare(hits, ALU.is_gt, thr[:].bitcast(F32)).then_inc(s["gt"], 1)
                compare(ties, ALU.is_equal, thr[:].bitcast(F32)).then_inc(s["eq"], 1)
                dve.wait_ge(s["n_gt"], 1)
                nc.vector.tensor_tensor(need[:], caps[:], ps_n[:, :, 0:NE], ALU.subtract).then_inc(s["need_sb"], 1)
                runs = [0]

                def ranks(done):
                    dve.wait_ge(done, 1)
                    for t in range(1, NT):
                        if t == NTP:
                            continue
                        if runs[0]:
                            dve.wait_ge(s["run"], runs[0])
                        nc.vector.tensor_tensor(before[:, t, :], before[:, t - 1, :], ps_s[:, (t - 1) * NE:t * NE], ALU.add)\
                            .then_inc(s["run"], 1)
                        runs[0] += 1
                    dve.wait_ge(s["run"], runs[0])
                    nc.vector.tensor_tensor(rank[:].rearrange("p t e -> p (t e)"), before[:].rearrange("p t e -> p (t e)"),
                                            ps_w[:, 0:NT * NE], ALU.add).then_inc(s["rank_sb"], 1)

                ranks(s["pre_ps"])
                dve.wait_ge(s["rank_sb"], 1)
                dve.wait_ge(s["need_sb"], 1)
                for seq in range(2):
                    nc.vector.tensor_tensor(rank[:, tiles[seq], :], rank[:, tiles[seq], :], per_tile(need, seq), ALU.is_le)\
                        .then_inc(s["ok"], 1)
                dve.wait_ge(s["ok"], 2)
                nc.vector.tensor_tensor(rank[:], rank[:], ties[:], ALU.mult).then_inc(s["tied"], 1)
                dve.wait_ge(s["tied"], 1)
                nc.vector.tensor_tensor(chosen[:], rank[:], hits[:], ALU.add).then_inc(s["sel"], 1)
                ranks(s["sel_ps"])
                dve.wait_ge(s["rank_sb"], 2)
                nc.vector.tensor_tensor(slot[:].rearrange("p (t e) -> p t e", e=NE), rank[:], chosen[:], ALU.mult)\
                    .then_inc(s["slot_sb"], 1)
                dve.wait_ge(s["slot_sb"], 1)

                def set_onehot(e, t):
                    w = CAPS[int(t >= NTP)]
                    nc.vector.tensor_scalar(onehot[:, t % R, 0:w], slot_row[:, 0:w], slot[:, bass.ds(e + t * NE, 1)], None,
                                            ALU.is_equal).then_inc(s["oh_set"], 1)
                for t in range(R):
                    set_onehot(0, t)
                with dve.Fori(0, NE - 1) as e:
                    for t in range(R, NT + R):
                        dve.wait_ge(s["oh_used"], e * NT + t - R + 1)
                        set_onehot(e + t // NT, t % NT)
                for t in range(R, NT):
                    dve.wait_ge(s["oh_used"], (NE - 1) * NT + t - R + 1)
                    set_onehot(NE - 1, t)
                dve.wait_ge(s["oh_used"], NE * NT)
                for j in range(ST):
                    v = ps_i[j][:, 0:2 * NE].rearrange("p (e c) -> p e c", c=2)
                    nc.vector.tensor_copy(rank[:, 0:2, :].rearrange("p t e -> p (t e)"), ps_i[j][:, 0:2 * NE])\
                        .then_inc(s["lists"], 1)
                    dve.wait_ge(s["lists"], 2 * j + 1)
                    v = rank[:, 0:2, :].rearrange("p t e -> p (t e)").rearrange("p (e c) -> p e c", c=2)
                    nc.vector.scalar_tensor_tensor(out=slots[:, j, :], in0=v[:, :, 0], scalar=float(P), in1=v[:, :, 1],
                                                   op0=ALU.mult, op1=ALU.add).then_inc(s["lists"], 1)
                    dve.wait_ge(s["lists"], 2 * j + 2)


def expert_phase(nc, A, slots):
    S = ST * P
    UC = 256
    NU = D // UC
    UNITS = [(w, j) for j in range(NU) for w in ("w_gate", "w_up")] + [("w_down", j) for j in range(NU)]
    M = len(UNITS)
    RS, RW = 4, 3
    ROUNDS = 2 * ST
    assert M % RS == 0 and M % RW == 0
    with Phase(nc, "exp") as ph:
        ident = ph.sb("ident", [P, P])
        stage = ph.sb("stage", [P, RS, KC, UC])
        w_hi = ph.sb("w_hi", [P, RW, KC, UC], F32R)
        w_lo = ph.sb("w_lo", [P, RW, KC, UC], F32R)
        xe = ph.sb("xe", [P, 2, ST, XN_COLS])
        xT_hi = ph.sb("xT_hi", [P, KC, S], F32R)
        xT_lo = ph.sb("xT_lo", [P, KC, S], F32R)
        hT_hi = ph.sb("hT_hi", [P, KC, S], F32R)
        hT_lo = ph.sb("hT_lo", [P, KC, S], F32R)
        act_g = ph.sb("act_g", [P, 2, S])
        hid = ph.sb("hid", [P, 2, S])
        ye = ph.sb("ye", [P, ST, D])
        gates = ph.sb("gates", [P, 2, ST])
        ps_g = ph.psum("ps_g", [P, 2, 512])
        ps_u = ph.psum("ps_u", [P, 2, 512])
        ps_d = ph.psum("ps_d", [P, ST, 512])
        ps_t = ph.psum("ps_t", [P, 4, P])
        down_banks = [[ps_d[:, q, :] for q in range(ST)], [ps_g[:, 0, :], ps_g[:, 1, :], ps_u[:, 0, :]]]
        down_banks += [down_banks[0], [ps_u[:, 0, :], ps_u[:, 1, :], ps_t[:].rearrange("p a b -> p (a b)")]]
        consts = ph.sem("consts")
        loaded = [ph.sem(f"loaded{r}") for r in range(RS)]
        gathered = [ph.sem(f"gathered{u}") for u in range(2)]
        names = "w_hi_sb w_lo_sb unit_done xT_ps xT_hi_sb xT_lo_sb act_sb hid_sb h_hi_sb h_lo_sb scattered gate_sb y_out".split()
        s = {n: ph.sem(n) for n in names}

        def loop(eng, body):
            with eng.Fori(0, NE // 2 - 1) as i:
                body(i, False)
            body(NE // 2 - 1, True)

        AFTER = {8: (0, 1), 9: (2, 3), 10: (4, 5), 11: ()}

        def ahead(e, m, by, more):
            if m + by < M:
                return e, m + by
            return (e + 1, m + by - M) if more else None

        with nc.Block() as block:
            @block.sync
            def _(sp):
                sp.dma_start(ident[:], A["ident"]).then_inc(consts, 16)

                def load(e, m):
                    w, j = UNITS[m]
                    for half in (1, 0):
                        k = half * KC // 2
                        src = A[w][bass.ds(e, 1), k * P:k * P + D // 2, j * UC:(j + 1) * UC]
                        sp.dma_start(stage[:, m % RS, k:k + KC // 2, :], src.rearrange("o (k p) c -> p (o k) c", p=P))\
                            .then_inc(loaded[m % RS], 16)
                for m in range(RS):
                    load(0, m)

                def body(i, last):
                    for u in range(2):
                        e = 2 * i + u
                        for m in range(M):
                            nxt = ahead(e, m, RS, not (last and u))
                            if nxt:
                                sp.wait_ge(s["w_lo_sb"], e * M + m + 1)
                                load(*nxt)
                loop(sp, body)

            @block.gpsimd
            def _(pool):
                def gather(e):
                    for j in range(ST):
                        nc.gpsimd.indirect_dma_start(xe[:, e % 2, j, :], None, A["xn"],
                                                     bass.IndirectOffsetOnAxis(ap=slots[:, j, e:e + 1], axis=0))\
                            .then_inc(gathered[e % 2], 16)
                def gate(e):
                    pool.wait_ge(gathered[e % 2], 16 * ST * (e // 2 + 1))
                    nc.gpsimd.tensor_copy(gates[:, e % 2, :], xe[:, e % 2, :, D + e]).then_inc(s["gate_sb"], 1)
                gather(0)
                gather(1)
                gate(0)
                gate(1)
                for e in range(NE):
                    pool.wait_ge(s["y_out"], (e + 1) * NU)
                    if e:
                        pool.wait_ge(s["scattered"], 16 * ST * e)
                    for j in range(ST):
                        nc.gpsimd.indirect_dma_start(A["y"], bass.IndirectOffsetOnAxis(ap=slots[:, j, e:e + 1], axis=0),
                                                     ye[:, j, :], None, compute_op=ALU.add).then_inc(s["scattered"], 16)
                    if e + 2 < NE:
                        pool.wait_ge(s["xT_lo_sb"], ROUNDS * (e + 1))
                        pool.wait_ge(s["gate_sb"], e + 1)
                        gather(e + 2)
                        gate(e + 2)
                pool.wait_ge(s["scattered"], 16 * ST * NE)

            @block.scalar
            def _(act):
                def split(e, m):
                    act.wait_ge(loaded[m % RS], 32 * (e * (M // RS) + m // RS + 1))
                    nc.scalar.activation(w_hi[:, m % RW, :, :], stage[:, m % RS, :, :], ACT.Copy).then_inc(s["w_hi_sb"], 1)

                def hi_x(e, r):
                    act.wait_ge(s["xT_ps"], e * ROUNDS + r + 1)
                    j, k = r // 2, r % 2 * 4
                    nc.scalar.activation(xT_hi[:, k:k + 4, j * P:(j + 1) * P], ps_t[:], ACT.Copy).then_inc(s["xT_hi_sb"], 1)

                def body(i, last):
                    for u in range(2):
                        e = 2 * i + u
                        more = not (last and u)
                        for m, (w, j) in enumerate(UNITS):
                            nxt = ahead(e, m, RW - 1, more)
                            if nxt:
                                ge(act, s["unit_done"], e * M + m)
                                split(*nxt)
                            if w == "w_gate":
                                act.wait_ge(s["unit_done"], e * M + m + 1)
                                ge(act, s["hid_sb"], e * NU + j)
                                nc.scalar.activation(act_g[:], ps_g[:, :, 0:S], ACT.Silu).then_inc(s["act_sb"], 1)
                            elif w == "w_up":
                                act.wait_ge(s["hid_sb"], e * NU + j + 1)
                                nc.scalar.activation(hT_hi[:, 2 * j:2 * j + 2, :], hid[:], ACT.Copy).then_inc(s["h_hi_sb"], 1)
                            else:
                                act.wait_ge(s["unit_done"], e * M + m + 1)
                                ge(act, s["scattered"], 16 * ST * e)
                                if j == 0:
                                    act.wait_ge(s["gate_sb"], e + 1)
                                for q in range(ST):
                                    x_ = nc.scalar.activation(ye[:, q, j * UC:(j + 1) * UC], down_banks[j][q][:, 0:UC], ACT.Copy,
                                                              scale=gates[:, u, q:q + 1])
                                x_.then_inc(s["y_out"], 1)
                                if more:
                                    for r in AFTER[m]:
                                        hi_x(e + 1, r)
                for m in range(RW - 1):
                    split(0, m)
                for r in range(ROUNDS):
                    hi_x(0, r)
                loop(act, body)

            @block.vector
            def _(dve):
                def split(e, m):
                    dve.wait_ge(s["w_hi_sb"], e * M + m + 1)
                    nc.vector.tensor_tensor(w_lo[:, m % RW, :, :], stage[:, m % RS, :, :], w_hi[:, m % RW, :, :].bitcast(F32),
                                            ALU.subtract).then_inc(s["w_lo_sb"], 1)

                def lo_x(e, r):
                    dve.wait_ge(s["xT_hi_sb"], e * ROUNDS + r + 1)
                    j, k = r // 2, r % 2 * 4
                    to = (slice(None), slice(k, k + 4), slice(j * P, (j + 1) * P))
                    nc.vector.tensor_tensor(xT_lo[to], ps_t[:], xT_hi[to].bitcast(F32), ALU.subtract).then_inc(s["xT_lo_sb"], 1)

                def body(i, last):
                    for u in range(2):
                        e = 2 * i + u
                        more = not (last and u)
                        for m, (w, j) in enumerate(UNITS):
                            nxt = ahead(e, m, RW - 1, more)
                            if nxt:
                                split(*nxt)
                            if w == "w_up":
                                dve.wait_ge(s["act_sb"], e * NU + j + 1)
                                dve.wait_ge(s["unit_done"], e * M + m + 1)
                                ge(dve, s["h_lo_sb"], e * NU + j)
                                nc.vector.tensor_tensor(hid[:], act_g[:], ps_u[:, :, 0:S], ALU.mult).then_inc(s["hid_sb"], 1)
                                dve.wait_ge(s["h_hi_sb"], e * NU + j + 1)
                                nc.vector.tensor_tensor(hT_lo[:, 2 * j:2 * j + 2, :], hid[:], hT_hi[:, 2 * j:2 * j + 2, :].bitcast(F32),
                                                        ALU.subtract).then_inc(s["h_lo_sb"], 1)
                            elif w == "w_down" and more:
                                for r in AFTER[m]:
                                    lo_x(e + 1, r)
                for m in range(RW - 1):
                    split(0, m)
                for r in range(ROUNDS):
                    lo_x(0, r)
                loop(dve, body)

            @block.tensor
            def _(pe):
                pe.wait_ge(consts, 16)

                def turn(e, u, n, r):
                    if r == 0:
                        pe.wait_ge(gathered[u], 16 * ST * n)
                    ge(pe, s["xT_lo_sb"], e * ROUNDS + r)
                    j, k0 = r // 2, r % 2 * 4
                    for k in range(4):
                        x_ = nc.tensor.transpose(ps_t[:, k, :], xe[:, u, j, (k0 + k) * P:(k0 + k + 1) * P], ident[:])
                    x_.then_inc(s["xT_ps"], 1)

                def passes(slot, hi, lo):
                    return ((w_lo, hi), (w_hi, lo), (w_hi, hi))

                def body(i, last):
                    for u in range(2):
                        e = 2 * i + u
                        more = not (last and u)
                        for m, (w, j) in enumerate(UNITS):
                            pe.wait_ge(s["w_lo_sb"], e * M + m + 1)
                            if m == 0:
                                pe.wait_ge(s["xT_lo_sb"], ROUNDS * (e + 1))
                            if w != "w_down":
                                ps, free = (ps_g, "act_sb") if w == "w_gate" else (ps_u, "hid_sb")
                                ge(pe, s[free], e * NU + j)
                                if m == 1:
                                    ge(pe, s["y_out"], e * NU)
                                for f in range(2):
                                    n = 0
                                    for k in range(KC):
                                        for a, b in passes(m % RW, xT_hi, xT_lo):
                                            x_ = nc.tensor.matmul(ps[:, f, 0:S], a[:, m % RW, k, f * P:(f + 1) * P], b[:, k, :],
                                                                  start=(n == 0), stop=(n == 3 * KC - 1))
                                            n += 1
                            else:
                                if j == 0:
                                    ge(pe, s["y_out"], e * NU)
                                elif j == 1:
                                    pe.wait_ge(s["act_sb"], (e + 1) * NU)
                                    pe.wait_ge(s["hid_sb"], (e + 1) * NU)
                                else:
                                    pe.wait_ge(s["y_out"], e * NU + j - 1)
                                if j == NU - 1 and more:
                                    pe.wait_ge(s["xT_lo_sb"], ROUNDS * (e + 2))
                                for k in range(KC):
                                    if j == 0 and k % 2 == 0:
                                        pe.wait_ge(s["h_lo_sb"], e * NU + k // 2 + 1)
                                    for q in range(ST):
                                        rows = slice(q * P, (q + 1) * P)
                                        for n, (a, b) in enumerate(passes(m % RW, hT_hi, hT_lo)):
                                            x_ = nc.tensor.matmul(down_banks[j][q][:, 0:UC], b[:, k, rows], a[:, m % RW, k, :],
                                                                  start=(k == 0 and n == 0), stop=(k == KC - 1 and n == 2))
                            x_.then_inc(s["unit_done"], 1)
                            if w == "w_down" and more:
                                for r in AFTER[m]:
                                    turn(e + 1, 1 - u, i + 1 + u, r)
                for r in range(ROUNDS):
                    turn(0, 0, 1, r)
                loop(pe, body)


def final_phase(nc, A):
    R = 4
    with Phase(nc, "fin") as ph:
        g = ph.sb("g", [P, D])
        y = ph.sb("y", [P, R, D])
        out = ph.sb("out", [P, R, D])
        stat = ph.sb("stat", [P, R, 4])
        half = ph.sb("half", [P, 1])
        g_loaded, half_set = ph.sem("g_loaded"), ph.sem("half_set")
        loaded = [ph.sem(f"loaded{r}") for r in range(R)]
        stored = [ph.sem(f"stored{r}") for r in range(R)]
        squared, meaned, powered, normed = (ph.sem(n) for n in ("squared", "meaned", "powered", "normed"))
        with nc.Block() as block:
            @block.sync
            def _(sp):
                sp.dma_start(g[:], A["g_final"]).then_inc(g_loaded, 16)
                for r in range(R):
                    sp.dma_start(y[:, r, :], A["y"][r * P:(r + 1) * P, :]).then_inc(loaded[r], 16)
                with sp.Fori(0, NT // R - 1) as i:
                    for r in range(R):
                        t = R * i + r
                        row = sp.snap((t + R) * P)
                        sp.wait_ge(normed, t + 1)
                        sp.dma_start(y[:, r, :], A["y"][bass.ds(row, P), :]).then_inc(loaded[r], 16)

            @block.scalar
            def _(act):
                with act.Fori(0, NT // R) as i:
                    for r in range(R):
                        t = R * i + r
                        act.wait_ge(loaded[r], 16 * (i + 1))
                        ge(act, stored[r], 16 * i)
                        nc.scalar.activation(out[:, r, :], y[:, r, :], ACT.Square, accum_out=stat[:, r, 0:1]).then_inc(squared, 1)

            @block.gpsimd
            def _(pool):
                nc.gpsimd.memset(half[:], -0.5).then_inc(half_set, 1)
                pool.wait_ge(half_set, 1)
                with pool.Fori(0, NT // R) as i:
                    for r in range(R):
                        t = R * i + r
                        pool.wait_ge(meaned, t + 1)
                        nc.gpsimd.tensor_tensor(stat[:, r, 2:3], stat[:, r, 1:2], half[:], ALU.pow).then_inc(powered, 1)
                        pool.wait_ge(normed, t + 1)
                        nc.gpsimd.dma_start(A["out"][bass.ds(t * P, P), :], out[:, r, :]).then_inc(stored[r], 16)
                for r in range(R):
                    pool.wait_ge(stored[r], 16 * (NT // R))

            @block.vector
            def _(dve):
                dve.wait_ge(g_loaded, 16)
                with dve.Fori(0, NT // R) as i:
                    for r in range(R):
                        t = R * i + r
                        dve.wait_ge(squared, t + 1)
                        nc.vector.tensor_scalar(stat[:, r, 1:2], stat[:, r, 0:1], 1.0 / D, EPS, ALU.mult, ALU.add).then_inc(meaned, 1)
                        dve.wait_ge(powered, t + 1)
                        nc.vector.scalar_tensor_tensor(out=out[:, r, :], in0=y[:, r, :], scalar=stat[:, r, 2:3], in1=g[:],
                                                       op0=ALU.mult, op1=ALU.mult).then_inc(normed, 1)


DRAM_IN = dict(x=(TOK, D), mem=(2 * MEM, D), w_in=(D, D_IN), w_mem_kv=(D, 2 * D_C), w_out=(D, D), w_router=(D, NE),
               w_gate=(NE, D, D), w_up=(NE, D, D), w_down=(NE, D, D), g_mix=(P, KC), g_mem=(P, KC), g_out=(P, KC),
               w_sT=(P, GB, P), b_sT=(P, GB), ln_g=(P, D_B), ln_b=(P, D_B), g_ffn=(P, D), g_final=(P, D),
               ident=(P, P), cossin=(TOK, 4 * HD // 2), masks=(P, 5, 2 * P), tri=(P, P), ids=(P, 2 * NT), slot_row=(P, CAPS[0]),
               bits=(P, BITS))
SCRATCH = dict(q=(TOK, D_A), kv=(KV_ROWS, 2 * D_A), obc=(TOK, D_B + D_C), o0=(TOK, O_COLS), o1=(TOK, O_COLS),
               o2=(TOK, O_COLS), xn=(TOK, XN_COLS), y=(TOK, D), aff=(TOK, NE))


def build(nc, A, upto=99):
    with Phase(nc, "memory") as keep:
        kmT = keep.sb("kmT", [P, 2, 2, MEM])
        vm = keep.sb("vm", [P, 2, 2, D_C])
        memory_phase(nc, A, kmT, vm)
        if upto >= 1:
            project_phase(nc, A, kmT, vm)
    if upto >= 2:
        attend_phase(nc, A)
    if upto >= 3:
        with Phase(nc, "route") as keep:
            slots = keep.sb("slots", [P, ST, NE], I32)
            affinity = keep.sb("affinity", [P, NT * NE])
            mix_phase(nc, A, affinity)
            if upto >= 4:
                choose_phase(nc, A, affinity, slots)
            if upto >= 5:
                expert_phase(nc, A, slots)
    if upto >= 6:
        final_phase(nc, A)


def constants():
    pos = np.concatenate([np.arange(s, dtype=np.float32) for s in SEQS])
    half = HD // 2
    inv = np.power(10000.0, -np.arange(half) * 2.0 / HD).astype(np.float32)
    ang = pos[:, None] * inv[None, :].astype(np.float32)
    cos, sin = np.cos(ang), np.sin(ang)
    cossin = np.concatenate([cos, cos, -sin, sin], axis=1).astype(np.float32)
    t, w = np.arange(P)[:, None], np.arange(2 * P)[None, :]
    band = np.abs(w - 64 - t) <= 64
    masks = np.zeros((P, 5, 2 * P), np.float32)
    masks[:, 0] = np.where(band & (w >= 64), 0, NEG)
    masks[:, 1] = np.where(band, 0, NEG)
    masks[:, 2] = np.where(band & (w < 64 + P), 0, NEG)
    masks[:, 3, :P] = np.where(np.abs(w[:, :P] - t) <= 64, 0, NEG)
    masks[:, 4, :P] = np.where(w[:, :P] // 64 == t // 64, 0, NEG)
    tri = (np.arange(P)[:, None] <= np.arange(P)[None, :]).astype(np.float32)
    ids = np.zeros((P, NT, 2), np.float32)
    ids[:, :, 0] = np.arange(NT)[None, :]
    ids[:, :, 1] = np.arange(P)[:, None]
    slot_row = np.broadcast_to(np.arange(1, CAPS[0] + 1, dtype=np.float32), (P, CAPS[0]))
    bits = (1 << np.arange(BITS - 1, -1, -1, dtype=np.int32)).astype(np.int32)
    return dict(ident=np.eye(P, dtype=np.float32), cossin=cossin, masks=masks, tri=tri, ids=ids.reshape(P, 2 * NT),
                slot_row=slot_row, bits=np.broadcast_to(bits.view(np.float32), (P, BITS)))


def lay_out(i):
    rows = lambda v: np.broadcast_to(np.asarray(v).reshape(1, -1), (P, v.size))
    cols = lambda v: np.asarray(v).reshape(KC, P).T
    a = {k: np.asarray(v) for k, v in i.items()}
    return dict(
        x=np.concatenate([a["x_prompt"][0], a["x_sample"][0]]), mem=np.concatenate([a["mem_prompt"][0], a["mem_sample"][0]]),
        w_in=a["w_in"][0], w_mem_kv=a["w_mem_kv"][0], w_out=a["w_out"][0], w_router=a["w_router"][0],
        w_gate=a["w_gate"][0], w_up=a["w_up"][0], w_down=a["w_down"][0],
        g_mix=cols(a["g_mix"]), g_mem=cols(a["g_mem"]), g_out=cols(a["g_out"]),
        w_sT=a["w_spatial"][0].transpose(2, 0, 1), b_sT=a["b_spatial"][0].T, ln_g=rows(a["ln_b_g"]), ln_b=rows(a["ln_b_b"]),
        g_ffn=rows(a["g_ffn"]), g_final=rows(a["g_final"]), **constants())


def kernel(**inputs):
    import concourse.bacc as bacc
    from concourse.bass_utils import run_bass_kernel_spmd

    nc = bacc.Bacc("TRN2", target_bir_lowering=False, num_devices=1)
    laid = lay_out(inputs)
    arrays, A = {}, {}
    for name, shape in DRAM_IN.items():
        arrays[f"in_{name}"] = np.ascontiguousarray(laid[name])
        A[name] = nc.dram_tensor(f"in_{name}", shape, F32, kind="ExternalInput").ap()
    for name, shape in SCRATCH.items():
        A[name] = nc.dram_tensor(f"scratch_{name}", shape, F32, kind="Internal").ap()
    A["out"] = nc.dram_tensor("out", (TOK, D), F32, kind="ExternalOutput").ap()
    build(nc, A)
    out = run_bass_kernel_spmd(nc, [arrays], core_ids=[0]).results[0]["out"]
    return out[None, :SEQS[0]], out[None, SEQS[0]:]
```

```python
from contextlib import ExitStack

import numpy as np

import concourse.bass as bass
from concourse import mybir

F32 = mybir.dt.float32
F32R = mybir.dt.float32r
BF16 = mybir.dt.bfloat16
I32 = mybir.dt.int32
U32 = mybir.dt.uint32
ACT = mybir.ActivationFunctionType
ALU = mybir.AluOpType
AX_X = mybir.AxisListType.X

P = 128
D = 1024
KC = D // P
SEQS = (2048, 1024)
TOK = sum(SEQS)
NT = TOK // P
NTP = SEQS[0] // P
PAIRS = NT // 2
PAIRS_P = NTP // 2
HA, HD = 8, 64
D_A = HA * HD
D_B = 256
GB, GD = 4, 64
HC = 4
D_C = HC * HD
D_IN = 3 * D_A + 2 * D_B + D_C
MEM = 256
NE = 16
EPS = 1e-6
SCALE = HD ** -0.5
NEG = -1e30
PAD = 256
KV_ROWS = sum(s + 2 * PAD for s in SEQS)
KV_BASE = (PAD, SEQS[0] + 3 * PAD)
O_COLS = D_A + 2 * HA
XN_COLS = D + NE
CAPS = tuple(2 * s // NE for s in SEQS)
ST = sum(CAPS) // P
BITS = 30
GELU_C = 2.0 * (2.0 / np.pi) ** 0.5


def ge(eng, sem, value):
    if isinstance(value, int) and value <= 0:
        return
    eng.wait_ge(sem, value)


def is_first(t):
    return isinstance(t, int) and t == 0


def bank_of(h):
    return h % 2 * 2 + h // 2


class Phase:

    def __init__(self, nc, name):
        self.nc, self.name, self.ctx, self.sems = nc, name, ExitStack(), []

    def __enter__(self):
        return self

    def __exit__(self, *e):
        self.ctx.close()
        if self.sems:
            self.nc.clear_and_free_semaphores(self.sems)
            self.nc.all_engine_barrier()

    def sb(self, name, shape, dt=F32):
        return self.ctx.enter_context(self.nc.sbuf_tensor(f"{self.name}_{name}", shape, dt))

    def psum(self, name, shape):
        return self.ctx.enter_context(self.nc.psum_tensor(f"{self.name}_{name}", shape, F32))

    def sem(self, name):
        self.sems.append(self.nc.alloc_semaphore(f"{self.name}_{name}"))
        return self.sems[-1]


def memory_phase(nc, A, kmT, vm):
    NM = 2 * MEM // P
    with Phase(nc, "mem") as ph:
        ident = ph.sb("ident", [P, P])
        m = ph.sb("rows", [P, NM, D])
        w = ph.sb("w", [P, KC, 2 * D_C])
        g = ph.sb("g", [P, KC])
        junk = ph.sb("junk", [P, D], BF16)
        ss = ph.sb("ss", [P, NM])
        ms = ph.sb("ms", [P, NM])
        rstd = ph.sb("rstd", [P, NM])
        half = ph.sb("half", [P, NM])
        mT = ph.sb("mT", [P, KC, P])
        kt = ph.sb("k", [P, D_C])
        zero = ph.sb("zero", [P, D_A])
        psT = ph.psum("psT", [P, KC, P])
        psKV = ph.psum("psKV", [P, 2 * D_C])
        psK = ph.psum("psK", [P, 4, P])
        loaded, zeroed, padded = ph.sem("loaded"), ph.sem("zeroed"), ph.sem("padded")
        squared, meaned, powered, scaled = (ph.sem(x) for x in ("squared", "meaned", "powered", "scaled"))
        w_scaled, turned, turned_sb, kv_ps = (ph.sem(x) for x in ("w_scaled", "turned", "turned_sb", "kv_ps"))
        k_sb, v_sb, kT_ps, kT_sb, half_set = (ph.sem(x) for x in ("k_sb", "v_sb", "kT_ps", "kT_sb", "half_set"))
        with nc.Block() as block:
            @block.sync
            def _(sp):
                sp.dma_start(m[:], A["mem"].rearrange("(n p) d -> p n d", p=P)).then_inc(loaded, 16)
                sp.dma_start(w[:], A["w_mem_kv"].rearrange("(n p) d -> p n d", p=P)).then_inc(loaded, 16)
                sp.dma_start(g[:], A["g_mem"]).then_inc(loaded, 16)
                sp.dma_start(ident[:], A["ident"]).then_inc(loaded, 16)
                sp.wait_ge(zeroed, 1)
                row = 0
                pads = 0
                for s in SEQS:
                    for r in (row, row + PAD + s):
                        for j in range(0, PAD, P):
                            sp.dma_start(A["v"][r + j:r + j + P, :], zero[:]).then_inc(padded, 16)
                            pads += 1
                    row += s + 2 * PAD
                sp.wait_ge(padded, 16 * pads)

            @block.gpsimd
            def _(pool):
                nc.gpsimd.memset(half[:], -0.5).then_inc(half_set, 1)
                pool.wait_ge(half_set, 1)
                pool.wait_ge(meaned, 1)
                nc.gpsimd.tensor_tensor(rstd[:], ms[:], half[:], ALU.pow).then_inc(powered, 1)

            @block.scalar
            def _(act):
                act.wait_ge(loaded, 64)
                for n in range(NM):
                    if n:
                        act.wait_ge(squared, n)
                    nc.scalar.activation(junk[:], m[:, n, :], ACT.Square, accum_out=ss[:, n:n + 1]).then_inc(squared, 1)
                act.wait_ge(powered, 1)
                for n in range(NM):
                    nc.scalar.activation(m[:, n, :], m[:, n, :], ACT.Copy, scale=rstd[:, n:n + 1]).then_inc(scaled, 1)
                for n in range(NM):
                    act.wait_ge(kv_ps, n + 1)
                    if n:
                        act.wait_ge(kT_ps, n)
                    nc.scalar.activation(kt[:], psKV[:, 0:D_C], ACT.Copy).then_inc(k_sb, 1)
                    nc.scalar.activation(vm[:, n // 2, n % 2, :], psKV[:, D_C:], ACT.Copy).then_inc(v_sb, 1)

            @block.vector
            def _(dve):
                nc.vector.memset(zero[:], 0.0).then_inc(zeroed, 1)
                dve.wait_ge(loaded, 64)
                for k in range(KC):
                    nc.vector.tensor_scalar(w[:, k, :], w[:, k, :], g[:, k:k + 1], None, ALU.mult).then_inc(w_scaled, 1)
                dve.wait_ge(squared, NM)
                nc.vector.tensor_scalar(ms[:], ss[:], 1.0 / D, EPS, ALU.mult, ALU.add).then_inc(meaned, 1)
                for n in range(NM):
                    dve.wait_ge(turned, n + 1)
                    if n:
                        dve.wait_ge(kv_ps, n)
                    nc.vector.tensor_copy(mT[:], psT[:]).then_inc(turned_sb, 1)
                    dve.wait_ge(kT_ps, n + 1)
                    nc.vector.tensor_copy(kmT[:, n // 2, :, (n % 2) * P:(n % 2 + 1) * P], psK[:, 0:2, :]).then_inc(kT_sb, 1)

            @block.tensor
            def _(pe):
                pe.wait_ge(w_scaled, KC)
                for n in range(NM):
                    pe.wait_ge(scaled, n + 1)
                    for k in range(KC):
                        last = nc.tensor.transpose(psT[:, k, :], m[:, n, k * P:(k + 1) * P], ident[:])
                    last.then_inc(turned, 1)
                    pe.wait_ge(turned_sb, n + 1)
                    if n:
                        pe.wait_ge(k_sb, n)
                        pe.wait_ge(v_sb, n)
                    for k in range(KC):
                        last = nc.tensor.matmul(psKV[:], mT[:, k, :], w[:, k, :], start=(k == 0), stop=(k == KC - 1))
                    last.then_inc(kv_ps, 1)
                    pe.wait_ge(k_sb, n + 1)
                    if n:
                        pe.wait_ge(kT_sb, n)
                    for j in range(2):
                        last = nc.tensor.transpose(psK[:, j, :], kt[:, j * P:(j + 1) * P], ident[:])
                    last.then_inc(kT_ps, 1)


def split_weights(nc, ph, dram, g, g_loaded, w_hi, w_lo, cols):
    with Phase(nc, ph.name + "_split") as sp_:
        stage = sp_.sb("stage", [P, 2, cols])
        loaded = [sp_.sem(f"loaded{i}") for i in range(2)]
        hi_done, lo_done = sp_.sem("hi_done"), sp_.sem("lo_done")
        with nc.Block() as block:
            @block.sync
            def _(sp):
                for k in range(KC):
                    ge(sp, lo_done, k - 1)
                    sp.dma_start(stage[:, k % 2, :], dram[k * P:(k + 1) * P, :]).then_inc(loaded[k % 2], 16)

            @block.scalar
            def _(act):
                act.wait_ge(g_loaded, 16)
                for k in range(KC):
                    act.wait_ge(loaded[k % 2], 16 * (k // 2 + 1))
                    nc.scalar.activation(w_hi[:, k, :], stage[:, k % 2, :], ACT.Copy, scale=g[:, k:k + 1]).then_inc(hi_done, 1)

            @block.vector
            def _(dve):
                for k in range(KC):
                    dve.wait_ge(hi_done, k + 1)
                    nc.vector.scalar_tensor_tensor(out=w_lo[:, k, :], in0=stage[:, k % 2, :], scalar=g[:, k:k + 1],
                                                   in1=w_hi[:, k, :].bitcast(F32), op0=ALU.mult,
                                                   op1=ALU.subtract).then_inc(lo_done, 1)


def project_phase(nc, A, kmT, vm):
    with Phase(nc, "prj") as ph:
        ident = ph.sb("ident", [P, P])
        w_hi = ph.sb("w_hi", [P, KC, D_IN], F32R)
        w_lo = ph.sb("w_lo", [P, KC, D_IN], F32R)
        g = ph.sb("g", [P, KC])
        consts = ph.sem("consts")
        g_loaded = ph.sem("g_loaded")
        with nc.Block() as block:
            @block.sync
            def _(sp):
                sp.dma_start(g[:], A["g_mix"]).then_inc(g_loaded, 16)
                sp.dma_start(ident[:], A["ident"]).then_inc(consts, 16)
                sp.wait_ge(consts, 16)
                sp.wait_ge(g_loaded, 16)
        split_weights(nc, ph, A["w_in"], g, g_loaded, w_hi, w_lo, D_IN)

        x = ph.sb("x", [P, 2, D])
        cs = ph.sb("cs", [P, 2, 4, HD // 2])
        hT_hi = ph.sb("hT_hi", [P, 2, KC, P], F32R)
        hT_lo = ph.sb("hT_lo", [P, 2, KC, P], F32R)
        qkv = ph.sb("qkv", [P, 3, D_A])
        obc = ph.sb("obc", [P, D_B + D_C])
        uv_a = ph.sb("uv_a", [P, 2 * D_B])
        uv_b = ph.sb("uv_b", [P, 2 * D_B])
        rot_b = ph.sb("rot_b", [P, D_A])
        vln = ph.sb("vln", [P, D_B])
        ob = uv_b[:, 0:D_B]
        oc = ph.sb("oc", [P, D_C])
        qc = ph.sb("qc", [P, D_C])
        qcT = ph.sb("qcT", [P, 2, P])
        prob = ph.sb("prob", [P, HC, MEM])
        probT = ph.sb("probT", [P, 2 * HC, P])
        wsT = ph.sb("wsT", [P, GB, P])
        bs = ph.sb("bs", [P, GB])
        ln_g = ph.sb("ln_g", [P, D_B])
        ln_b = ph.sb("ln_b", [P, D_B])
        stat = ph.sb("stat", [P, 64])
        half = ph.sb("half", [P, 2])
        ssx, msx, rsx = stat[:, 0:1], stat[:, 1:2], stat[:, 2:3]
        bn6, mv, vev, rsv = stat[:, 4:10], stat[:, 10:12], stat[:, 12:13], stat[:, 13:14]
        mx, nmx, den, rden = stat[:, 16:20], stat[:, 20:24], stat[:, 24:28], stat[:, 28:32]
        ssb, ssc, msbc, rsbc = stat[:, 32:33], stat[:, 33:34], stat[:, 34:36], stat[:, 36:38]

        ps_x = ph.psum("ps_x", [P, 8, P])
        ps_a = ph.psum("ps_a", [P, 512])
        ps_b = ph.psum("ps_b", [P, 512])
        ps_c = ph.psum("ps_c", [P, 512])
        ps_s = ph.psum("ps_s", [P, HC, MEM])
        ps_o = ph.psum("ps_o", [P, 512])

        names = """squared_x meaned_x powered_x scaled_x z_qc z_uv z_q z_k z_v qc_sb qcT_ps qcT_sb sc_ps xT
            hi_sb lo_sb uv_sq inner0 inner g_exp g_exp1 g_rec guv bn_a bn_b var_eps rstd_v vn vn_g vln_sb sp_ps ob_sb
            rotq_a rotq rotq_sb rotk_a rotk rotk_sb maxed nmx_sb p_sb pT_ps pT_a pT_b v_sb pv_ps rden_sb oc_sb
            sq_b sq_c ms_bc rs_bc ob_out oc_out half_set qT_ps qT_sb kT_ps kT_sb""".split()
        s = {n: ph.sem(n) for n in names}
        x_loaded = [ph.sem(f"x_loaded{u}") for u in range(2)]
        q_stored, k_stored, v_stored, obc_stored = (ph.sem(n) for n in ("q_stored", "k_stored", "v_stored", "obc_stored"))

        def loop(eng, body, start=None):
            if start:
                start()
            body(0, 0, False)
            with eng.Fori(1, PAIRS_P) as i:
                body(i, 0, False)
            with eng.Fori(PAIRS_P, PAIRS - 1) as i:
                body(i, 1, False)
            body(PAIRS - 1, 1, True)

        with nc.Block() as block:
            @block.sync
            def _(sp):
                for dst, src in ((wsT, "w_sT"), (bs, "b_sT"), (ln_g, "ln_g"), (ln_b, "ln_b")):
                    sp.dma_start(dst[:], A[src]).then_inc(consts, 16)

                def load(t, u):
                    sp.dma_start(x[:, u, :], A["x"][bass.ds(t * P, P), :]).then_inc(x_loaded[u], 16)
                    sp.dma_start(cs[:, u, :, :], A["cossin"][bass.ds(t * P, P), :]).then_inc(x_loaded[u], 16)

                def body(i, seq, last):
                    for u in range(2):
                        t = 2 * i + u
                        row = KV_BASE[seq] - (SEQS[0] if seq else 0)
                        sp.wait_ge(s["rotk_sb"], t + 1)
                        if not last:
                            sp.wait_ge(s["xT"], t + 1)
                            load(t + 2, u)
                        sp.wait_ge(s["v_sb"], t + 1)
                        sp.dma_start(A["v"][bass.ds(t * P + row, P), :], qkv[:, 2, :]).then_inc(v_stored, 16)
                        sp.wait_ge(s["ob_out"], t + 1)
                        sp.wait_ge(s["oc_out"], t + 1)
                        sp.wait_ge(s["qT_sb"], t + 1)
                        sp.dma_start(A["obc"][bass.ds(t * P, P), :], obc[:]).then_inc(obc_stored, 16)
                        sp.dma_start(A["qT"][:, :, bass.ds(t * P, P)], qkv[:, 0, :].rearrange("p (j c) -> p j c", c=P)).then_inc(q_stored, 16)
                        sp.wait_ge(s["kT_sb"], t + 1)
                        sp.dma_start(A["kT"][:, :, bass.ds(t * P, P)], qkv[:, 1, :].rearrange("p (j c) -> p j c", c=P)).then_inc(k_stored, 16)

                def start():
                    load(0, 0)
                    load(1, 1)
                loop(sp, body, start)
                for stored in (q_stored, k_stored, v_stored, obc_stored):
                    sp.wait_ge(stored, 16 * NT)

            @block.gpsimd
            def _(pool):
                nc.gpsimd.memset(half[:], -0.5).then_inc(s["half_set"], 1)
                pool.wait_ge(s["half_set"], 1)

                def prep(t):
                    pool.wait_ge(s["meaned_x"], t + 1)
                    ge(pool, s["scaled_x"], t)
                    nc.gpsimd.tensor_tensor(rsx, msx, half[:, 0:1], ALU.pow).then_inc(s["powered_x"], 1)

                def body(i, seq, last):
                    for u in range(2):
                        t = 2 * i + u
                        if not (last and u):
                            prep(t + 1)
                        pool.wait_ge(s["var_eps"], t + 1)
                        ge(pool, s["vn"], t)
                        nc.gpsimd.tensor_tensor(rsv, vev, half[:, 0:1], ALU.pow).then_inc(s["rstd_v"], 1)
                        pool.wait_ge(s["rotq"], t + 1)
                        nc.gpsimd.tensor_tensor(qkv[:, 0, :], qkv[:, 0, :], rot_b[:], ALU.add).then_inc(s["rotq_sb"], 1)
                        pool.wait_ge(s["rotk"], t + 1)
                        nc.gpsimd.tensor_tensor(qkv[:, 1, :], qkv[:, 1, :], rot_b[:], ALU.add).then_inc(s["rotk_sb"], 1)
                        pool.wait_ge(s["ms_bc"], t + 1)
                        ge(pool, s["oc_out"], t)
                        nc.gpsimd.tensor_tensor(rsbc, msbc, half[:], ALU.pow).then_inc(s["rs_bc"], 1)
                loop(pool, body, lambda: prep(0))

            @block.scalar
            def _(act):
                act.wait_ge(consts, 16 * 5)

                def square_x(t, u, n):
                    act.wait_ge(x_loaded[u], 32 * n)
                    ge(act, s["meaned_x"], t)
                    ge(act, s["pv_ps"], t - 1)
                    nc.scalar.activation(probT[:], x[:, u, :].rearrange("p (k c) -> p k c", c=P), ACT.Square, accum_out=ssx).then_inc(s["squared_x"], 1)

                def scale_x(t, u):
                    act.wait_ge(s["powered_x"], t + 1)
                    nc.scalar.activation(x[:, u, :], x[:, u, :], ACT.Copy, scale=rsx).then_inc(s["scaled_x"], 1)

                def hi_x(t, u):
                    act.wait_ge(s["xT"], t + 1)
                    ge(act, s["z_v"], t - 1)
                    nc.scalar.activation(hT_hi[:, u, :, :], ps_x[:], ACT.Copy).then_inc(s["hi_sb"], 1)

                def out_k(t):
                    act.wait_ge(s["kT_ps"], t + 1)
                    nc.scalar.activation(qkv[:, 1, :], ps_c[:], ACT.Copy).then_inc(s["kT_sb"], 1)

                def body(i, seq, last):
                    for u in range(2):
                        t = 2 * i + u
                        more = not (last and u)
                        n = i + 1 + u
                        act.wait_ge(s["z_qc"], t + 1)
                        ge(act, s["qcT_ps"], t)
                        nc.scalar.activation(qc[:], ps_a[:, 0:D_C], ACT.Copy).then_inc(s["qc_sb"], 1)
                        if more:
                            square_x(t + 1, 1 - u, n)
                        act.wait_ge(s["z_uv"], t + 1)
                        ge(act, s["guv"], t)
                        nc.scalar.activation(uv_a[:], ps_b[:], ACT.Square).then_inc(s["uv_sq"], 1)
                        if not is_first(t):
                            out_k(t - 1)
                        act.wait_ge(s["qcT_ps"], t + 1)
                        ge(act, s["sc_ps"], t)
                        nc.scalar.activation(qcT[:], ps_s[:, 0, :], ACT.Copy).then_inc(s["qcT_sb"], 1)
                        if more:
                            scale_x(t + 1, 1 - u)
                        act.wait_ge(s["inner"], t + 1)
                        nc.scalar.activation(uv_a[:], uv_b[:], ACT.Exp, scale=-GELU_C).then_inc(s["g_exp"], 1)
                        if more:
                            hi_x(t + 1, 1 - u)
                        act.wait_ge(s["nmx_sb"], t + 1)
                        ge(act, s["pT_ps"], t)
                        ge(act, s["rden_sb"], t)
                        for h in range(HC):
                            j = bank_of(h)
                            last_exp = nc.scalar.activation(prob[:, h, :], ps_s[:, j, :], ACT.Exp, bias=nmx[:, j:j + 1],
                                                            scale=SCALE, accum_out=den[:, h:h + 1])
                        last_exp.then_inc(s["p_sb"], 1)
                        act.wait_ge(s["ob_sb"], t + 1)
                        ge(act, s["ms_bc"], t)
                        nc.scalar.activation(qc[:], ob, ACT.Square, accum_out=ssb).then_inc(s["sq_b"], 1)
                        act.wait_ge(s["pT_ps"], t + 1)
                        ge(act, s["pv_ps"], t)
                        nc.scalar.activation(probT[:, 0:HC, :], ps_x[:, 0:HC, :], ACT.Copy).then_inc(s["pT_a"], 1)
                        act.wait_ge(s["qT_ps"], t + 1)
                        nc.scalar.activation(qkv[:, 0, :], ps_c[:], ACT.Copy).then_inc(s["qT_sb"], 1)
                        act.wait_ge(s["z_v"], t + 1)
                        ge(act, v_stored, 16 * t)
                        nc.scalar.activation(qkv[:, 2, :], ps_b[:], ACT.Copy).then_inc(s["v_sb"], 1)
                        act.wait_ge(s["oc_sb"], t + 1)
                        act.wait_ge(s["sq_b"], t + 1)
                        nc.scalar.activation(qc[:], oc[:], ACT.Square, accum_out=ssc).then_inc(s["sq_c"], 1)
                        act.wait_ge(s["rs_bc"], t + 1)
                        ge(act, obc_stored, 16 * t)
                        nc.scalar.activation(obc[:, 0:D_B], ob, ACT.Copy, scale=rsbc[:, 0:1]).then_inc(s["ob_out"], 1)
                        nc.scalar.activation(obc[:, D_B:], oc[:], ACT.Copy, scale=rsbc[:, 1:2]).then_inc(s["oc_out"], 1)

                def start():
                    square_x(0, 0, 1)
                    scale_x(0, 0)
                    hi_x(0, 0)
                loop(act, body, start)
                out_k(NT - 1)

            @block.vector
            def _(dve):
                dve.wait_ge(consts, 16 * 5)

                def mean_x(t):
                    dve.wait_ge(s["squared_x"], t + 1)
                    ge(dve, s["powered_x"], t)
                    nc.vector.tensor_scalar(msx, ssx, 1.0 / D, EPS, ALU.mult, ALU.add).then_inc(s["meaned_x"], 1)

                def lo_x(t, u):
                    dve.wait_ge(s["hi_sb"], t + 1)
                    nc.vector.tensor_tensor(hT_lo[:, u, :, :], ps_x[:], hT_hi[:, u, :, :].bitcast(F32),
                                            ALU.subtract).then_inc(s["lo_sb"], 1)

                def rotate(z, out, u, first, second):
                    zh = z.rearrange("p (h two c) -> p h two c", h=HA, two=2)
                    ah = out.rearrange("p (h two c) -> p h two c", h=HA, two=2)
                    bh = rot_b[:].rearrange("p (h two c) -> p h two c", h=HA, two=2)
                    for j in range(2):
                        cos = cs[:, u, j:j + 1, :].broadcast_to([P, HA, HD // 2])
                        last_a = nc.vector.tensor_tensor(ah[:, :, j, :], zh[:, :, j, :], cos, ALU.mult)
                    last_a.then_inc(first, 1)
                    for j in range(2):
                        sin = cs[:, u, 2 + j:3 + j, :].broadcast_to([P, HA, HD // 2])
                        last_b = nc.vector.tensor_tensor(bh[:, :, j, :], zh[:, :, 1 - j, :], sin, ALU.mult)
                    last_b.then_inc(second, 1)

                def body(i, seq, last):
                    for u in range(2):
                        t = 2 * i + u
                        more = not (last and u)
                        if more:
                            mean_x(t + 1)
                        dve.wait_ge(s["uv_sq"], t + 1)
                        ge(dve, s["ob_out"], t)
                        nc.vector.tensor_scalar(uv_b[:], uv_a[:], 0.044715, 1.0, ALU.mult, ALU.add).then_inc(s["inner0"], 1)
                        dve.wait_ge(s["inner0"], t + 1)
                        nc.vector.tensor_tensor(uv_b[:], uv_b[:], ps_b[:], ALU.mult).then_inc(s["inner"], 1)
                        dve.wait_ge(s["g_exp"], t + 1)
                        nc.vector.tensor_scalar(uv_a[:], uv_a[:], 1.0, None, ALU.add).then_inc(s["g_exp1"], 1)
                        dve.wait_ge(s["g_exp1"], t + 1)
                        nc.vector.reciprocal(uv_a[:], uv_a[:]).then_inc(s["g_rec"], 1)
                        dve.wait_ge(s["g_rec"], t + 1)
                        nc.vector.tensor_tensor(uv_b[:], uv_a[:], ps_b[:], ALU.mult).then_inc(s["guv"], 1)
                        dve.wait_ge(s["guv"], t + 1)
                        nc.vector.bn_stats(bn6, uv_b[:, D_B:]).then_inc(s["bn_a"], 1)
                        dve.wait_ge(s["bn_a"], t + 1)
                        nc.vector.memset(stat[:, 40:41], 0.0)
                        nc.vector.bn_aggr(mv, bn6).then_inc(s["bn_b"], 1)
                        dve.wait_ge(s["bn_b"], t + 1)
                        ge(dve, s["rstd_v"], t)
                        nc.vector.tensor_scalar(vev, mv[:, 1:2], EPS, None, ALU.add).then_inc(s["var_eps"], 1)
                        dve.wait_ge(s["z_q"], t + 1)
                        ge(dve, s["rotk_sb"], t)
                        ge(dve, q_stored, 16 * t)
                        rotate(ps_c[:], qkv[:, 0, :], u, s["rotq_a"], s["rotq"])
                        dve.wait_ge(s["rstd_v"], t + 1)
                        ge(dve, s["sp_ps"], t)
                        nc.vector.tensor_scalar(vln[:], uv_b[:, D_B:], mv[:, 0:1], rsv, ALU.subtract, ALU.mult).then_inc(s["vn"], 1)
                        dve.wait_ge(s["vn"], t + 1)
                        nc.vector.tensor_tensor(vln[:], vln[:], ln_g[:], ALU.mult).then_inc(s["vn_g"], 1)
                        dve.wait_ge(s["vn_g"], t + 1)
                        nc.vector.tensor_tensor(vln[:], vln[:], ln_b[:], ALU.add).then_inc(s["vln_sb"], 1)
                        dve.wait_ge(s["sc_ps"], t + 1)
                        nc.vector.tensor_reduce(mx, ps_s[:], AX_X, ALU.max).then_inc(s["maxed"], 1)
                        dve.wait_ge(s["maxed"], t + 1)
                        ge(dve, s["p_sb"], t)
                        nc.vector.tensor_scalar(nmx, mx, -SCALE, None, ALU.mult).then_inc(s["nmx_sb"], 1)
                        if more:
                            lo_x(t + 1, 1 - u)
                        dve.wait_ge(s["z_k"], t + 1)
                        dve.wait_ge(s["rotq_sb"], t + 1)
                        ge(dve, k_stored, 16 * t)
                        rotate(ps_a[:], qkv[:, 1, :], u, s["rotk_a"], s["rotk"])
                        dve.wait_ge(s["sp_ps"], t + 1)
                        for gi in range(GB):
                            c = slice(gi * GD, (gi + 1) * GD)
                            gated = nc.vector.scalar_tensor_tensor(
                                out=ob[:, c], in0=ps_o[:, D_C + gi * GD:D_C + (gi + 1) * GD], scalar=bs[:, gi:gi + 1],
                                in1=uv_b[:, c], op0=ALU.add, op1=ALU.mult)
                        gated.then_inc(s["ob_sb"], 1)
                        dve.wait_ge(s["pT_ps"], t + 1)
                        ge(dve, s["pv_ps"], t)
                        nc.vector.tensor_copy(probT[:, HC:, :], ps_x[:, HC:, :]).then_inc(s["pT_b"], 1)
                        dve.wait_ge(s["p_sb"], t + 1)
                        ge(dve, s["oc_sb"], t)
                        nc.vector.reciprocal(rden, den).then_inc(s["rden_sb"], 1)
                        dve.wait_ge(s["rden_sb"], t + 1)
                        dve.wait_ge(s["pv_ps"], t + 1)
                        ge(dve, s["oc_out"], t)
                        nc.vector.tensor_tensor(oc[:].rearrange("p (h c) -> p h c", h=HC),
                                                ps_o[:, 0:D_C].rearrange("p (h c) -> p h c", h=HC),
                                                rden.rearrange("p (h one) -> p h one", one=1).broadcast_to([P, HC, HD]),
                                                ALU.mult).then_inc(s["oc_sb"], 1)
                        dve.wait_ge(s["sq_b"], t + 1)
                        dve.wait_ge(s["sq_c"], t + 1)
                        ge(dve, s["rs_bc"], t)
                        nc.vector.tensor_scalar(msbc, stat[:, 32:34], 1.0 / D_B, EPS, ALU.mult, ALU.add).then_inc(s["ms_bc"], 1)

                def start():
                    mean_x(0)
                    lo_x(0, 0)
                loop(dve, body, start)

            @block.tensor
            def _(pe):
                pe.wait_ge(consts, 16 * 5)

                def turn(t, u):
                    pe.wait_ge(s["scaled_x"], t + 1)
                    ge(pe, s["pT_a"], t - 1)
                    ge(pe, s["pT_b"], t - 1)
                    for k in range(KC):
                        last = nc.tensor.transpose(ps_x[:, k, :], x[:, u, k * P:(k + 1) * P], ident[:])
                    last.then_inc(s["xT"], 1)

                def turn_k(t):
                    pe.wait_ge(s["rotk_sb"], t + 1)
                    pe.wait_ge(s["qT_sb"], t + 1)
                    for j in range(HA // 2):
                        x_ = nc.tensor.transpose(ps_c[:, j * P:(j + 1) * P], qkv[:, 1, j * P:(j + 1) * P], ident[:])
                    x_.then_inc(s["kT_ps"], 1)

                def product(ps, u, col, width):
                    n = 0
                    for k in range(KC):
                        for a, b in ((hT_lo, w_hi), (hT_hi, w_lo), (hT_hi, w_hi)):
                            last = nc.tensor.matmul(ps[:, 0:width], a[:, u, k, :], b[:, k, col:col + width],
                                                    start=(n == 0), stop=(n == 3 * KC - 1))
                            n += 1
                    return last

                def body(i, seq, last):
                    for u in range(2):
                        t = 2 * i + u
                        pe.wait_ge(s["lo_sb"], t + 1)
                        ge(pe, s["rotk"], t)
                        product(ps_a, u, 3 * D_A + 2 * D_B, D_C).then_inc(s["z_qc"], 1)
                        ge(pe, s["v_sb"], t)
                        product(ps_b, u, 3 * D_A, 2 * D_B).then_inc(s["z_uv"], 1)
                        if not is_first(t):
                            turn_k(t - 1)
                        pe.wait_ge(s["qc_sb"], t + 1)
                        ge(pe, s["p_sb"], t)
                        for j in range(2):
                            x_ = nc.tensor.transpose(ps_s[:, 0, j * P:(j + 1) * P], qc[:, j * P:(j + 1) * P], ident[:])
                        x_.then_inc(s["qcT_ps"], 1)
                        ge(pe, s["kT_sb"], t)
                        product(ps_c, u, 0, D_A).then_inc(s["z_q"], 1)
                        pe.wait_ge(s["qcT_sb"], t + 1)
                        for h in range(HC):
                            lane = slice((h % 2) * HD, (h % 2 + 1) * HD)
                            x_ = nc.tensor.matmul(ps_s[:, bank_of(h), :], qcT[lane, h // 2, :], kmT[lane, seq, h // 2, :],
                                                  start=True, stop=True)
                        x_.then_inc(s["sc_ps"], 1)
                        if not (last and u):
                            turn(t + 1, 1 - u)
                        pe.wait_ge(s["qc_sb"], t + 1)
                        product(ps_a, u, D_A, D_A).then_inc(s["z_k"], 1)
                        pe.wait_ge(s["rotq_sb"], t + 1)
                        for j in range(HA // 2):
                            x_ = nc.tensor.transpose(ps_c[:, j * P:(j + 1) * P], qkv[:, 0, j * P:(j + 1) * P], ident[:])
                        x_.then_inc(s["qT_ps"], 1)
                        pe.wait_ge(s["vln_sb"], t + 1)
                        ge(pe, s["ob_sb"], t)
                        for gi in range(GB):
                            x_ = nc.tensor.matmul(ps_o[:, D_C + gi * GD:D_C + (gi + 1) * GD], wsT[:, gi, :],
                                                  vln[:, gi * GD:(gi + 1) * GD], start=True, stop=True)
                        x_.then_inc(s["sp_ps"], 1)
                        pe.wait_ge(s["p_sb"], t + 1)
                        if not (last and u):
                            pe.wait_ge(s["lo_sb"], t + 2)
                        for h in range(HC):
                            for c in range(2):
                                x_ = nc.tensor.transpose(ps_x[:, 2 * h + c, :], prob[:, h, c * P:(c + 1) * P], ident[:])
                        x_.then_inc(s["pT_ps"], 1)
                        pe.wait_ge(s["guv"], t + 1)
                        product(ps_b, u, 2 * D_A, D_A).then_inc(s["z_v"], 1)
                        pe.wait_ge(s["pT_a"], t + 1)
                        pe.wait_ge(s["pT_b"], t + 1)
                        ge(pe, s["oc_sb"], t)
                        for h in range(HC):
                            for c in range(2):
                                x_ = nc.tensor.matmul(ps_o[:, h * HD:(h + 1) * HD], probT[:, 2 * h + c, :],
                                                      vm[:, seq, c, h * HD:(h + 1) * HD], start=(c == 0), stop=(c == 1))
                        x_.then_inc(s["pv_ps"], 1)
                loop(pe, body, lambda: turn(0, 0))
                turn_k(NT - 1)


class Pattern:

    def __init__(self, seq, which, dil, before):
        self.seq, self.which, self.dil, self.before = seq, which, dil, before
        self.whole = dil == 16
        sub = SEQS[seq] // dil
        self.per = max(1, P // sub)
        self.blocks = SEQS[seq] // P
        self.pairs = self.blocks // 2
        self.chunks = 1 if self.whole else 2
        self.W = self.chunks * P
        self.next = None

    def mask(self, i, u):
        if self.whole:
            return 3 + self.seq
        at, of = (2 * i + u, self.blocks) if self.dil == 1 else (i // 2, self.pairs // 2)
        return 0 if at == 0 else 2 if at == of - 1 else 1

    def masks(self, i):
        return self.mask(i, 0), self.mask(i, 1), self.mask(min(i + 1, self.pairs - 1), 0)

    def run(self, eng, body, key=lambda i: 0, enter=lambda i: None):
        enter(0)
        body(0, 0, True, False)
        lo = 1
        while lo < self.pairs - 1:
            hi = lo + 1
            while hi < self.pairs - 1 and key(hi) == key(lo):
                hi += 1
            enter(lo)
            if hi - lo == 1:
                body(lo, lo, False, False)
            else:
                with eng.Fori(lo, hi) as i:
                    body(i, lo, False, False)
            lo = hi
        enter(self.pairs - 1)
        body(self.pairs - 1, self.pairs - 1, False, True)

    def after(self, i, like, u, last):
        if u == 0:
            return self, i, like, 1
        if not last:
            return self, i + 1, like + 1, 0
        return (self.next, 0, 0, 0) if self.next else None

    def place(self, i, u):
        if self.dil == 1:
            return (2 * i + u) * P, 0
        if self.whole:
            return 0, (2 * i + u) * self.per
        return i // 2 * P, i % 2 * 2 + u

    def rows(self, dram, i, u, j):
        base = self.seq * SEQS[0]
        v = dram[base:base + SEQS[self.seq], :].rearrange("(n d) c -> n d c", d=self.dil)
        n, r = self.place(i, u)
        return v[bass.ds(n, P // self.per), bass.ds(r + j, 1), :].rearrange("n d c -> n (d c)")

    def values(self, dram, i, u, j):
        base = KV_BASE[self.seq] - PAD
        v = dram[base:base + SEQS[self.seq] + 2 * PAD, :].rearrange("(n d) c -> n d c", d=self.dil)
        n, r = self.place(i, u)
        if self.whole:
            return v[PAD // self.dil:PAD // self.dil + P // self.per, bass.ds(r + j, 1), :]
        v = v[bass.ds(n + PAD // self.dil - 64, 2 * P), bass.ds(r, 1), :]
        return v.rearrange("(c p) d e -> p c (d e)", p=P)

    def queries(self, qT, i, u):
        base = self.seq * SEQS[0]
        v = qT[:, :, base:base + SEQS[self.seq]].rearrange("p j (n d) -> p j n d", d=self.dil)
        n, r = self.place(i, u)
        return v[:, :, bass.ds(n, P // self.per), bass.ds(r, self.per)].rearrange("p j n r -> p j r n")

    def keys(self, kT, i, u):
        base = KV_BASE[self.seq] - PAD
        v = kT[:, base:base + SEQS[self.seq] + 2 * PAD].rearrange("p (n d) -> p n d", d=self.dil)
        n, r = self.place(i, u)
        if self.whole:
            v = v[:, PAD // self.dil:(PAD + SEQS[self.seq]) // self.dil, bass.ds(r, self.per)]
        else:
            v = v[:, bass.ds(n + PAD // self.dil - 64, 2 * P), bass.ds(r, 1)]
        return v.rearrange("p n r -> p r n")


def attend_phase(nc, A):
    U, L = HA // 2, 3
    PIECES = 4
    PT = SEQS[0] // PIECES
    with Phase(nc, "att") as ph:
        ident = ph.sb("ident", [P, P])
        masks = ph.sb("masks", [P, 5, 2 * P])
        qT = ph.sb("qT", [P, U, TOK])
        kT = ph.sb("kT", [P, U, KV_ROWS])
        q = ph.sb("q", [P, 2, U, 2, P])
        v = ph.sb("v", [P, 2, 2, D_A])
        score = ph.sb("score", [P, U, 2, 2 * P])
        prob = ph.sb("prob", [P, U, 2, 2 * P])
        probT = ph.sb("probT", [P, 2, 4, P])
        o = ph.sb("o", [P, 2, O_COLS])
        stats = ph.sb("stats", [P, 2, 2 * HA])
        nmx = ph.sb("nmx", [P, U, 2])
        spare = ph.sb("spare", [P, 1])
        lane = ph.sb("lane", [P, 2])
        carry = ph.sb("carry", [P, 1])
        ps_s = ph.psum("ps_s", [P, U, 2, 2 * P])
        ps_p = ph.psum("ps_p", [P, 2, 4, P])
        ps_o = ph.psum("ps_o", [P, 2, D_A])
        consts, padded, lanes_set = ph.sem("consts"), ph.sem("padded"), ph.sem("lanes_set")
        piece_loaded = [ph.sem(f"piece_loaded{n}") for n in range(PIECES + 1)]
        v_loaded = [ph.sem(f"v_loaded{u}") for u in range(2)]
        o_stored = [ph.sem(f"o_stored{u}") for u in range(2)]
        names = "scored masked nmx_sb p_sb pT_ps pT_sb pv_ps o_sb q_free q_set".split()
        s = {n: ph.sem(n) for n in names}

        patterns = []
        for seq in range(2):
            for which, dil in enumerate((1, 4, 16)):
                patterns.append(Pattern(seq, which, dil, sum(q.blocks for q in patterns)))
        for a, b in zip(patterns, patterns[1:]):
            a.next = b
        BLOCKS = sum(pt.blocks for pt in patterns)

        def heads(j):
            return 2 * j, 2 * j + 1

        def reach(pt, i):
            return (i + 1) // 2 if pt is patterns[0] and i < pt.pairs - 1 else 0

        def await_piece(eng, pt, i):
            if pt is patterns[0] and i < pt.pairs - 1:
                eng.wait_ge(piece_loaded[reach(pt, i)], 32)
            elif i == pt.pairs - 1 and pt.next and pt.next.seq != pt.seq:
                eng.wait_ge(piece_loaded[PIECES], 32)

        def unit_ahead(pt, i, like, u, j, last):
            if j + L < U:
                return pt, i, like, u, j + L
            b = pt.after(i, like, u, last)
            return b and (*b, j + L - U)

        with nc.Block() as block:
            @block.sync
            def _(sp):
                def piece(k_at, q_at, size, done):
                    sp.dma_start(kT[:, :, k_at:k_at + size], A["kT"][:, :, q_at:q_at + size]).then_inc(done, 16)
                    sp.dma_start(qT[:, :, q_at:q_at + size], A["qT"][:, :, q_at:q_at + size]).then_inc(done, 16)

                def load_v(pt, i, u):
                    c = pt.before + 2 * i + u
                    part = P // pt.per
                    ge(sp, s["pv_ps"], U * (c - 1))
                    for j in range(pt.per):
                        at = slice(j * part, (j + 1) * part)
                        sp.dma_start(v[at, u, 0:pt.chunks, :], pt.values(A["v"], i, u, j)).then_inc(v_loaded[u], 32 // pt.per)

                def store(pt, i, u):
                    c = pt.before + 2 * i + u
                    part = P // pt.per
                    sp.wait_ge(s["o_sb"], c + 1)
                    for j in range(pt.per):
                        at = slice(j * part, (j + 1) * part)
                        sp.dma_start(pt.rows(A[f"o{pt.which}"], i, u, j), o[at, u, :]).then_inc(o_stored[u], 32 // pt.per)

                sp.dma_start(ident[:], A["ident"]).then_inc(consts, 16)
                sp.dma_start(masks[:], A["masks"]).then_inc(consts, 16)
                for n in range(PIECES):
                    piece(KV_BASE[0] + n * PT, n * PT, PT, piece_loaded[n])
                    if n == 0:
                        load_v(patterns[0], 0, 0)
                        load_v(patterns[0], 0, 1)
                for pt in patterns:
                    def body(i, like, first, last):
                        for u in range(2):
                            if not (first and u == 0):
                                store(pt, i - 1 + u, 1 - u)
                            nxt = pt.after(i, like, u, last)
                            if nxt and not (pt is patterns[0] and first and u == 0):
                                load_v(nxt[0], nxt[1], nxt[3])
                    pt.run(sp, body)
                    store(pt, pt.pairs - 1, 1)
                    if pt is patterns[0]:
                        piece(KV_BASE[1], SEQS[0], SEQS[1], piece_loaded[PIECES])
                for u in range(2):
                    sp.wait_ge(o_stored[u], 16 * BLOCKS)

            @block.gpsimd
            def _(pool):
                nc.gpsimd.memset(carry[:], 0.0).then_inc(padded, 1)
                nc.gpsimd.memset(lane[:], 0.0).then_inc(lanes_set, 1)
                pool.wait_ge(lanes_set, 1)
                for f in range(2):
                    nc.gpsimd.memset(lane[f * HD:(f + 1) * HD, f:f + 1], 1.0).then_inc(lanes_set, 1)
                    pool.wait_ge(lanes_set, f + 2)
                nc.gpsimd.memset(kT[:, :, 0:PAD], 0.0).then_inc(padded, 1)
                nc.gpsimd.memset(kT[:, :, KV_BASE[0] + SEQS[0]:KV_BASE[1]], 0.0).then_inc(padded, 1)
                nc.gpsimd.memset(kT[:, :, KV_ROWS - PAD:], 0.0).then_inc(padded, 1)

                def copy_q(pt, i, u):
                    c = pt.before + 2 * i + u
                    free = U * (c - 1)
                    if not (isinstance(free, int) and free <= 0):
                        ge(pool, s["q_free"], c - 2)
                        pool.wait_ge(s["scored"], free)
                        nc.gpsimd.tensor_tensor(carry[:], carry[:], carry[:], ALU.add).then_inc(s["q_free"], 1)
                    for f in range(2):
                        one = lane[:, f:f + 1].rearrange("p (a b c) -> p a b c", a=1, b=1).broadcast_to([P, U, pt.per, P // pt.per])
                        x_ = nc.gpsimd.tensor_tensor(q[:, u, :, f, :].rearrange("p j (r n) -> p j r n", r=pt.per),
                                                     pt.queries(qT, i, u), one, ALU.mult)
                    x_.then_inc(s["q_set"], 1)
                pool.wait_ge(padded, 4)
                pool.wait_ge(piece_loaded[0], 32)
                copy_q(patterns[0], 0, 0)
                for pt in patterns:
                    def body(i, like, first, last):
                        for u in range(2):
                            nxt = pt.after(i, like, u, last)
                            if nxt:
                                copy_q(nxt[0], nxt[1], nxt[3])
                    pt.run(pool, body, key=lambda i: reach(pt, i), enter=lambda i: await_piece(pool, pt, i))

            @block.tensor
            def _(pe):
                pe.wait_ge(consts, 32)
                pe.wait_ge(padded, 4)

                def scores(pt, i, u, j):
                    for f, h in enumerate(heads(j)):
                        out = ps_s[:, j, f, 0:pt.W].rearrange("p (r n) -> p r n", r=pt.per)
                        x_ = nc.tensor.matmul(out, q[:, u, j, f, :], pt.keys(kT[:, j, :], i, u),
                                              start=True, stop=True)
                    x_.then_inc(s["scored"], 1)

                def turn_p(pt, n, j, nxt):
                    if nxt and nxt[4] == 0:
                        pe.wait_ge(s["q_set"], nxt[0].before + 2 * nxt[1] + nxt[3] + 1)
                    pe.wait_ge(s["p_sb"], n + 1)
                    for f in range(2):
                        for k in range(pt.chunks):
                            x_ = nc.tensor.transpose(ps_p[:, j % 2, pt.chunks * f + k, :], prob[:, j, f, k * P:(k + 1) * P], ident[:])
                    x_.then_inc(s["pT_ps"], 1)

                def values(pt, c, i, u, j):
                    pe.wait_ge(s["pT_sb"], U * c + j + 1)
                    if j == 0:
                        pe.wait_ge(v_loaded[u], 32 * (pt.before // 2 + i + 1))
                        ge(pe, s["o_sb"], c - 1)
                    for f, h in enumerate(heads(j)):
                        for k in range(pt.chunks):
                            x_ = nc.tensor.matmul(ps_o[:, u, h * HD:(h + 1) * HD], probT[:, j % 2, pt.chunks * f + k, :],
                                                  v[:, u, k, h * HD:(h + 1) * HD], start=(k == 0), stop=(k == pt.chunks - 1))
                    x_.then_inc(s["pv_ps"], 1)

                for pt in patterns:
                    def body(i, like, first, last):
                        for u in range(2):
                            c = pt.before + 2 * i + u
                            for j in range(U):
                                nxt = unit_ahead(pt, i, like, u, j, last)
                                turn_p(pt, U * c + j, j, nxt)
                                if nxt:
                                    scores(nxt[0], nxt[1], nxt[3], nxt[4])
                                values(pt, c, i, u, j)

                    if pt is patterns[0]:
                        pe.wait_ge(piece_loaded[0], 32)
                        pe.wait_ge(s["q_set"], 1)
                        for j in range(L):
                            scores(pt, 0, 0, j)
                    pt.run(pe, body, key=lambda i: reach(pt, i), enter=lambda i: await_piece(pe, pt, i))

            @block.scalar
            def _(act):
                def exps(pt, c, u, j):
                    n = U * c + j
                    act.wait_ge(s["nmx_sb"], n + 1)
                    ge(act, s["pT_ps"], n - U + 1)
                    for f, h in enumerate(heads(j)):
                        x_ = nc.scalar.activation(prob[:, j, f, 0:pt.W], score[:, j, f, 0:pt.W], ACT.Exp, bias=nmx[:, j, f:f + 1],
                                                  scale=SCALE, accum_out=stats[:, u, HA + h:HA + h + 1])
                    x_.then_inc(s["p_sb"], 1)

                def out_o(c, u, n):
                    act.wait_ge(s["pv_ps"], U * (c + 1))
                    ge(act, o_stored[u], 32 * n)
                    nc.scalar.activation(o[:, u, 0:D_A], ps_o[:, u, :], ACT.Copy)
                    nc.scalar.activation(o[:, u, D_A:], stats[:, u, :], ACT.Copy).then_inc(s["o_sb"], 1)

                for pt in patterns:
                    def body(i, like, first, last):
                        for u in range(2):
                            for j in range(U):
                                c = pt.before + 2 * i + u
                                if j == 1 and not (pt is patterns[0] and first and u == 0):
                                    out_o(c - 1, 1 - u, pt.before // 2 + i - 1 + u)
                                nxt = unit_ahead(pt, i, like, u, j, last)
                                if nxt:
                                    exps(nxt[0], nxt[0].before + 2 * nxt[1] + nxt[3], nxt[3], nxt[4])
                    if pt is patterns[0]:
                        for j in range(L):
                            exps(pt, 0, 0, j)
                    pt.run(act, body)
                out_o(BLOCKS - 1, 1, BLOCKS // 2 - 1)

            @block.vector
            def _(dve):
                dve.wait_ge(consts, 32)

                def mask(pt, i, like, u, j):
                    c = pt.before + 2 * i + u
                    n = U * c + j
                    dve.wait_ge(s["scored"], n + 1)
                    ge(dve, s["p_sb"], n - U + 1)
                    if j == 0:
                        ge(dve, s["o_sb"], c - 1)
                    nc.vector.memset(spare[:], 0.0)
                    for f, h in enumerate(heads(j)):
                        x_ = nc.vector.tensor_tensor_reduce(
                            out=score[:, j, f, 0:pt.W], in0=ps_s[:, j, f, 0:pt.W], in1=masks[:, pt.mask(like, u), 0:pt.W], scale=1.0,
                            scalar=-3e38, op0=ALU.add, op1=ALU.max, accum_out=stats[:, u, h:h + 1])
                    x_.then_inc(s["masked"], 1)
                    dve.wait_ge(s["masked"], n + 1)
                    nc.vector.tensor_scalar(nmx[:, j, :], stats[:, u, 2 * j:2 * j + 2], -SCALE, None, ALU.mult)\
                        .then_inc(s["nmx_sb"], 1)

                def out_p(pt, n, j):
                    dve.wait_ge(s["pT_ps"], n + 1)
                    ge(dve, s["pv_ps"], n - 1)
                    nc.vector.tensor_copy(probT[:, j % 2, 0:2 * pt.chunks, :], ps_p[:, j % 2, 0:2 * pt.chunks, :])\
                        .then_inc(s["pT_sb"], 1)

                for pt in patterns:
                    def body(i, like, first, last):
                        for u in range(2):
                            c = pt.before + 2 * i + u
                            for j in range(U):
                                out_p(pt, U * c + j, j)
                                nxt = unit_ahead(pt, i, like, u, j, last)
                                if nxt:
                                    mask(*nxt)
                    if pt is patterns[0]:
                        for j in range(L):
                            mask(pt, 0, 0, 0, j)
                    pt.run(dve, body, key=pt.masks)


def mix_phase(nc, A, affinity):
    with Phase(nc, "mix") as ph:
        ident = ph.sb("ident", [P, P])
        w_hi = ph.sb("w_hi", [P, KC, D], F32R)
        w_lo = ph.sb("w_lo", [P, KC, D], F32R)
        w_r = ph.sb("w_r", [P, KC, NE])
        g = ph.sb("g", [P, KC])
        g_ffn = ph.sb("g_ffn", [P, D])
        consts, g_loaded = ph.sem("consts"), ph.sem("g_loaded")
        with nc.Block() as block:
            @block.sync
            def _(sp):
                sp.dma_start(g[:], A["g_out"]).then_inc(g_loaded, 16)
                sp.dma_start(ident[:], A["ident"]).then_inc(consts, 16)
                sp.dma_start(g_ffn[:], A["g_ffn"]).then_inc(consts, 16)
                sp.dma_start(w_r[:], A["w_router"].rearrange("(k p) e -> p k e", p=P)).then_inc(consts, 16)
                sp.wait_ge(consts, 48)
                sp.wait_ge(g_loaded, 16)
        split_weights(nc, ph, A["w_out"], g, g_loaded, w_hi, w_lo, D)

        o3 = ph.sb("o3", [P, 2, 3, O_COLS])
        obc = ph.sb("obc", [P, 2, D_B + D_C])
        oa = ph.sb("oa", [P, 2, D_A])
        cT_hi = ph.sb("cT_hi", [P, 2, KC, P], F32R)
        cT_lo = ph.sb("cT_lo", [P, 2, KC, P], F32R)
        x = ph.sb("x", [P, 2, D])
        xn = ph.sb("xn", [P, 2, XN_COLS])
        xnT = ph.sb("xnT", [P, KC, P])
        junk = ph.sb("junk", [P, D], BF16)
        stat = ph.sb("stat", [P, 160])
        half = ph.sb("half", [P, 1])
        top, wts, wden = stat[:, 0:8], stat[:, 8:32], stat[:, 32:56]
        tot, rtot, wfin = stat[:, 56:64], stat[:, 64:72], stat[:, 72:96]
        ss_a, ms_a, rs_a = stat[:, 96:97], stat[:, 97:98], stat[:, 98:99]
        ss_y, ms_y, rs_y = stat[:, 100:101], stat[:, 101:102], stat[:, 102:103]
        rmax, rneg, rden, rrec, rexp = stat[:, 104:105], stat[:, 105:106], stat[:, 106:107], stat[:, 107:108], stat[:, 112:128]
        ps_c = ph.psum("ps_c", [P, KC, P])
        ps_y = ph.psum("ps_y", [P, 2, 512])
        ps_n = ph.psum("ps_n", [P, KC, P])
        ps_r = ph.psum("ps_r", [P, 512])
        names = """topped shifted weighted wden_sb tot_sb rtot_sb wfin_sb scaled3 added_a added_b sq_a ms_a rs_a
            oa_out cT_ps hi_sb lo_sb y_a y_b x1_a x1_b sq_y ms_y rs_y xn_sb nT_ps nT_sb r_ps rmax_sb rneg_sb
            rexp_sb rrec_sb aff_a aff_b half_set""".split()
        s = {n: ph.sem(n) for n in names}
        o_loaded = [ph.sem(f"o_loaded{u}") for u in range(2)]
        x_loaded = [ph.sem(f"x_loaded{u}") for u in range(2)]
        y_stored = [ph.sem(f"y_stored{u}") for u in range(2)]
        xn_stored = [ph.sem(f"xn_stored{u}") for u in range(2)]

        def loop(eng, body):
            body(0, True, False)
            with eng.Fori(1, PAIRS - 1) as i:
                body(i, False, False)
            body(PAIRS - 1, False, True)

        with nc.Block() as block:
            @block.sync
            def _(sp):
                def load_o(t, u):
                    ge(sp, s["added_b"], t - 1)
                    ge(sp, s["cT_ps"], t - 1)
                    for j in range(3):
                        sp.dma_start(o3[:, u, j, :], A[f"o{j}"][bass.ds(t * P, P), :]).then_inc(o_loaded[u], 16)
                    sp.dma_start(obc[:, u, :], A["obc"][bass.ds(t * P, P), :]).then_inc(o_loaded[u], 16)

                def load_x(t, u, n):
                    ge(sp, y_stored[u], 16 * n)
                    ge(sp, s["xn_sb"], t - 1)
                    sp.dma_start(x[:, u, :], A["x"][bass.ds(t * P, P), :]).then_inc(x_loaded[u], 16)

                def store(t, u):
                    sp.wait_ge(s["x1_b"], t + 1)
                    sp.dma_start(A["y"][bass.ds(t * P, P), :], x[:, u, :]).then_inc(y_stored[u], 16)
                    sp.wait_ge(s["aff_a"], t + 1)
                    sp.dma_start(A["xn"][bass.ds(t * P, P), :], xn[:, u, :]).then_inc(xn_stored[u], 16)

                def body(i, first, last):
                    for u in range(2):
                        t = 2 * i + u
                        if not last:
                            load_o(t + 2, u)
                        if not (first and u == 0):
                            store(t - 1, 1 - u)
                        if not (last and u):
                            load_x(t + 1, 1 - u, i + u)
                load_o(0, 0)
                load_o(1, 1)
                load_x(0, 0, 0)
                loop(sp, body)
                store(NT - 1, 1)
                for u in range(2):
                    sp.wait_ge(y_stored[u], 16 * PAIRS)
                    sp.wait_ge(xn_stored[u], 16 * PAIRS)

            @block.gpsimd
            def _(pool):
                nc.gpsimd.memset(half[:], -0.5).then_inc(s["half_set"], 1)
                pool.wait_ge(s["half_set"], 1)

                def join(t, u):
                    pool.wait_ge(s["scaled3"], t + 1)
                    ge(pool, s["oa_out"], t)
                    a, b, c = (o3[:, u, j, 0:D_A] for j in range(3))
                    nc.gpsimd.tensor_tensor(a, a, b, ALU.add).then_inc(s["added_a"], 1)
                    pool.wait_ge(s["added_a"], t + 1)
                    ge(pool, s["cT_ps"], t - 1)
                    nc.gpsimd.tensor_tensor(oa[:, u, :], a, c, ALU.add).then_inc(s["added_b"], 1)
                    pool.wait_ge(s["ms_a"], t + 1)
                    nc.gpsimd.tensor_tensor(rs_a, ms_a, half[:], ALU.pow).then_inc(s["rs_a"], 1)

                def norm(t):
                    pool.wait_ge(s["ms_y"], t + 1)
                    ge(pool, s["xn_sb"], t)
                    nc.gpsimd.tensor_tensor(rs_y, ms_y, half[:], ALU.pow).then_inc(s["rs_y"], 1)

                def body(i, first, last):
                    for u in range(2):
                        t = 2 * i + u
                        if not (first and u == 0):
                            norm(t - 1)
                        if not last:
                            join(t + 2, u)
                join(0, 0)
                join(1, 1)
                loop(pool, body)
                norm(NT - 1)

            @block.scalar
            def _(act):
                act.wait_ge(consts, 48)

                def join(t, u):
                    act.wait_ge(s["shifted"], t + 1)
                    nc.scalar.activation(wts, wts, ACT.Exp, scale=SCALE).then_inc(s["weighted"], 1)
                    act.wait_ge(s["added_b"], t + 1)
                    ge(act, s["ms_a"], t)
                    nc.scalar.activation(junk[:, 0:D_A], oa[:, u, :], ACT.Square, accum_out=ss_a).then_inc(s["sq_a"], 1)
                    act.wait_ge(s["rs_a"], t + 1)
                    nc.scalar.activation(oa[:, u, :], oa[:, u, :], ACT.Copy, scale=rs_a).then_inc(s["oa_out"], 1)

                def hi(t, u):
                    act.wait_ge(s["cT_ps"], t + 1)
                    ge(act, s["y_b"], t - 1)
                    nc.scalar.activation(cT_hi[:, u, :, :], ps_c[:], ACT.Copy).then_inc(s["hi_sb"], 1)

                def square(t, u):
                    act.wait_ge(s["x1_b"], t + 1)
                    ge(act, s["ms_y"], t)
                    nc.scalar.activation(junk[:], x[:, u, :], ACT.Square, accum_out=ss_y).then_inc(s["sq_y"], 1)

                def out_n(t):
                    act.wait_ge(s["nT_ps"], t + 1)
                    ge(act, s["r_ps"], t)
                    nc.scalar.activation(xnT[:], ps_n[:], ACT.Copy).then_inc(s["nT_sb"], 1)

                def softmax(t):
                    act.wait_ge(s["rneg_sb"], t + 1)
                    ge(act, s["aff_b"], t)
                    nc.scalar.activation(rexp, ps_r[:, 0:NE], ACT.Exp, bias=rneg, accum_out=rden).then_inc(s["rexp_sb"], 1)

                def body(i, first, last):
                    for u in range(2):
                        t = 2 * i + u
                        past = not (first and u == 0)
                        if past:
                            square(t - 1, 1 - u)
                            out_n(t - 1)
                        if not (last and u):
                            hi(t + 1, 1 - u)
                        if not last:
                            join(t + 2, u)
                        if past:
                            softmax(t - 1)
                join(0, 0)
                hi(0, 0)
                join(1, 1)
                loop(act, body)
                square(NT - 1, 1)
                out_n(NT - 1)
                softmax(NT - 1)

            @block.vector
            def _(dve):
                dve.wait_ge(consts, 48)

                def heads(ap):
                    return ap.rearrange("p (j h) -> p j h", j=3)

                def over(ap):
                    return ap.rearrange("p (one h) -> p one h", one=1).broadcast_to([P, 3, HA])

                def join(t, u, n):
                    dve.wait_ge(o_loaded[u], 64 * n)
                    mj = o3[:, u, :, D_A:D_A + HA]
                    nc.vector.tensor_reduce(top, mj.rearrange("p j h -> p h j"), AX_X, ALU.max).then_inc(s["topped"], 1)
                    dve.wait_ge(s["topped"], t + 1)
                    ge(dve, s["wfin_sb"], t)
                    nc.vector.tensor_tensor(heads(wts), mj, over(top), ALU.subtract).then_inc(s["shifted"], 1)
                    dve.wait_ge(s["weighted"], t + 1)
                    nc.vector.tensor_tensor(heads(wden), heads(wts), o3[:, u, :, D_A + HA:], ALU.mult).then_inc(s["wden_sb"], 1)
                    dve.wait_ge(s["wden_sb"], t + 1)
                    nc.vector.tensor_reduce(tot, wden.rearrange("p (j h) -> p h j", j=3), AX_X, ALU.add).then_inc(s["tot_sb"], 1)
                    dve.wait_ge(s["tot_sb"], t + 1)
                    nc.vector.reciprocal(rtot, tot).then_inc(s["rtot_sb"], 1)
                    dve.wait_ge(s["rtot_sb"], t + 1)
                    nc.vector.tensor_tensor(heads(wfin), heads(wts), over(rtot), ALU.mult).then_inc(s["wfin_sb"], 1)
                    dve.wait_ge(s["wfin_sb"], t + 1)
                    for j in range(3):
                        v = o3[:, u, j, 0:D_A].rearrange("p (h c) -> p h c", h=HA)
                        by = wfin[:, j * HA:(j + 1) * HA].rearrange("p (h one) -> p h one", one=1).broadcast_to([P, HA, HD])
                        x_ = nc.vector.tensor_tensor(v, v, by, ALU.mult)
                    x_.then_inc(s["scaled3"], 1)
                    dve.wait_ge(s["sq_a"], t + 1)
                    ge(dve, s["oa_out"], t)
                    nc.vector.tensor_scalar(ms_a, ss_a, 1.0 / D_A, EPS, ALU.mult, ALU.add).then_inc(s["ms_a"], 1)

                def lo(t, u):
                    dve.wait_ge(s["hi_sb"], t + 1)
                    nc.vector.tensor_tensor(cT_lo[:, u, :, :], ps_c[:], cT_hi[:, u, :, :].bitcast(F32), ALU.subtract)\
                        .then_inc(s["lo_sb"], 1)

                def add_x(t, u, j, n):
                    if j == 0:
                        dve.wait_ge(x_loaded[u], 16 * n)
                    c = slice(j * 512, (j + 1) * 512)
                    dve.wait_ge(s["y_b" if j else "y_a"], t + 1)
                    nc.vector.tensor_tensor(x[:, u, c], x[:, u, c], ps_y[:, j, :], ALU.add).then_inc(s["x1_b" if j else "x1_a"], 1)

                def norm(t, u, n):
                    dve.wait_ge(s["sq_y"], t + 1)
                    ge(dve, s["rs_y"], t)
                    nc.vector.tensor_scalar(ms_y, ss_y, 1.0 / D, EPS, ALU.mult, ALU.add).then_inc(s["ms_y"], 1)
                    dve.wait_ge(s["rs_y"], t + 1)
                    ge(dve, xn_stored[u], 16 * n)
                    ge(dve, s["nT_ps"], t - 1)
                    nc.vector.scalar_tensor_tensor(out=xn[:, u, 0:D], in0=x[:, u, :], scalar=rs_y, in1=g_ffn[:],
                                                   op0=ALU.mult, op1=ALU.mult).then_inc(s["xn_sb"], 1)

                def softmax(t, u):
                    dve.wait_ge(s["r_ps"], t + 1)
                    nc.vector.tensor_reduce(rmax, ps_r[:, 0:NE], AX_X, ALU.max).then_inc(s["rmax_sb"], 1)
                    dve.wait_ge(s["rmax_sb"], t + 1)
                    ge(dve, s["rexp_sb"], t)
                    nc.vector.tensor_scalar(rneg, rmax, -1.0, None, ALU.mult).then_inc(s["rneg_sb"], 1)
                    dve.wait_ge(s["rexp_sb"], t + 1)
                    nc.vector.reciprocal(rrec, rden).then_inc(s["rrec_sb"], 1)
                    dve.wait_ge(s["rrec_sb"], t + 1)
                    nc.vector.tensor_scalar(xn[:, u, D:], rexp, rrec, None, ALU.mult).then_inc(s["aff_a"], 1)
                    nc.vector.tensor_scalar(affinity[:, bass.ds(t * NE, NE)], rexp, rrec, None, ALU.mult).then_inc(s["aff_b"], 1)

                def body(i, first, last):
                    for u in range(2):
                        t = 2 * i + u
                        past = not (first and u == 0)
                        if past:
                            add_x(t - 1, 1 - u, 1, None)
                            norm(t - 1, 1 - u, i - 1 + u)
                        add_x(t, u, 0, i + 1)
                        if not (last and u):
                            lo(t + 1, 1 - u)
                        if not last:
                            join(t + 2, u, i + 2)
                        if past:
                            softmax(t - 1, 1 - u)
                join(0, 0, 1)
                lo(0, 0)
                join(1, 1, 1)
                loop(dve, body)
                add_x(NT - 1, 1, 1, None)
                norm(NT - 1, 1, PAIRS - 1)
                softmax(NT - 1, 1)

            @block.tensor
            def _(pe):
                pe.wait_ge(consts, 48)

                def turn(t, u):
                    pe.wait_ge(s["oa_out"], t + 1)
                    ge(pe, s["lo_sb"], t)
                    for k in range(KC):
                        src = oa[:, u, k * P:(k + 1) * P] if k < 4 else obc[:, u, (k - 4) * P:(k - 3) * P]
                        x_ = nc.tensor.transpose(ps_c[:, k, :], src, ident[:])
                    x_.then_inc(s["cT_ps"], 1)

                def turn_n(t, u):
                    pe.wait_ge(s["xn_sb"], t + 1)
                    ge(pe, s["nT_sb"], t)
                    for k in range(KC):
                        x_ = nc.tensor.transpose(ps_n[:, k, :], xn[:, u, k * P:(k + 1) * P], ident[:])
                    x_.then_inc(s["nT_ps"], 1)

                def product(t, u, j):
                    ge(pe, s["x1_b" if j else "x1_a"], t)
                    n = 0
                    for k in range(KC):
                        for a, b in ((cT_lo, w_hi), (cT_hi, w_lo), (cT_hi, w_hi)):
                            x_ = nc.tensor.matmul(ps_y[:, j, :], a[:, u, k, :], b[:, k, j * 512:(j + 1) * 512],
                                                  start=(n == 0), stop=(n == 3 * KC - 1))
                            n += 1
                    x_.then_inc(s["y_b" if j else "y_a"], 1)

                def route(t):
                    pe.wait_ge(s["nT_sb"], t + 1)
                    ge(pe, s["rexp_sb"], t)
                    for k in range(KC):
                        x_ = nc.tensor.matmul(ps_r[:, 0:NE], xnT[:, k, :], w_r[:, k, :], start=(k == 0), stop=(k == KC - 1))
                    x_.then_inc(s["r_ps"], 1)

                def body(i, first, last):
                    for u in range(2):
                        t = 2 * i + u
                        past = not (first and u == 0)
                        pe.wait_ge(s["lo_sb"], t + 1)
                        product(t, u, 0)
                        if past:
                            turn_n(t - 1, 1 - u)
                        if not (last and u):
                            turn(t + 1, 1 - u)
                        product(t, u, 1)
                        if past:
                            route(t - 1)
                turn(0, 0)
                loop(pe, body)
                turn_n(NT - 1, 1)
                route(NT - 1)


def choose_phase(nc, A, affinity, slots):
    with Phase(nc, "top") as ph:
        load = ph.sb("load", [P, P + 2 * NT + CAPS[0]])
        bits = ph.sb("bits", [P, BITS], I32)
        ones = ph.sb("ones", [P, P], BF16)
        tri = ph.sb("tri", [P, P], BF16)
        ids = ph.sb("ids", [P, 2 * NT], BF16)
        slot_row = ph.sb("slot_row", [P, CAPS[0]], BF16)
        caps = ph.sb("caps", [P, 2, NE])
        thr = ph.sb("thr", [P, 2, NE], I32)
        cand = ph.sb("cand", [P, 2, NE], I32)
        kept = ph.sb("kept", [P, 2, NE], I32)
        hits = ph.sb("hits", [P, NT, NE], BF16)
        ties = ph.sb("ties", [P, NT, NE], BF16)
        chosen = ph.sb("chosen", [P, NT, NE], BF16)
        need = ph.sb("need", [P, 2, NE])
        before = ph.sb("before", [P, NT, NE])
        rank = ph.sb("rank", [P, NT, NE])
        slot = ph.sb("slot", [P, NT * NE])
        R = 8
        onehot = ph.sb("onehot", [P, R, CAPS[0]], BF16)
        ps_n = ph.psum("ps_n", [P, 2, 256])
        ps_w = ph.psum("ps_w", [P, 512])
        ps_s = ph.psum("ps_s", [P, 512])
        ps_i = [ph.psum(f"ps_i{j}", [P, 512]) for j in range(ST)]
        names = """loaded made cand_set hit counted kept_set thr_set gt eq n_gt pre_ps need_sb run rank_sb ok tied sel
            sel_ps slot_sb oh_set oh_used lists""".split()
        s = {n: ph.sem(n) for n in names}
        MADE = 8
        tiles = (slice(0, NTP), slice(NTP, NT))

        def per_tile(ap, seq):
            n = tiles[seq].stop - tiles[seq].start
            return ap[:, seq:seq + 1, :].broadcast_to([P, n, NE])

        with nc.Block() as block:
            @block.sync
            def _(sp):
                sp.dma_start(load[:, 0:P], A["tri"]).then_inc(s["loaded"], 16)
                sp.dma_start(load[:, P:P + 2 * NT], A["ids"]).then_inc(s["loaded"], 16)
                sp.dma_start(load[:, P + 2 * NT:], A["slot_row"]).then_inc(s["loaded"], 16)
                sp.dma_start(bits[:].bitcast(F32), A["bits"]).then_inc(s["loaded"], 16)

            @block.tensor
            def _(pe):
                pe.wait_ge(s["made"], MADE)

                def count(what):
                    for seq in range(2):
                        t0, t1 = tiles[seq].start, tiles[seq].stop
                        for t in range(t0, t1):
                            x_ = nc.tensor.matmul(ps_n[:, seq, 0:NE], ones[:], what[:, t, :], start=(t == t0), stop=(t == t1 - 1))
                    return x_

                def prefix(what, done):
                    nc.tensor.matmul(ps_w[:, 0:NT * NE], tri[:], what[:].rearrange("p t e -> p (t e)"), start=True, stop=True)
                    nc.tensor.matmul(ps_s[:, 0:NT * NE], ones[:], what[:].rearrange("p t e -> p (t e)"), start=True, stop=True)\
                        .then_inc(done, 1)
                with pe.Fori(0, BITS) as b:
                    pe.wait_ge(s["hit"], b + 1)
                    count(hits).then_inc(s["counted"], 1)
                pe.wait_ge(s["gt"], 1)
                count(hits).then_inc(s["n_gt"], 1)
                pe.wait_ge(s["eq"], 1)
                prefix(ties, s["pre_ps"])
                pe.wait_ge(s["sel"], 1)
                prefix(chosen, s["sel_ps"])
                with pe.Fori(0, NE) as e:
                    for t in range(NT):
                        seq = int(t >= NTP)
                        pe.wait_ge(s["oh_set"], e * NT + t + 1)
                        for j in range(CAPS[seq] // P):
                            x_ = nc.tensor.matmul(ps_i[2 * seq + j][:, bass.ds(2 * e, 2)], onehot[:, t % R, j * P:(j + 1) * P],
                                                  ids[:, 2 * t:2 * t + 2], start=(t in (0, NTP)), stop=(t in (NTP - 1, NT - 1)))
                        x_.then_inc(s["oh_used"], 1)

            @block.vector
            def _(dve):
                nc.vector.memset(ones[:], 1.0).then_inc(s["made"], 1)
                nc.vector.memset(thr[:], 0).then_inc(s["made"], 1)
                for seq in range(2):
                    nc.vector.memset(caps[:, seq, :], float(CAPS[seq])).then_inc(s["made"], 1)
                    nc.vector.memset(before[:, tiles[seq].start, :], 0.0).then_inc(s["made"], 1)
                dve.wait_ge(s["loaded"], 64)
                nc.vector.tensor_copy(tri[:], load[:, 0:P])
                nc.vector.tensor_copy(ids[:], load[:, P:P + 2 * NT]).then_inc(s["made"], 1)
                nc.vector.tensor_copy(slot_row[:], load[:, P + 2 * NT:]).then_inc(s["made"], 1)
                dve.wait_ge(s["made"], MADE)
                aff = affinity[:].rearrange("p (t e) -> p t e", e=NE)

                def compare(out, op, level):
                    for seq in range(2):
                        x_ = nc.vector.tensor_tensor(out[:, tiles[seq], :], aff[:, tiles[seq], :], per_tile(level, seq), op)
                    return x_

                def halve(b):
                    ge(dve, s["thr_set"], b)
                    nc.vector.tensor_tensor(cand[:].rearrange("p s e -> p (s e)"), thr[:].rearrange("p s e -> p (s e)"),
                                            bits[:, bass.ds(b, 1)].broadcast_to([P, 2 * NE]), ALU.bitwise_or).then_inc(s["cand_set"], 1)
                    dve.wait_ge(s["cand_set"], b + 1)
                    ge(dve, s["counted"], b)
                    compare(hits, ALU.is_ge, cand[:].bitcast(F32)).then_inc(s["hit"], 1)
                    dve.wait_ge(s["counted"], b + 1)
                    nc.vector.tensor_tensor(kept[:], ps_n[:, :, 0:NE], caps[:], ALU.is_ge).then_inc(s["kept_set"], 1)
                    dve.wait_ge(s["kept_set"], b + 1)
                    nc.vector.memset(slot[:, 0:1], 0.0)
                    nc.vector.copy_predicated(thr[:], kept[:], cand[:]).then_inc(s["thr_set"], 1)
                halve(0)
                with dve.Fori(1, BITS) as b:
                    halve(b)

                dve.wait_ge(s["thr_set"], BITS)
                compare(hits, ALU.is_gt, thr[:].bitcast(F32)).then_inc(s["gt"], 1)
                compare(ties, ALU.is_equal, thr[:].bitcast(F32)).then_inc(s["eq"], 1)
                dve.wait_ge(s["n_gt"], 1)
                nc.vector.tensor_tensor(need[:], caps[:], ps_n[:, :, 0:NE], ALU.subtract).then_inc(s["need_sb"], 1)
                runs = [0]

                def ranks(done):
                    dve.wait_ge(done, 1)
                    for t in range(1, NT):
                        if t == NTP:
                            continue
                        if runs[0]:
                            dve.wait_ge(s["run"], runs[0])
                        nc.vector.tensor_tensor(before[:, t, :], before[:, t - 1, :], ps_s[:, (t - 1) * NE:t * NE], ALU.add)\
                            .then_inc(s["run"], 1)
                        runs[0] += 1
                    dve.wait_ge(s["run"], runs[0])
                    nc.vector.tensor_tensor(rank[:].rearrange("p t e -> p (t e)"), before[:].rearrange("p t e -> p (t e)"),
                                            ps_w[:, 0:NT * NE], ALU.add).then_inc(s["rank_sb"], 1)

                ranks(s["pre_ps"])
                dve.wait_ge(s["rank_sb"], 1)
                dve.wait_ge(s["need_sb"], 1)
                for seq in range(2):
                    nc.vector.tensor_tensor(rank[:, tiles[seq], :], rank[:, tiles[seq], :], per_tile(need, seq), ALU.is_le)\
                        .then_inc(s["ok"], 1)
                dve.wait_ge(s["ok"], 2)
                nc.vector.tensor_tensor(rank[:], rank[:], ties[:], ALU.mult).then_inc(s["tied"], 1)
                dve.wait_ge(s["tied"], 1)
                nc.vector.tensor_tensor(chosen[:], rank[:], hits[:], ALU.add).then_inc(s["sel"], 1)
                ranks(s["sel_ps"])
                dve.wait_ge(s["rank_sb"], 2)
                nc.vector.tensor_tensor(slot[:].rearrange("p (t e) -> p t e", e=NE), rank[:], chosen[:], ALU.mult)\
                    .then_inc(s["slot_sb"], 1)
                dve.wait_ge(s["slot_sb"], 1)

                def set_onehot(e, t):
                    w = CAPS[int(t >= NTP)]
                    nc.vector.tensor_scalar(onehot[:, t % R, 0:w], slot_row[:, 0:w], slot[:, bass.ds(e + t * NE, 1)], None,
                                            ALU.is_equal).then_inc(s["oh_set"], 1)
                for t in range(R):
                    set_onehot(0, t)
                with dve.Fori(0, NE - 1) as e:
                    for t in range(R, NT + R):
                        dve.wait_ge(s["oh_used"], e * NT + t - R + 1)
                        set_onehot(e + t // NT, t % NT)
                for t in range(R, NT):
                    dve.wait_ge(s["oh_used"], (NE - 1) * NT + t - R + 1)
                    set_onehot(NE - 1, t)
                dve.wait_ge(s["oh_used"], NE * NT)
                for j in range(ST):
                    v = ps_i[j][:, 0:2 * NE].rearrange("p (e c) -> p e c", c=2)
                    nc.vector.tensor_copy(rank[:, 0:2, :].rearrange("p t e -> p (t e)"), ps_i[j][:, 0:2 * NE])\
                        .then_inc(s["lists"], 1)
                    dve.wait_ge(s["lists"], 2 * j + 1)
                    v = rank[:, 0:2, :].rearrange("p t e -> p (t e)").rearrange("p (e c) -> p e c", c=2)
                    nc.vector.scalar_tensor_tensor(out=slots[:, j, :], in0=v[:, :, 0], scalar=float(P), in1=v[:, :, 1],
                                                   op0=ALU.mult, op1=ALU.add).then_inc(s["lists"], 1)
                    dve.wait_ge(s["lists"], 2 * j + 2)


def expert_phase(nc, A, slots):
    S = ST * P
    UC = 256
    NU = D // UC
    UNITS = [(w, j) for j in range(NU) for w in ("w_gate", "w_up")] + [("w_down", j) for j in range(NU)]
    M = len(UNITS)
    RS, RW = 4, 3
    ROUNDS = 2 * ST
    assert M % RS == 0 and M % RW == 0
    with Phase(nc, "exp") as ph:
        ident = ph.sb("ident", [P, P])
        stage = ph.sb("stage", [P, RS, KC, UC])
        w_hi = ph.sb("w_hi", [P, RW, KC, UC], F32R)
        w_lo = ph.sb("w_lo", [P, RW, KC, UC], F32R)
        xe = ph.sb("xe", [P, 2, ST, XN_COLS])
        xT_hi = ph.sb("xT_hi", [P, KC, S], F32R)
        xT_lo = ph.sb("xT_lo", [P, KC, S], F32R)
        hT_hi = ph.sb("hT_hi", [P, KC, S], F32R)
        hT_lo = ph.sb("hT_lo", [P, KC, S], F32R)
        act_g = ph.sb("act_g", [P, 2, S])
        hid = ph.sb("hid", [P, 2, S])
        ye = ph.sb("ye", [P, ST, D])
        gates = ph.sb("gates", [P, 2, ST])
        ps_g = ph.psum("ps_g", [P, 2, 512])
        ps_u = ph.psum("ps_u", [P, 2, 512])
        ps_d = ph.psum("ps_d", [P, ST, 512])
        ps_t = ph.psum("ps_t", [P, 4, P])
        down_banks = [[ps_d[:, q, :] for q in range(ST)], [ps_g[:, 0, :], ps_g[:, 1, :], ps_u[:, 0, :]]]
        down_banks += [down_banks[0], [ps_u[:, 0, :], ps_u[:, 1, :], ps_t[:].rearrange("p a b -> p (a b)")]]
        consts = ph.sem("consts")
        loaded = [ph.sem(f"loaded{r}") for r in range(RS)]
        gathered = [ph.sem(f"gathered{u}") for u in range(2)]
        names = "w_hi_sb w_lo_sb unit_done xT_ps xT_hi_sb xT_lo_sb act_sb hid_sb h_hi_sb h_lo_sb scattered gate_sb y_out".split()
        s = {n: ph.sem(n) for n in names}

        def loop(eng, body):
            body(0, False)
            with eng.Fori(1, NE // 2 - 1) as i:
                body(i, False)
            body(NE // 2 - 1, True)

        AFTER = {8: (0, 1), 9: (2, 3), 10: (4, 5), 11: ()}

        def ahead(e, m, by, more):
            if m + by < M:
                return e, m + by
            return (e + 1, m + by - M) if more else None

        with nc.Block() as block:
            @block.sync
            def _(sp):
                sp.dma_start(ident[:], A["ident"]).then_inc(consts, 16)

                def load(e, m):
                    w, j = UNITS[m]
                    for half in (1, 0):
                        k = half * KC // 2
                        src = A[w][bass.ds(e, 1), k * P:k * P + D // 2, j * UC:(j + 1) * UC]
                        sp.dma_start(stage[:, m % RS, k:k + KC // 2, :], src.rearrange("o (k p) c -> p (o k) c", p=P))\
                            .then_inc(loaded[m % RS], 16)
                for m in range(RS):
                    load(0, m)

                def body(i, last):
                    for u in range(2):
                        e = 2 * i + u
                        for m in range(M):
                            nxt = ahead(e, m, RS, not (last and u))
                            if nxt:
                                sp.wait_ge(s["w_lo_sb"], e * M + m + 1)
                                load(*nxt)
                loop(sp, body)

            @block.gpsimd
            def _(pool):
                def gather(e):
                    for j in range(ST):
                        nc.gpsimd.indirect_dma_start(xe[:, e % 2, j, :], None, A["xn"],
                                                     bass.IndirectOffsetOnAxis(ap=slots[:, j, e:e + 1], axis=0))\
                            .then_inc(gathered[e % 2], 16)
                def gate(e):
                    pool.wait_ge(gathered[e % 2], 16 * ST * (e // 2 + 1))
                    nc.gpsimd.tensor_copy(gates[:, e % 2, :], xe[:, e % 2, :, D + e]).then_inc(s["gate_sb"], 1)
                gather(0)
                gather(1)
                gate(0)
                gate(1)
                for e in range(NE):
                    pool.wait_ge(s["y_out"], (e + 1) * NU)
                    if e:
                        pool.wait_ge(s["scattered"], 16 * ST * e)
                    for j in range(ST):
                        nc.gpsimd.indirect_dma_start(A["y"], bass.IndirectOffsetOnAxis(ap=slots[:, j, e:e + 1], axis=0),
                                                     ye[:, j, :], None, compute_op=ALU.add).then_inc(s["scattered"], 16)
                    if e + 2 < NE:
                        pool.wait_ge(s["xT_lo_sb"], ROUNDS * (e + 1))
                        pool.wait_ge(s["gate_sb"], e + 1)
                        gather(e + 2)
                        gate(e + 2)
                pool.wait_ge(s["scattered"], 16 * ST * NE)

            @block.scalar
            def _(act):
                def split(e, m):
                    act.wait_ge(loaded[m % RS], 32 * (e * (M // RS) + m // RS + 1))
                    nc.scalar.activation(w_hi[:, m % RW, :, :], stage[:, m % RS, :, :], ACT.Copy).then_inc(s["w_hi_sb"], 1)

                def hi_x(e, r):
                    act.wait_ge(s["xT_ps"], e * ROUNDS + r + 1)
                    j, k = r // 2, r % 2 * 4
                    nc.scalar.activation(xT_hi[:, k:k + 4, j * P:(j + 1) * P], ps_t[:], ACT.Copy).then_inc(s["xT_hi_sb"], 1)

                def body(i, last):
                    for u in range(2):
                        e = 2 * i + u
                        more = not (last and u)
                        for m, (w, j) in enumerate(UNITS):
                            nxt = ahead(e, m, RW - 1, more)
                            if nxt:
                                ge(act, s["unit_done"], e * M + m)
                                split(*nxt)
                            if w == "w_gate":
                                act.wait_ge(s["unit_done"], e * M + m + 1)
                                ge(act, s["hid_sb"], e * NU + j)
                                nc.scalar.activation(act_g[:], ps_g[:, :, 0:S], ACT.Silu).then_inc(s["act_sb"], 1)
                            elif w == "w_up":
                                act.wait_ge(s["hid_sb"], e * NU + j + 1)
                                nc.scalar.activation(hT_hi[:, 2 * j:2 * j + 2, :], hid[:], ACT.Copy).then_inc(s["h_hi_sb"], 1)
                            else:
                                act.wait_ge(s["unit_done"], e * M + m + 1)
                                ge(act, s["scattered"], 16 * ST * e)
                                if j == 0:
                                    act.wait_ge(s["gate_sb"], e + 1)
                                for q in range(ST):
                                    x_ = nc.scalar.activation(ye[:, q, j * UC:(j + 1) * UC], down_banks[j][q][:, 0:UC], ACT.Copy,
                                                              scale=gates[:, u, q:q + 1])
                                x_.then_inc(s["y_out"], 1)
                                if more:
                                    for r in AFTER[m]:
                                        hi_x(e + 1, r)
                for m in range(RW - 1):
                    split(0, m)
                for r in range(ROUNDS):
                    hi_x(0, r)
                loop(act, body)

            @block.vector
            def _(dve):
                def split(e, m):
                    dve.wait_ge(s["w_hi_sb"], e * M + m + 1)
                    nc.vector.tensor_tensor(w_lo[:, m % RW, :, :], stage[:, m % RS, :, :], w_hi[:, m % RW, :, :].bitcast(F32),
                                            ALU.subtract).then_inc(s["w_lo_sb"], 1)

                def lo_x(e, r):
                    dve.wait_ge(s["xT_hi_sb"], e * ROUNDS + r + 1)
                    j, k = r // 2, r % 2 * 4
                    to = (slice(None), slice(k, k + 4), slice(j * P, (j + 1) * P))
                    nc.vector.tensor_tensor(xT_lo[to], ps_t[:], xT_hi[to].bitcast(F32), ALU.subtract).then_inc(s["xT_lo_sb"], 1)

                def body(i, last):
                    for u in range(2):
                        e = 2 * i + u
                        more = not (last and u)
                        for m, (w, j) in enumerate(UNITS):
                            nxt = ahead(e, m, RW - 1, more)
                            if nxt:
                                split(*nxt)
                            if w == "w_up":
                                dve.wait_ge(s["act_sb"], e * NU + j + 1)
                                dve.wait_ge(s["unit_done"], e * M + m + 1)
                                ge(dve, s["h_lo_sb"], e * NU + j)
                                nc.vector.tensor_tensor(hid[:], act_g[:], ps_u[:, :, 0:S], ALU.mult).then_inc(s["hid_sb"], 1)
                                dve.wait_ge(s["h_hi_sb"], e * NU + j + 1)
                                nc.vector.tensor_tensor(hT_lo[:, 2 * j:2 * j + 2, :], hid[:], hT_hi[:, 2 * j:2 * j + 2, :].bitcast(F32),
                                                        ALU.subtract).then_inc(s["h_lo_sb"], 1)
                            elif w == "w_down" and more:
                                for r in AFTER[m]:
                                    lo_x(e + 1, r)
                for m in range(RW - 1):
                    split(0, m)
                for r in range(ROUNDS):
                    lo_x(0, r)
                loop(dve, body)

            @block.tensor
            def _(pe):
                pe.wait_ge(consts, 16)

                def turn(e, u, n, r):
                    if r == 0:
                        pe.wait_ge(gathered[u], 16 * ST * n)
                    ge(pe, s["xT_lo_sb"], e * ROUNDS + r)
                    j, k0 = r // 2, r % 2 * 4
                    for k in range(4):
                        x_ = nc.tensor.transpose(ps_t[:, k, :], xe[:, u, j, (k0 + k) * P:(k0 + k + 1) * P], ident[:])
                    x_.then_inc(s["xT_ps"], 1)

                def passes(slot, hi, lo):
                    return ((w_lo, hi), (w_hi, lo), (w_hi, hi))

                def body(i, last):
                    for u in range(2):
                        e = 2 * i + u
                        more = not (last and u)
                        for m, (w, j) in enumerate(UNITS):
                            pe.wait_ge(s["w_lo_sb"], e * M + m + 1)
                            if m == 0:
                                pe.wait_ge(s["xT_lo_sb"], ROUNDS * (e + 1))
                            if w != "w_down":
                                ps, free = (ps_g, "act_sb") if w == "w_gate" else (ps_u, "hid_sb")
                                ge(pe, s[free], e * NU + j)
                                if m == 1:
                                    ge(pe, s["y_out"], e * NU)
                                for f in range(2):
                                    n = 0
                                    for k in range(KC):
                                        for a, b in passes(m % RW, xT_hi, xT_lo):
                                            x_ = nc.tensor.matmul(ps[:, f, 0:S], a[:, m % RW, k, f * P:(f + 1) * P], b[:, k, :],
                                                                  start=(n == 0), stop=(n == 3 * KC - 1))
                                            n += 1
                            else:
                                if j == 0:
                                    ge(pe, s["y_out"], e * NU)
                                elif j == 1:
                                    pe.wait_ge(s["act_sb"], (e + 1) * NU)
                                    pe.wait_ge(s["hid_sb"], (e + 1) * NU)
                                else:
                                    pe.wait_ge(s["y_out"], e * NU + j - 1)
                                if j == NU - 1 and more:
                                    pe.wait_ge(s["xT_lo_sb"], ROUNDS * (e + 2))
                                for k in range(KC):
                                    if j == 0 and k % 2 == 0:
                                        pe.wait_ge(s["h_lo_sb"], e * NU + k // 2 + 1)
                                    for q in range(ST):
                                        rows = slice(q * P, (q + 1) * P)
                                        for n, (a, b) in enumerate(passes(m % RW, hT_hi, hT_lo)):
                                            x_ = nc.tensor.matmul(down_banks[j][q][:, 0:UC], b[:, k, rows], a[:, m % RW, k, :],
                                                                  start=(k == 0 and n == 0), stop=(k == KC - 1 and n == 2))
                            x_.then_inc(s["unit_done"], 1)
                            if w == "w_down" and more:
                                for r in AFTER[m]:
                                    turn(e + 1, 1 - u, i + 1 + u, r)
                for r in range(ROUNDS):
                    turn(0, 0, 1, r)
                loop(pe, body)


def final_phase(nc, A):
    R = 4
    with Phase(nc, "fin") as ph:
        g = ph.sb("g", [P, D])
        y = ph.sb("y", [P, R, D])
        out = ph.sb("out", [P, R, D])
        stat = ph.sb("stat", [P, R, 4])
        half = ph.sb("half", [P, 1])
        g_loaded, half_set = ph.sem("g_loaded"), ph.sem("half_set")
        loaded = [ph.sem(f"loaded{r}") for r in range(R)]
        stored = [ph.sem(f"stored{r}") for r in range(R)]
        squared, meaned, powered, normed = (ph.sem(n) for n in ("squared", "meaned", "powered", "normed"))
        with nc.Block() as block:
            @block.sync
            def _(sp):
                sp.dma_start(g[:], A["g_final"]).then_inc(g_loaded, 16)
                for r in range(R):
                    sp.dma_start(y[:, r, :], A["y"][r * P:(r + 1) * P, :]).then_inc(loaded[r], 16)
                with sp.Fori(0, NT // R - 1) as i:
                    for r in range(R):
                        t = R * i + r
                        row = sp.snap((t + R) * P)
                        sp.wait_ge(normed, t + 1)
                        sp.dma_start(y[:, r, :], A["y"][bass.ds(row, P), :]).then_inc(loaded[r], 16)

            @block.scalar
            def _(act):
                def tiles_of(i):
                    for r in range(R):
                        t = R * i + r
                        act.wait_ge(loaded[r], 16 * (i + 1))
                        ge(act, stored[r], 16 * i)
                        nc.scalar.activation(out[:, r, :], y[:, r, :], ACT.Square, accum_out=stat[:, r, 0:1]).then_inc(squared, 1)
                tiles_of(0)
                with act.Fori(1, NT // R) as i:
                    tiles_of(i)

            @block.gpsimd
            def _(pool):
                nc.gpsimd.memset(half[:], -0.5).then_inc(half_set, 1)
                pool.wait_ge(half_set, 1)
                with pool.Fori(0, NT // R) as i:
                    for r in range(R):
                        t = R * i + r
                        pool.wait_ge(meaned, t + 1)
                        nc.gpsimd.tensor_tensor(stat[:, r, 2:3], stat[:, r, 1:2], half[:], ALU.pow).then_inc(powered, 1)
                        pool.wait_ge(normed, t + 1)
                        nc.gpsimd.dma_start(A["out"][bass.ds(t * P, P), :], out[:, r, :]).then_inc(stored[r], 16)
                for r in range(R):
                    pool.wait_ge(stored[r], 16 * (NT // R))

            @block.vector
            def _(dve):
                dve.wait_ge(g_loaded, 16)
                with dve.Fori(0, NT // R) as i:
                    for r in range(R):
                        t = R * i + r
                        dve.wait_ge(squared, t + 1)
                        nc.vector.tensor_scalar(stat[:, r, 1:2], stat[:, r, 0:1], 1.0 / D, EPS, ALU.mult, ALU.add).then_inc(meaned, 1)
                        dve.wait_ge(powered, t + 1)
                        nc.vector.scalar_tensor_tensor(out=out[:, r, :], in0=y[:, r, :], scalar=stat[:, r, 2:3], in1=g[:],
                                                       op0=ALU.mult, op1=ALU.mult).then_inc(normed, 1)


DRAM_IN = dict(x=(TOK, D), mem=(2 * MEM, D), w_in=(D, D_IN), w_mem_kv=(D, 2 * D_C), w_out=(D, D), w_router=(D, NE),
               w_gate=(NE, D, D), w_up=(NE, D, D), w_down=(NE, D, D), g_mix=(P, KC), g_mem=(P, KC), g_out=(P, KC),
               w_sT=(P, GB, P), b_sT=(P, GB), ln_g=(P, D_B), ln_b=(P, D_B), g_ffn=(P, D), g_final=(P, D),
               ident=(P, P), cossin=(TOK, 4 * HD // 2), masks=(P, 5, 2 * P), tri=(P, P), ids=(P, 2 * NT), slot_row=(P, CAPS[0]),
               bits=(P, BITS))
SCRATCH = dict(qT=(P, HA // 2, TOK), kT=(P, HA // 2, TOK), v=(KV_ROWS, D_A), obc=(TOK, D_B + D_C), o0=(TOK, O_COLS), o1=(TOK, O_COLS),
               o2=(TOK, O_COLS), xn=(TOK, XN_COLS), y=(TOK, D), aff=(TOK, NE))


def build(nc, A, upto=99):
    with Phase(nc, "memory") as keep:
        kmT = keep.sb("kmT", [P, 2, 2, MEM])
        vm = keep.sb("vm", [P, 2, 2, D_C])
        memory_phase(nc, A, kmT, vm)
        if upto >= 1:
            project_phase(nc, A, kmT, vm)
    if upto >= 2:
        attend_phase(nc, A)
    if upto >= 3:
        with Phase(nc, "route") as keep:
            slots = keep.sb("slots", [P, ST, NE], I32)
            affinity = keep.sb("affinity", [P, NT * NE])
            mix_phase(nc, A, affinity)
            if upto >= 4:
                choose_phase(nc, A, affinity, slots)
            if upto >= 5:
                expert_phase(nc, A, slots)
    if upto >= 6:
        final_phase(nc, A)


def constants():
    pos = np.concatenate([np.arange(s, dtype=np.float32) for s in SEQS])
    half = HD // 2
    inv = np.power(10000.0, -np.arange(half) * 2.0 / HD).astype(np.float32)
    ang = pos[:, None] * inv[None, :].astype(np.float32)
    cos, sin = np.cos(ang), np.sin(ang)
    cossin = np.concatenate([cos, cos, -sin, sin], axis=1).astype(np.float32)
    t, w = np.arange(P)[:, None], np.arange(2 * P)[None, :]
    band = np.abs(w - 64 - t) <= 64
    masks = np.zeros((P, 5, 2 * P), np.float32)
    masks[:, 0] = np.where(band & (w >= 64), 0, NEG)
    masks[:, 1] = np.where(band, 0, NEG)
    masks[:, 2] = np.where(band & (w < 64 + P), 0, NEG)
    masks[:, 3, :P] = np.where(np.abs(w[:, :P] - t) <= 64, 0, NEG)
    masks[:, 4, :P] = np.where(w[:, :P] // 64 == t // 64, 0, NEG)
    tri = (np.arange(P)[:, None] <= np.arange(P)[None, :]).astype(np.float32)
    ids = np.zeros((P, NT, 2), np.float32)
    ids[:, :, 0] = np.arange(NT)[None, :]
    ids[:, :, 1] = np.arange(P)[:, None]
    slot_row = np.broadcast_to(np.arange(1, CAPS[0] + 1, dtype=np.float32), (P, CAPS[0]))
    bits = (1 << np.arange(BITS - 1, -1, -1, dtype=np.int32)).astype(np.int32)
    return dict(ident=np.eye(P, dtype=np.float32), cossin=cossin, masks=masks, tri=tri, ids=ids.reshape(P, 2 * NT),
                slot_row=slot_row, bits=np.broadcast_to(bits.view(np.float32), (P, BITS)))


def lay_out(i):
    rows = lambda v: np.broadcast_to(np.asarray(v).reshape(1, -1), (P, v.size))
    cols = lambda v: np.asarray(v).reshape(KC, P).T
    a = {k: np.asarray(v) for k, v in i.items()}
    return dict(
        x=np.concatenate([a["x_prompt"][0], a["x_sample"][0]]), mem=np.concatenate([a["mem_prompt"][0], a["mem_sample"][0]]),
        w_in=a["w_in"][0], w_mem_kv=a["w_mem_kv"][0], w_out=a["w_out"][0], w_router=a["w_router"][0],
        w_gate=a["w_gate"][0], w_up=a["w_up"][0], w_down=a["w_down"][0],
        g_mix=cols(a["g_mix"]), g_mem=cols(a["g_mem"]), g_out=cols(a["g_out"]),
        w_sT=a["w_spatial"][0].transpose(2, 0, 1), b_sT=a["b_spatial"][0].T, ln_g=rows(a["ln_b_g"]), ln_b=rows(a["ln_b_b"]),
        g_ffn=rows(a["g_ffn"]), g_final=rows(a["g_final"]), **constants())


def kernel(**inputs):
    import concourse.bacc as bacc
    from concourse.bass_utils import run_bass_kernel_spmd

    nc = bacc.Bacc("TRN2", target_bir_lowering=False, num_devices=1)
    laid = lay_out(inputs)
    arrays, A = {}, {}
    for name, shape in DRAM_IN.items():
        arrays[f"in_{name}"] = np.ascontiguousarray(laid[name])
        A[name] = nc.dram_tensor(f"in_{name}", shape, F32, kind="ExternalInput").ap()
    for name, shape in SCRATCH.items():
        A[name] = nc.dram_tensor(f"scratch_{name}", shape, F32, kind="Internal").ap()
    A["out"] = nc.dram_tensor("out", (TOK, D), F32, kind="ExternalOutput").ap()
    build(nc, A)
    out = run_bass_kernel_spmd(nc, [arrays], core_ids=[0]).results[0]["out"]
    return out[None, :SEQS[0]], out[None, SEQS[0]:]
```

```python
from contextlib import ExitStack

import numpy as np

import concourse.bass as bass
from concourse import mybir

F32 = mybir.dt.float32
F32R = mybir.dt.float32r
BF16 = mybir.dt.bfloat16
I32 = mybir.dt.int32
U32 = mybir.dt.uint32
ACT = mybir.ActivationFunctionType
ALU = mybir.AluOpType
AX_X = mybir.AxisListType.X

P = 128
D = 1024
KC = D // P
SEQS = (2048, 1024)
TOK = sum(SEQS)
NT = TOK // P
NTP = SEQS[0] // P
PAIRS = NT // 2
PAIRS_P = NTP // 2
HA, HD = 8, 64
D_A = HA * HD
D_B = 256
GB, GD = 4, 64
HC = 4
D_C = HC * HD
D_IN = 3 * D_A + 2 * D_B + D_C
MEM = 256
NE = 16
EPS = 1e-6
SCALE = HD ** -0.5
NEG = -1e30
PAD = 256
KV_ROWS = sum(s + 2 * PAD for s in SEQS)
KV_BASE = (PAD, SEQS[0] + 3 * PAD)
O_COLS = D_A + 2 * HA
XN_COLS = D + NE
CAPS = tuple(2 * s // NE for s in SEQS)
ST = sum(CAPS) // P
BITS = 30
GELU_C = 2.0 * (2.0 / np.pi) ** 0.5


def ge(eng, sem, value):
    if isinstance(value, int) and value <= 0:
        return
    eng.wait_ge(sem, value)


def is_first(t):
    return isinstance(t, int) and t == 0


def bank_of(h):
    return h % 2 * 2 + h // 2


class Phase:

    def __init__(self, nc, name):
        self.nc, self.name, self.ctx, self.sems = nc, name, ExitStack(), []

    def __enter__(self):
        return self

    def __exit__(self, *e):
        self.ctx.close()
        if self.sems:
            self.nc.clear_and_free_semaphores(self.sems)
            self.nc.all_engine_barrier()

    def sb(self, name, shape, dt=F32):
        return self.ctx.enter_context(self.nc.sbuf_tensor(f"{self.name}_{name}", shape, dt))

    def psum(self, name, shape):
        return self.ctx.enter_context(self.nc.psum_tensor(f"{self.name}_{name}", shape, F32))

    def sem(self, name):
        self.sems.append(self.nc.alloc_semaphore(f"{self.name}_{name}"))
        return self.sems[-1]


def memory_phase(nc, A, kmT, vm, w_hi, w_lo):
    NM = 2 * MEM // P
    RI, IC = 3, D_IN // 2
    PIECES = 2 * KC
    with Phase(nc, "mem") as ph:
        ident = ph.sb("ident", [P, P])
        m = ph.sb("rows", [P, NM, D])
        w = ph.sb("w", [P, KC, 2 * D_C])
        g = ph.sb("g", [P, KC])
        junk = ph.sb("junk", [P, D], BF16)
        ss = ph.sb("ss", [P, NM])
        ms = ph.sb("ms", [P, NM])
        rstd = ph.sb("rstd", [P, NM])
        half = ph.sb("half", [P, NM])
        mT = ph.sb("mT", [P, KC, P])
        kt = ph.sb("k", [P, D_C])
        zero = ph.sb("zero", [P, D_A])
        g_mix = ph.sb("g_mix", [P, KC])
        stage = ph.sb("stage", [P, RI, IC])
        psT = ph.psum("psT", [P, KC, P])
        psKV = ph.psum("psKV", [P, 2 * D_C])
        psK = ph.psum("psK", [P, 4, P])
        m_loaded, loaded, zeroed, padded = (ph.sem(n) for n in ("m_loaded", "loaded", "zeroed", "padded"))
        in_loaded = [ph.sem(f"in_loaded{u}") for u in range(RI)]
        hi_done, lo_done = ph.sem("hi_done"), ph.sem("lo_done")

        def piece(n):
            return n // 2, slice(n % 2 * IC, (n % 2 + 1) * IC)

        squared, meaned, powered, scaled = (ph.sem(x) for x in ("squared", "meaned", "powered", "scaled"))
        w_scaled, turned, turned_sb, kv_ps = (ph.sem(x) for x in ("w_scaled", "turned", "turned_sb", "kv_ps"))
        k_sb, v_sb, kT_ps, kT_sb, half_set = (ph.sem(x) for x in ("k_sb", "v_sb", "kT_ps", "kT_sb", "half_set"))
        with nc.Block() as block:
            @block.sync
            def _(sp):
                sp.dma_start(m[:], A["mem"].rearrange("(n p) d -> p n d", p=P)).then_inc(m_loaded, 16)
                sp.dma_start(w[:], A["w_mem_kv"].rearrange("(n p) d -> p n d", p=P)).then_inc(loaded, 16)
                sp.dma_start(g[:], A["g_mem"]).then_inc(loaded, 16)
                sp.dma_start(ident[:], A["ident"]).then_inc(loaded, 16)
                sp.dma_start(g_mix[:], A["g_mix"]).then_inc(loaded, 16)
                for n in range(PIECES):
                    k, cols = piece(n)
                    ge(sp, lo_done, n - RI + 1)
                    sp.dma_start(stage[:, n % RI, :], A["w_in"][k * P:(k + 1) * P, cols]).then_inc(in_loaded[n % RI], 16)
                sp.wait_ge(zeroed, 1)
                row = 0
                pads = 0
                for s in SEQS:
                    for r in (row, row + PAD + s):
                        for j in range(0, PAD, P):
                            sp.dma_start(A["v"][r + j:r + j + P, :], zero[:]).then_inc(padded, 16)
                            pads += 1
                    row += s + 2 * PAD
                sp.wait_ge(padded, 16 * pads)

            @block.gpsimd
            def _(pool):
                nc.gpsimd.memset(half[:], -0.5).then_inc(half_set, 1)
                pool.wait_ge(half_set, 1)
                pool.wait_ge(meaned, 1)
                nc.gpsimd.tensor_tensor(rstd[:], ms[:], half[:], ALU.pow).then_inc(powered, 1)

            @block.scalar
            def _(act):
                act.wait_ge(m_loaded, 16)
                for n in range(NM):
                    if n:
                        act.wait_ge(squared, n)
                    nc.scalar.activation(junk[:], m[:, n, :], ACT.Square, accum_out=ss[:, n:n + 1]).then_inc(squared, 1)
                act.wait_ge(powered, 1)
                for n in range(NM):
                    nc.scalar.activation(m[:, n, :], m[:, n, :], ACT.Copy, scale=rstd[:, n:n + 1]).then_inc(scaled, 1)
                act.wait_ge(loaded, 64)
                for n in range(NM):
                    for q in range(n * PIECES // NM, (n + 1) * PIECES // NM):
                        k, cols = piece(q)
                        act.wait_ge(in_loaded[q % RI], 16 * (q // RI + 1))
                        nc.scalar.activation(w_hi[:, k, cols], stage[:, q % RI, :], ACT.Copy, scale=g_mix[:, k:k + 1]).then_inc(hi_done, 1)
                    act.wait_ge(kv_ps, n + 1)
                    if n:
                        act.wait_ge(kT_ps, n)
                    nc.scalar.activation(kt[:], psKV[:, 0:D_C], ACT.Copy).then_inc(k_sb, 1)
                    nc.scalar.activation(vm[:, n // 2, n % 2, :], psKV[:, D_C:], ACT.Copy).then_inc(v_sb, 1)

            @block.vector
            def _(dve):
                nc.vector.memset(zero[:], 0.0).then_inc(zeroed, 1)
                dve.wait_ge(loaded, 64)
                for k in range(KC):
                    nc.vector.tensor_scalar(w[:, k, :], w[:, k, :], g[:, k:k + 1], None, ALU.mult).then_inc(w_scaled, 1)
                dve.wait_ge(squared, NM)
                nc.vector.tensor_scalar(ms[:], ss[:], 1.0 / D, EPS, ALU.mult, ALU.add).then_inc(meaned, 1)
                for n in range(NM):
                    dve.wait_ge(turned, n + 1)
                    if n:
                        dve.wait_ge(kv_ps, n)
                    nc.vector.tensor_copy(mT[:], psT[:]).then_inc(turned_sb, 1)
                    for q in range(n * PIECES // NM, (n + 1) * PIECES // NM):
                        k, cols = piece(q)
                        dve.wait_ge(hi_done, q + 1)
                        nc.vector.scalar_tensor_tensor(out=w_lo[:, k, cols], in0=stage[:, q % RI, :], scalar=g_mix[:, k:k + 1],
                                                       in1=w_hi[:, k, cols].bitcast(F32), op0=ALU.mult,
                                                       op1=ALU.subtract).then_inc(lo_done, 1)
                    dve.wait_ge(kT_ps, n + 1)
                    nc.vector.tensor_copy(kmT[:, n // 2, :, (n % 2) * P:(n % 2 + 1) * P], psK[:, 0:2, :]).then_inc(kT_sb, 1)

            @block.tensor
            def _(pe):
                pe.wait_ge(w_scaled, KC)
                for n in range(NM):
                    pe.wait_ge(scaled, n + 1)
                    for k in range(KC):
                        last = nc.tensor.transpose(psT[:, k, :], m[:, n, k * P:(k + 1) * P], ident[:])
                    last.then_inc(turned, 1)
                    pe.wait_ge(turned_sb, n + 1)
                    if n:
                        pe.wait_ge(k_sb, n)
                        pe.wait_ge(v_sb, n)
                    for k in range(KC):
                        last = nc.tensor.matmul(psKV[:], mT[:, k, :], w[:, k, :], start=(k == 0), stop=(k == KC - 1))
                    last.then_inc(kv_ps, 1)
                    pe.wait_ge(k_sb, n + 1)
                    if n:
                        pe.wait_ge(kT_sb, n)
                    for j in range(2):
                        last = nc.tensor.transpose(psK[:, j, :], kt[:, j * P:(j + 1) * P], ident[:])
                    last.then_inc(kT_ps, 1)


def project_phase(nc, A, kmT, vm, w_hi, w_lo):
    with Phase(nc, "prj") as ph:
        ident = ph.sb("ident", [P, P])
        consts = ph.sem("consts")
        x = ph.sb("x", [P, 2, D])
        cs = ph.sb("cs", [P, 2, 4, HD // 2])
        hT_hi = ph.sb("hT_hi", [P, 2, KC, P], F32R)
        hT_lo = ph.sb("hT_lo", [P, 2, KC, P], F32R)
        qkv = ph.sb("qkv", [P, 3, D_A])
        obc = ph.sb("obc", [P, D_B + D_C])
        uv_a = ph.sb("uv_a", [P, 2 * D_B])
        uv_b = ph.sb("uv_b", [P, 2 * D_B])
        rot_b = ph.sb("rot_b", [P, D_A])
        vln = ph.sb("vln", [P, D_B])
        ob = uv_b[:, 0:D_B]
        oc = ph.sb("oc", [P, D_C])
        qc = ph.sb("qc", [P, D_C])
        qcT = ph.sb("qcT", [P, 2, P])
        prob = ph.sb("prob", [P, HC, MEM])
        probT = ph.sb("probT", [P, 2 * HC, P])
        wsT = ph.sb("wsT", [P, GB, P])
        bs = ph.sb("bs", [P, GB])
        ln_g = ph.sb("ln_g", [P, D_B])
        ln_b = ph.sb("ln_b", [P, D_B])
        stat = ph.sb("stat", [P, 64])
        half = ph.sb("half", [P, 2])
        ssx, msx, rsx = stat[:, 0:1], stat[:, 1:2], stat[:, 2:3]
        bn6, mv, vev, rsv = stat[:, 4:10], stat[:, 10:12], stat[:, 12:13], stat[:, 13:14]
        mx, nmx, den, rden = stat[:, 16:20], stat[:, 20:24], stat[:, 24:28], stat[:, 28:32]
        ssb, ssc, msbc, rsbc = stat[:, 32:33], stat[:, 33:34], stat[:, 34:36], stat[:, 36:38]

        ps_x = ph.psum("ps_x", [P, 8, P])
        ps_a = ph.psum("ps_a", [P, 512])
        ps_b = ph.psum("ps_b", [P, 512])
        ps_c = ph.psum("ps_c", [P, 512])
        ps_s = ph.psum("ps_s", [P, HC, MEM])
        ps_o = ph.psum("ps_o", [P, 512])

        names = """squared_x meaned_x powered_x scaled_x z_qc z_uv z_q z_k z_v qc_sb qcT_ps qcT_sb sc_ps xT
            hi_sb lo_sb uv_sq inner0 inner g_exp g_exp1 g_rec guv bn_a bn_b var_eps rstd_v vn vn_g vln_sb sp_ps ob_sb
            rotq_a rotq rotq_sb rotk_a rotk rotk_sb maxed nmx_sb p_sb pT_ps pT_a pT_b v_sb pv_ps rden_sb oc_sb
            sq_b sq_c ms_bc rs_bc ob_out oc_out half_set qT_ps qT_sb kT_ps kT_sb""".split()
        s = {n: ph.sem(n) for n in names}
        x_loaded = [ph.sem(f"x_loaded{u}") for u in range(2)]
        q_stored, k_stored, v_stored, obc_stored = (ph.sem(n) for n in ("q_stored", "k_stored", "v_stored", "obc_stored"))

        def loop(eng, body, start=None):
            if start:
                start()
            body(0, 0, False)
            with eng.Fori(1, PAIRS_P) as i:
                body(i, 0, False)
            with eng.Fori(PAIRS_P, PAIRS - 1) as i:
                body(i, 1, False)
            body(PAIRS - 1, 1, True)

        with nc.Block() as block:
            @block.sync
            def _(sp):
                for dst, src in ((ident, "ident"), (wsT, "w_sT"), (bs, "b_sT"), (ln_g, "ln_g"), (ln_b, "ln_b")):
                    sp.dma_start(dst[:], A[src]).then_inc(consts, 16)

                def load(t, u):
                    sp.dma_start(x[:, u, :], A["x"][bass.ds(t * P, P), :]).then_inc(x_loaded[u], 16)
                    sp.dma_start(cs[:, u, :, :], A["cossin"][bass.ds(t * P, P), :]).then_inc(x_loaded[u], 16)

                def body(i, seq, last):
                    for u in range(2):
                        t = 2 * i + u
                        row = KV_BASE[seq] - (SEQS[0] if seq else 0)
                        sp.wait_ge(s["rotk_sb"], t + 1)
                        if not last:
                            sp.wait_ge(s["xT"], t + 1)
                            load(t + 2, u)
                        sp.wait_ge(s["v_sb"], t + 1)
                        sp.dma_start(A["v"][bass.ds(t * P + row, P), :], qkv[:, 2, :]).then_inc(v_stored, 16)
                        sp.wait_ge(s["ob_out"], t + 1)
                        sp.wait_ge(s["oc_out"], t + 1)
                        sp.wait_ge(s["qT_sb"], t + 1)
                        sp.dma_start(A["obc"][bass.ds(t * P, P), :], obc[:]).then_inc(obc_stored, 16)
                        sp.dma_start(A["qT"][:, :, bass.ds(t * P, P)], qkv[:, 0, :].rearrange("p (j c) -> p j c", c=P)).then_inc(q_stored, 16)
                        sp.wait_ge(s["kT_sb"], t + 1)
                        sp.dma_start(A["kT"][:, :, bass.ds(t * P, P)], qkv[:, 1, :].rearrange("p (j c) -> p j c", c=P)).then_inc(k_stored, 16)

                def start():
                    load(0, 0)
                    load(1, 1)
                loop(sp, body, start)
                for stored in (q_stored, k_stored, v_stored, obc_stored):
                    sp.wait_ge(stored, 16 * NT)

            @block.gpsimd
            def _(pool):
                nc.gpsimd.memset(half[:], -0.5).then_inc(s["half_set"], 1)
                pool.wait_ge(s["half_set"], 1)

                def prep(t):
                    pool.wait_ge(s["meaned_x"], t + 1)
                    ge(pool, s["scaled_x"], t)
                    nc.gpsimd.tensor_tensor(rsx, msx, half[:, 0:1], ALU.pow).then_inc(s["powered_x"], 1)

                def body(i, seq, last):
                    for u in range(2):
                        t = 2 * i + u
                        if not (last and u):
                            prep(t + 1)
                        pool.wait_ge(s["var_eps"], t + 1)
                        ge(pool, s["vn"], t)
                        nc.gpsimd.tensor_tensor(rsv, vev, half[:, 0:1], ALU.pow).then_inc(s["rstd_v"], 1)
                        pool.wait_ge(s["rotq"], t + 1)
                        nc.gpsimd.tensor_tensor(qkv[:, 0, :], qkv[:, 0, :], rot_b[:], ALU.add).then_inc(s["rotq_sb"], 1)
                        pool.wait_ge(s["rotk"], t + 1)
                        nc.gpsimd.tensor_tensor(qkv[:, 1, :], qkv[:, 1, :], rot_b[:], ALU.add).then_inc(s["rotk_sb"], 1)
                        pool.wait_ge(s["ms_bc"], t + 1)
                        ge(pool, s["oc_out"], t)
                        nc.gpsimd.tensor_tensor(rsbc, msbc, half[:], ALU.pow).then_inc(s["rs_bc"], 1)
                loop(pool, body, lambda: prep(0))

            @block.scalar
            def _(act):
                act.wait_ge(consts, 16 * 5)

                def square_x(t, u, n):
                    act.wait_ge(x_loaded[u], 32 * n)
                    ge(act, s["meaned_x"], t)
                    ge(act, s["pv_ps"], t - 1)
                    nc.scalar.activation(probT[:], x[:, u, :].rearrange("p (k c) -> p k c", c=P), ACT.Square, accum_out=ssx).then_inc(s["squared_x"], 1)

                def scale_x(t, u):
                    act.wait_ge(s["powered_x"], t + 1)
                    nc.scalar.activation(x[:, u, :], x[:, u, :], ACT.Copy, scale=rsx).then_inc(s["scaled_x"], 1)

                def hi_x(t, u):
                    act.wait_ge(s["xT"], t + 1)
                    ge(act, s["z_v"], t - 1)
                    nc.scalar.activation(hT_hi[:, u, :, :], ps_x[:], ACT.Copy).then_inc(s["hi_sb"], 1)

                def out_k(t):
                    act.wait_ge(s["kT_ps"], t + 1)
                    nc.scalar.activation(qkv[:, 1, :], ps_c[:], ACT.Copy).then_inc(s["kT_sb"], 1)

                def body(i, seq, last):
                    for u in range(2):
                        t = 2 * i + u
                        more = not (last and u)
                        n = i + 1 + u
                        act.wait_ge(s["z_qc"], t + 1)
                        ge(act, s["qcT_ps"], t)
                        nc.scalar.activation(qc[:], ps_a[:, 0:D_C], ACT.Copy).then_inc(s["qc_sb"], 1)
                        if more:
                            square_x(t + 1, 1 - u, n)
                        act.wait_ge(s["z_uv"], t + 1)
                        ge(act, s["guv"], t)
                        nc.scalar.activation(uv_a[:], ps_b[:], ACT.Square).then_inc(s["uv_sq"], 1)
                        if not is_first(t):
                            out_k(t - 1)
                        act.wait_ge(s["qcT_ps"], t + 1)
                        ge(act, s["sc_ps"], t)
                        nc.scalar.activation(qcT[:], ps_s[:, 0, :], ACT.Copy).then_inc(s["qcT_sb"], 1)
                        if more:
                            scale_x(t + 1, 1 - u)
                        act.wait_ge(s["inner"], t + 1)
                        nc.scalar.activation(uv_a[:], uv_b[:], ACT.Exp, scale=-GELU_C).then_inc(s["g_exp"], 1)
                        if more:
                            hi_x(t + 1, 1 - u)
                        act.wait_ge(s["nmx_sb"], t + 1)
                        ge(act, s["pT_ps"], t)
                        ge(act, s["rden_sb"], t)
                        for h in range(HC):
                            j = bank_of(h)
                            last_exp = nc.scalar.activation(prob[:, h, :], ps_s[:, j, :], ACT.Exp, bias=nmx[:, j:j + 1],
                                                            scale=SCALE, accum_out=den[:, h:h + 1])
                        last_exp.then_inc(s["p_sb"], 1)
                        act.wait_ge(s["ob_sb"], t + 1)
                        ge(act, s["ms_bc"], t)
                        nc.scalar.activation(qc[:], ob, ACT.Square, accum_out=ssb).then_inc(s["sq_b"], 1)
                        act.wait_ge(s["pT_ps"], t + 1)
                        ge(act, s["pv_ps"], t)
                        nc.scalar.activation(probT[:, 0:HC, :], ps_x[:, 0:HC, :], ACT.Copy).then_inc(s["pT_a"], 1)
                        act.wait_ge(s["qT_ps"], t + 1)
                        nc.scalar.activation(qkv[:, 0, :], ps_c[:], ACT.Copy).then_inc(s["qT_sb"], 1)
                        act.wait_ge(s["z_v"], t + 1)
                        ge(act, v_stored, 16 * t)
                        nc.scalar.activation(qkv[:, 2, :], ps_b[:], ACT.Copy).then_inc(s["v_sb"], 1)
                        act.wait_ge(s["oc_sb"], t + 1)
                        act.wait_ge(s["sq_b"], t + 1)
                        nc.scalar.activation(qc[:], oc[:], ACT.Square, accum_out=ssc).then_inc(s["sq_c"], 1)
                        act.wait_ge(s["rs_bc"], t + 1)
                        ge(act, obc_stored, 16 * t)
                        nc.scalar.activation(obc[:, 0:D_B], ob, ACT.Copy, scale=rsbc[:, 0:1]).then_inc(s["ob_out"], 1)
                        nc.scalar.activation(obc[:, D_B:], oc[:], ACT.Copy, scale=rsbc[:, 1:2]).then_inc(s["oc_out"], 1)

                def start():
                    square_x(0, 0, 1)
                    scale_x(0, 0)
                    hi_x(0, 0)
                loop(act, body, start)
                out_k(NT - 1)

            @block.vector
            def _(dve):
                dve.wait_ge(consts, 16 * 5)

                def mean_x(t):
                    dve.wait_ge(s["squared_x"], t + 1)
                    ge(dve, s["powered_x"], t)
                    nc.vector.tensor_scalar(msx, ssx, 1.0 / D, EPS, ALU.mult, ALU.add).then_inc(s["meaned_x"], 1)

                def lo_x(t, u):
                    dve.wait_ge(s["hi_sb"], t + 1)
                    nc.vector.tensor_tensor(hT_lo[:, u, :, :], ps_x[:], hT_hi[:, u, :, :].bitcast(F32),
                                            ALU.subtract).then_inc(s["lo_sb"], 1)

                def rotate(z, out, u, first, second):
                    zh = z.rearrange("p (h two c) -> p h two c", h=HA, two=2)
                    ah = out.rearrange("p (h two c) -> p h two c", h=HA, two=2)
                    bh = rot_b[:].rearrange("p (h two c) -> p h two c", h=HA, two=2)
                    for j in range(2):
                        cos = cs[:, u, j:j + 1, :].broadcast_to([P, HA, HD // 2])
                        last_a = nc.vector.tensor_tensor(ah[:, :, j, :], zh[:, :, j, :], cos, ALU.mult)
                    last_a.then_inc(first, 1)
                    for j in range(2):
                        sin = cs[:, u, 2 + j:3 + j, :].broadcast_to([P, HA, HD // 2])
                        last_b = nc.vector.tensor_tensor(bh[:, :, j, :], zh[:, :, 1 - j, :], sin, ALU.mult)
                    last_b.then_inc(second, 1)

                def body(i, seq, last):
                    for u in range(2):
                        t = 2 * i + u
                        more = not (last and u)
                        if more:
                            mean_x(t + 1)
                        dve.wait_ge(s["uv_sq"], t + 1)
                        ge(dve, s["ob_out"], t)
                        nc.vector.tensor_scalar(uv_b[:], uv_a[:], 0.044715, 1.0, ALU.mult, ALU.add).then_inc(s["inner0"], 1)
                        dve.wait_ge(s["inner0"], t + 1)
                        nc.vector.tensor_tensor(uv_b[:], uv_b[:], ps_b[:], ALU.mult).then_inc(s["inner"], 1)
                        dve.wait_ge(s["g_exp"], t + 1)
                        nc.vector.tensor_scalar(uv_a[:], uv_a[:], 1.0, None, ALU.add).then_inc(s["g_exp1"], 1)
                        dve.wait_ge(s["g_exp1"], t + 1)
                        nc.vector.reciprocal(uv_a[:], uv_a[:]).then_inc(s["g_rec"], 1)
                        dve.wait_ge(s["g_rec"], t + 1)
                        nc.vector.tensor_tensor(uv_b[:], uv_a[:], ps_b[:], ALU.mult).then_inc(s["guv"], 1)
                        dve.wait_ge(s["guv"], t + 1)
                        nc.vector.bn_stats(bn6, uv_b[:, D_B:]).then_inc(s["bn_a"], 1)
                        dve.wait_ge(s["bn_a"], t + 1)
                        nc.vector.memset(stat[:, 40:41], 0.0)
                        nc.vector.bn_aggr(mv, bn6).then_inc(s["bn_b"], 1)
                        dve.wait_ge(s["bn_b"], t + 1)
                        ge(dve, s["rstd_v"], t)
                        nc.vector.tensor_scalar(vev, mv[:, 1:2], EPS, None, ALU.add).then_inc(s["var_eps"], 1)
                        dve.wait_ge(s["z_q"], t + 1)
                        ge(dve, s["rotk_sb"], t)
                        ge(dve, q_stored, 16 * t)
                        rotate(ps_c[:], qkv[:, 0, :], u, s["rotq_a"], s["rotq"])
                        dve.wait_ge(s["rstd_v"], t + 1)
                        ge(dve, s["sp_ps"], t)
                        nc.vector.tensor_scalar(vln[:], uv_b[:, D_B:], mv[:, 0:1], rsv, ALU.subtract, ALU.mult).then_inc(s["vn"], 1)
                        dve.wait_ge(s["vn"], t + 1)
                        nc.vector.tensor_tensor(vln[:], vln[:], ln_g[:], ALU.mult).then_inc(s["vn_g"], 1)
                        dve.wait_ge(s["vn_g"], t + 1)
                        nc.vector.tensor_tensor(vln[:], vln[:], ln_b[:], ALU.add).then_inc(s["vln_sb"], 1)
                        dve.wait_ge(s["sc_ps"], t + 1)
                        nc.vector.tensor_reduce(mx, ps_s[:], AX_X, ALU.max).then_inc(s["maxed"], 1)
                        dve.wait_ge(s["maxed"], t + 1)
                        ge(dve, s["p_sb"], t)
                        nc.vector.tensor_scalar(nmx, mx, -SCALE, None, ALU.mult).then_inc(s["nmx_sb"], 1)
                        if more:
                            lo_x(t + 1, 1 - u)
                        dve.wait_ge(s["z_k"], t + 1)
                        dve.wait_ge(s["rotq_sb"], t + 1)
                        ge(dve, k_stored, 16 * t)
                        rotate(ps_a[:], qkv[:, 1, :], u, s["rotk_a"], s["rotk"])
                        dve.wait_ge(s["sp_ps"], t + 1)
                        for gi in range(GB):
                            c = slice(gi * GD, (gi + 1) * GD)
                            gated = nc.vector.scalar_tensor_tensor(
                                out=ob[:, c], in0=ps_o[:, D_C + gi * GD:D_C + (gi + 1) * GD], scalar=bs[:, gi:gi + 1],
                                in1=uv_b[:, c], op0=ALU.add, op1=ALU.mult)
                        gated.then_inc(s["ob_sb"], 1)
                        dve.wait_ge(s["pT_ps"], t + 1)
                        ge(dve, s["pv_ps"], t)
                        nc.vector.tensor_copy(probT[:, HC:, :], ps_x[:, HC:, :]).then_inc(s["pT_b"], 1)
                        dve.wait_ge(s["p_sb"], t + 1)
                        ge(dve, s["oc_sb"], t)
                        nc.vector.reciprocal(rden, den).then_inc(s["rden_sb"], 1)
                        dve.wait_ge(s["rden_sb"], t + 1)
                        dve.wait_ge(s["pv_ps"], t + 1)
                        ge(dve, s["oc_out"], t)
                        nc.vector.tensor_tensor(oc[:].rearrange("p (h c) -> p h c", h=HC),
                                                ps_o[:, 0:D_C].rearrange("p (h c) -> p h c", h=HC),
                                                rden.rearrange("p (h one) -> p h one", one=1).broadcast_to([P, HC, HD]),
                                                ALU.mult).then_inc(s["oc_sb"], 1)
                        dve.wait_ge(s["sq_b"], t + 1)
                        dve.wait_ge(s["sq_c"], t + 1)
                        ge(dve, s["rs_bc"], t)
                        nc.vector.tensor_scalar(msbc, stat[:, 32:34], 1.0 / D_B, EPS, ALU.mult, ALU.add).then_inc(s["ms_bc"], 1)

                def start():
                    mean_x(0)
                    lo_x(0, 0)
                loop(dve, body, start)

            @block.tensor
            def _(pe):
                pe.wait_ge(consts, 16 * 5)

                def turn(t, u):
                    pe.wait_ge(s["scaled_x"], t + 1)
                    ge(pe, s["pT_a"], t - 1)
                    ge(pe, s["pT_b"], t - 1)
                    for k in range(KC):
                        last = nc.tensor.transpose(ps_x[:, k, :], x[:, u, k * P:(k + 1) * P], ident[:])
                    last.then_inc(s["xT"], 1)

                def turn_k(t):
                    pe.wait_ge(s["rotk_sb"], t + 1)
                    pe.wait_ge(s["qT_sb"], t + 1)
                    for j in range(HA // 2):
                        x_ = nc.tensor.transpose(ps_c[:, j * P:(j + 1) * P], qkv[:, 1, j * P:(j + 1) * P], ident[:])
                    x_.then_inc(s["kT_ps"], 1)

                def product(ps, u, col, width):
                    n = 0
                    for k in range(KC):
                        for a, b in ((hT_lo, w_hi), (hT_hi, w_lo), (hT_hi, w_hi)):
                            last = nc.tensor.matmul(ps[:, 0:width], a[:, u, k, :], b[:, k, col:col + width],
                                                    start=(n == 0), stop=(n == 3 * KC - 1))
                            n += 1
                    return last

                def body(i, seq, last):
                    for u in range(2):
                        t = 2 * i + u
                        pe.wait_ge(s["lo_sb"], t + 1)
                        ge(pe, s["rotk"], t)
                        product(ps_a, u, 3 * D_A + 2 * D_B, D_C).then_inc(s["z_qc"], 1)
                        ge(pe, s["v_sb"], t)
                        product(ps_b, u, 3 * D_A, 2 * D_B).then_inc(s["z_uv"], 1)
                        if not is_first(t):
                            turn_k(t - 1)
                        pe.wait_ge(s["qc_sb"], t + 1)
                        ge(pe, s["p_sb"], t)
                        for j in range(2):
                            x_ = nc.tensor.transpose(ps_s[:, 0, j * P:(j + 1) * P], qc[:, j * P:(j + 1) * P], ident[:])
                        x_.then_inc(s["qcT_ps"], 1)
                        ge(pe, s["kT_sb"], t)
                        product(ps_c, u, 0, D_A).then_inc(s["z_q"], 1)
                        pe.wait_ge(s["qcT_sb"], t + 1)
                        for h in range(HC):
                            lane = slice((h % 2) * HD, (h % 2 + 1) * HD)
                            x_ = nc.tensor.matmul(ps_s[:, bank_of(h), :], qcT[lane, h // 2, :], kmT[lane, seq, h // 2, :],
                                                  start=True, stop=True)
                        x_.then_inc(s["sc_ps"], 1)
                        if not (last and u):
                            turn(t + 1, 1 - u)
                        pe.wait_ge(s["qc_sb"], t + 1)
                        product(ps_a, u, D_A, D_A).then_inc(s["z_k"], 1)
                        pe.wait_ge(s["rotq_sb"], t + 1)
                        for j in range(HA // 2):
                            x_ = nc.tensor.transpose(ps_c[:, j * P:(j + 1) * P], qkv[:, 0, j * P:(j + 1) * P], ident[:])
                        x_.then_inc(s["qT_ps"], 1)
                        pe.wait_ge(s["vln_sb"], t + 1)
                        ge(pe, s["ob_sb"], t)
                        for gi in range(GB):
                            x_ = nc.tensor.matmul(ps_o[:, D_C + gi * GD:D_C + (gi + 1) * GD], wsT[:, gi, :],
                                                  vln[:, gi * GD:(gi + 1) * GD], start=True, stop=True)
                        x_.then_inc(s["sp_ps"], 1)
                        pe.wait_ge(s["p_sb"], t + 1)
                        if not (last and u):
                            pe.wait_ge(s["lo_sb"], t + 2)
                        for h in range(HC):
                            for c in range(2):
                                x_ = nc.tensor.transpose(ps_x[:, 2 * h + c, :], prob[:, h, c * P:(c + 1) * P], ident[:])
                        x_.then_inc(s["pT_ps"], 1)
                        pe.wait_ge(s["guv"], t + 1)
                        product(ps_b, u, 2 * D_A, D_A).then_inc(s["z_v"], 1)
                        pe.wait_ge(s["pT_a"], t + 1)
                        pe.wait_ge(s["pT_b"], t + 1)
                        ge(pe, s["oc_sb"], t)
                        for h in range(HC):
                            for c in range(2):
                                x_ = nc.tensor.matmul(ps_o[:, h * HD:(h + 1) * HD], probT[:, 2 * h + c, :],
                                                      vm[:, seq, c, h * HD:(h + 1) * HD], start=(c == 0), stop=(c == 1))
                        x_.then_inc(s["pv_ps"], 1)
                loop(pe, body, lambda: turn(0, 0))
                turn_k(NT - 1)


class Pattern:

    def __init__(self, seq, which, dil, before):
        self.seq, self.which, self.dil, self.before = seq, which, dil, before
        self.whole = dil == 16
        sub = SEQS[seq] // dil
        self.per = max(1, P // sub)
        self.blocks = SEQS[seq] // P
        self.pairs = self.blocks // 2
        self.chunks = 1 if self.whole else 2
        self.W = self.chunks * P
        self.next = None

    def mask(self, i, u):
        if self.whole:
            return 3 + self.seq
        at, of = (2 * i + u, self.blocks) if self.dil == 1 else (i // 2, self.pairs // 2)
        return 0 if at == 0 else 2 if at == of - 1 else 1

    def masks(self, i):
        return self.mask(i, 0), self.mask(i, 1), self.mask(min(i + 1, self.pairs - 1), 0)

    def run(self, eng, body, key=lambda i: 0, enter=lambda i: None):
        enter(0)
        body(0, 0, True, False)
        lo = 1
        while lo < self.pairs - 1:
            hi = lo + 1
            while hi < self.pairs - 1 and key(hi) == key(lo):
                hi += 1
            enter(lo)
            if hi - lo == 1:
                body(lo, lo, False, False)
            else:
                with eng.Fori(lo, hi) as i:
                    body(i, lo, False, False)
            lo = hi
        enter(self.pairs - 1)
        body(self.pairs - 1, self.pairs - 1, False, True)

    def after(self, i, like, u, last):
        if u == 0:
            return self, i, like, 1
        if not last:
            return self, i + 1, like + 1, 0
        return (self.next, 0, 0, 0) if self.next else None

    def place(self, i, u):
        if self.dil == 1:
            return (2 * i + u) * P, 0
        if self.whole:
            return 0, (2 * i + u) * self.per
        return i // 2 * P, i % 2 * 2 + u

    def rows(self, dram, i, u, j):
        base = self.seq * SEQS[0]
        v = dram[base:base + SEQS[self.seq], :].rearrange("(n d) c -> n d c", d=self.dil)
        n, r = self.place(i, u)
        return v[bass.ds(n, P // self.per), bass.ds(r + j, 1), :].rearrange("n d c -> n (d c)")

    def values(self, dram, i, u, j):
        base = KV_BASE[self.seq] - PAD
        v = dram[base:base + SEQS[self.seq] + 2 * PAD, :].rearrange("(n d) c -> n d c", d=self.dil)
        n, r = self.place(i, u)
        if self.whole:
            return v[PAD // self.dil:PAD // self.dil + P // self.per, bass.ds(r + j, 1), :]
        v = v[bass.ds(n + PAD // self.dil - 64, 2 * P), bass.ds(r, 1), :]
        return v.rearrange("(c p) d e -> p c (d e)", p=P)

    def queries(self, qT, i, u):
        base = self.seq * SEQS[0]
        v = qT[:, :, base:base + SEQS[self.seq]].rearrange("p j (n d) -> p j n d", d=self.dil)
        n, r = self.place(i, u)
        return v[:, :, bass.ds(n, P // self.per), bass.ds(r, self.per)].rearrange("p j n r -> p j r n")

    def keys(self, kT, i, u):
        base = KV_BASE[self.seq] - PAD
        v = kT[:, base:base + SEQS[self.seq] + 2 * PAD].rearrange("p (n d) -> p n d", d=self.dil)
        n, r = self.place(i, u)
        if self.whole:
            v = v[:, PAD // self.dil:(PAD + SEQS[self.seq]) // self.dil, bass.ds(r, self.per)]
        else:
            v = v[:, bass.ds(n + PAD // self.dil - 64, 2 * P), bass.ds(r, 1)]
        return v.rearrange("p n r -> p r n")


def attend_phase(nc, A, w_out):
    U, L = HA // 2, 3
    PIECES = 4
    PT = SEQS[0] // PIECES
    with Phase(nc, "att") as ph:
        ident = ph.sb("ident", [P, P])
        masks = ph.sb("masks", [P, 5, 2 * P])
        qT = ph.sb("qT", [P, U, TOK])
        kT = ph.sb("kT", [P, U, KV_ROWS])
        q = ph.sb("q", [P, 2, U, 2, P])
        v = ph.sb("v", [P, 2, 2, D_A])
        prob = ph.sb("prob", [P, U, 2, 2 * P])
        probT = ph.sb("probT", [P, 2, 4, P])
        o = ph.sb("o", [P, 2, O_COLS])
        stats = ph.sb("stats", [P, 2, 2 * HA])
        nmx = ph.sb("nmx", [P, U, 2])
        spare = ph.sb("spare", [P, 1])
        lane = ph.sb("lane", [P, 2])
        carry = ph.sb("carry", [P, 1])
        ps_s = ph.psum("ps_s", [P, U, 2, 2 * P])
        ps_p = ph.psum("ps_p", [P, 2, 4, P])
        ps_o = ph.psum("ps_o", [P, 2, D_A])
        consts, padded, lanes_set = ph.sem("consts"), ph.sem("padded"), ph.sem("lanes_set")
        piece_loaded = [ph.sem(f"piece_loaded{n}") for n in range(PIECES + 1)]
        v_loaded = [ph.sem(f"v_loaded{u}") for u in range(2)]
        o_stored = [ph.sem(f"o_stored{u}") for u in range(2)]
        w_loaded = ph.sem("w_loaded")
        names = "scored masked nmx_sb p_sb pT_ps pT_sb pv_ps o_sb q_free q_set".split()
        s = {n: ph.sem(n) for n in names}

        patterns = []
        for seq in range(2):
            for which, dil in enumerate((1, 4, 16)):
                patterns.append(Pattern(seq, which, dil, sum(q.blocks for q in patterns)))
        for a, b in zip(patterns, patterns[1:]):
            a.next = b
        BLOCKS = sum(pt.blocks for pt in patterns)

        def heads(j):
            return 2 * j, 2 * j + 1

        def reach(pt, i):
            return (i + 1) // 2 if pt is patterns[0] and i < pt.pairs - 1 else 0

        def await_piece(eng, pt, i):
            if pt is patterns[0] and i < pt.pairs - 1:
                eng.wait_ge(piece_loaded[reach(pt, i)], 32)
            elif i == pt.pairs - 1 and pt.next and pt.next.seq != pt.seq:
                eng.wait_ge(piece_loaded[PIECES], 32)

        def unit_ahead(pt, i, like, u, j, last):
            if j + L < U:
                return pt, i, like, u, j + L
            b = pt.after(i, like, u, last)
            return b and (*b, j + L - U)

        with nc.Block() as block:
            @block.sync
            def _(sp):
                def piece(k_at, q_at, size, done):
                    sp.dma_start(kT[:, :, k_at:k_at + size], A["kT"][:, :, q_at:q_at + size]).then_inc(done, 16)
                    sp.dma_start(qT[:, :, q_at:q_at + size], A["qT"][:, :, q_at:q_at + size]).then_inc(done, 16)

                def load_v(pt, i, u):
                    c = pt.before + 2 * i + u
                    part = P // pt.per
                    ge(sp, s["pv_ps"], U * (c - 1))
                    for j in range(pt.per):
                        at = slice(j * part, (j + 1) * part)
                        sp.dma_start(v[at, u, 0:pt.chunks, :], pt.values(A["v"], i, u, j)).then_inc(v_loaded[u], 32 // pt.per)

                def store(pt, i, u):
                    c = pt.before + 2 * i + u
                    part = P // pt.per
                    sp.wait_ge(s["o_sb"], c + 1)
                    for j in range(pt.per):
                        at = slice(j * part, (j + 1) * part)
                        sp.dma_start(pt.rows(A[f"o{pt.which}"], i, u, j), o[at, u, :]).then_inc(o_stored[u], 32 // pt.per)

                sp.dma_start(ident[:], A["ident"]).then_inc(consts, 16)
                sp.dma_start(masks[:], A["masks"]).then_inc(consts, 16)
                for n in range(PIECES):
                    piece(KV_BASE[0] + n * PT, n * PT, PT, piece_loaded[n])
                    if n == 0:
                        load_v(patterns[0], 0, 0)
                        load_v(patterns[0], 0, 1)
                sp.dma_start(w_out[:], A["w_out"].rearrange("(k p) c -> p k c", p=P)).then_inc(w_loaded, 16)
                for pt in patterns:
                    def body(i, like, first, last):
                        for u in range(2):
                            if not (first and u == 0):
                                store(pt, i - 1 + u, 1 - u)
                            nxt = pt.after(i, like, u, last)
                            if nxt and not (pt is patterns[0] and first and u == 0):
                                load_v(nxt[0], nxt[1], nxt[3])
                    pt.run(sp, body)
                    store(pt, pt.pairs - 1, 1)
                    if pt is patterns[0]:
                        piece(KV_BASE[1], SEQS[0], SEQS[1], piece_loaded[PIECES])
                for u in range(2):
                    sp.wait_ge(o_stored[u], 16 * BLOCKS)
                sp.wait_ge(w_loaded, 16)

            @block.gpsimd
            def _(pool):
                nc.gpsimd.memset(carry[:], 0.0).then_inc(padded, 1)
                nc.gpsimd.memset(lane[:], 0.0).then_inc(lanes_set, 1)
                pool.wait_ge(lanes_set, 1)
                for f in range(2):
                    nc.gpsimd.memset(lane[f * HD:(f + 1) * HD, f:f + 1], 1.0).then_inc(lanes_set, 1)
                    pool.wait_ge(lanes_set, f + 2)
                nc.gpsimd.memset(kT[:, :, 0:PAD], 0.0).then_inc(padded, 1)
                nc.gpsimd.memset(kT[:, :, KV_BASE[0] + SEQS[0]:KV_BASE[1]], 0.0).then_inc(padded, 1)
                nc.gpsimd.memset(kT[:, :, KV_ROWS - PAD:], 0.0).then_inc(padded, 1)

                def copy_q(pt, i, u):
                    c = pt.before + 2 * i + u
                    free = U * (c - 1)
                    if not (isinstance(free, int) and free <= 0):
                        ge(pool, s["q_free"], c - 2)
                        pool.wait_ge(s["scored"], free)
                        nc.gpsimd.tensor_tensor(carry[:], carry[:], carry[:], ALU.add).then_inc(s["q_free"], 1)
                    for f in range(2):
                        one = lane[:, f:f + 1].rearrange("p (a b c) -> p a b c", a=1, b=1).broadcast_to([P, U, pt.per, P // pt.per])
                        x_ = nc.gpsimd.tensor_tensor(q[:, u, :, f, :].rearrange("p j (r n) -> p j r n", r=pt.per),
                                                     pt.queries(qT, i, u), one, ALU.mult)
                    x_.then_inc(s["q_set"], 1)
                pool.wait_ge(padded, 4)
                pool.wait_ge(piece_loaded[0], 32)
                copy_q(patterns[0], 0, 0)
                for pt in patterns:
                    def body(i, like, first, last):
                        for u in range(2):
                            nxt = pt.after(i, like, u, last)
                            if nxt:
                                copy_q(nxt[0], nxt[1], nxt[3])
                    pt.run(pool, body, key=lambda i: reach(pt, i), enter=lambda i: await_piece(pool, pt, i))

            @block.tensor
            def _(pe):
                pe.wait_ge(consts, 32)
                pe.wait_ge(padded, 4)

                def scores(pt, i, u, j):
                    for f, h in enumerate(heads(j)):
                        out = ps_s[:, j, f, 0:pt.W].rearrange("p (r n) -> p r n", r=pt.per)
                        x_ = nc.tensor.matmul(out, q[:, u, j, f, :], pt.keys(kT[:, j, :], i, u),
                                              start=True, stop=True)
                    x_.then_inc(s["scored"], 1)

                def turn_p(pt, n, j, nxt):
                    if nxt and nxt[4] == 0:
                        pe.wait_ge(s["q_set"], nxt[0].before + 2 * nxt[1] + nxt[3] + 1)
                    pe.wait_ge(s["p_sb"], n + 1)
                    for f in range(2):
                        for k in range(pt.chunks):
                            x_ = nc.tensor.transpose(ps_p[:, j % 2, pt.chunks * f + k, :], prob[:, j, f, k * P:(k + 1) * P], ident[:])
                    x_.then_inc(s["pT_ps"], 1)

                def values(pt, c, i, u, j):
                    pe.wait_ge(s["pT_sb"], U * c + j + 1)
                    if j == 0:
                        pe.wait_ge(v_loaded[u], 32 * (pt.before // 2 + i + 1))
                        ge(pe, s["o_sb"], c - 1)
                    for f, h in enumerate(heads(j)):
                        for k in range(pt.chunks):
                            x_ = nc.tensor.matmul(ps_o[:, u, h * HD:(h + 1) * HD], probT[:, j % 2, pt.chunks * f + k, :],
                                                  v[:, u, k, h * HD:(h + 1) * HD], start=(k == 0), stop=(k == pt.chunks - 1))
                    x_.then_inc(s["pv_ps"], 1)

                for pt in patterns:
                    def body(i, like, first, last):
                        for u in range(2):
                            c = pt.before + 2 * i + u
                            for j in range(U):
                                nxt = unit_ahead(pt, i, like, u, j, last)
                                turn_p(pt, U * c + j, j, nxt)
                                if nxt:
                                    scores(nxt[0], nxt[1], nxt[3], nxt[4])
                                if j:
                                    values(pt, c, i, u, j - 1)
                                elif not first or u:
                                    values(pt, c - 1, None, 1 - u, U - 1)
                                elif pt is not patterns[0]:
                                    values(before, c - 1, None, 1, U - 1)

                    if pt is patterns[0]:
                        pe.wait_ge(piece_loaded[0], 32)
                        pe.wait_ge(s["q_set"], 1)
                        for j in range(L):
                            scores(pt, 0, 0, j)
                    before = patterns[max(0, patterns.index(pt) - 1)]
                    pt.run(pe, body, key=lambda i: reach(pt, i), enter=lambda i: await_piece(pe, pt, i))
                values(patterns[-1], BLOCKS - 1, None, 1, U - 1)

            @block.scalar
            def _(act):
                def exps(pt, c, u, j):
                    n = U * c + j
                    act.wait_ge(s["nmx_sb"], n + 1)
                    for f, h in enumerate(heads(j)):
                        x_ = nc.scalar.activation(prob[:, j, f, 0:pt.W], prob[:, j, f, 0:pt.W], ACT.Exp, bias=nmx[:, j, f:f + 1],
                                                  scale=SCALE, accum_out=stats[:, u, HA + h:HA + h + 1])
                    x_.then_inc(s["p_sb"], 1)

                def out_o(c, u, n):
                    act.wait_ge(s["pv_ps"], U * (c + 1))
                    ge(act, o_stored[u], 32 * n)
                    nc.scalar.activation(o[:, u, 0:D_A], ps_o[:, u, :], ACT.Copy)
                    nc.scalar.activation(o[:, u, D_A:], stats[:, u, :], ACT.Copy).then_inc(s["o_sb"], 1)

                for pt in patterns:
                    def body(i, like, first, last):
                        for u in range(2):
                            for j in range(U):
                                c = pt.before + 2 * i + u
                                if j == 1 and not (pt is patterns[0] and first and u == 0):
                                    out_o(c - 1, 1 - u, pt.before // 2 + i - 1 + u)
                                nxt = unit_ahead(pt, i, like, u, j, last)
                                if nxt:
                                    exps(nxt[0], nxt[0].before + 2 * nxt[1] + nxt[3], nxt[3], nxt[4])
                    if pt is patterns[0]:
                        for j in range(L):
                            exps(pt, 0, 0, j)
                    pt.run(act, body)
                out_o(BLOCKS - 1, 1, BLOCKS // 2 - 1)

            @block.vector
            def _(dve):
                dve.wait_ge(consts, 32)

                def mask(pt, i, like, u, j):
                    c = pt.before + 2 * i + u
                    n = U * c + j
                    dve.wait_ge(s["scored"], n + 1)
                    ge(dve, s["pT_ps"], n - U + 1)
                    if j == 0:
                        ge(dve, s["o_sb"], c - 1)
                    nc.vector.memset(spare[:], 0.0)
                    for f, h in enumerate(heads(j)):
                        x_ = nc.vector.tensor_tensor_reduce(
                            out=prob[:, j, f, 0:pt.W], in0=ps_s[:, j, f, 0:pt.W], in1=masks[:, pt.mask(like, u), 0:pt.W], scale=1.0,
                            scalar=-3e38, op0=ALU.add, op1=ALU.max, accum_out=stats[:, u, h:h + 1])
                    x_.then_inc(s["masked"], 1)
                    dve.wait_ge(s["masked"], n + 1)
                    nc.vector.tensor_scalar(nmx[:, j, :], stats[:, u, 2 * j:2 * j + 2], -SCALE, None, ALU.mult)\
                        .then_inc(s["nmx_sb"], 1)

                def out_p(pt, n, j):
                    dve.wait_ge(s["pT_ps"], n + 1)
                    ge(dve, s["pv_ps"], n - 1)
                    nc.vector.tensor_copy(probT[:, j % 2, 0:2 * pt.chunks, :], ps_p[:, j % 2, 0:2 * pt.chunks, :])\
                        .then_inc(s["pT_sb"], 1)

                for pt in patterns:
                    def body(i, like, first, last):
                        for u in range(2):
                            c = pt.before + 2 * i + u
                            for j in range(U):
                                out_p(pt, U * c + j, j)
                                nxt = unit_ahead(pt, i, like, u, j, last)
                                if nxt:
                                    mask(*nxt)
                    if pt is patterns[0]:
                        for j in range(L):
                            mask(pt, 0, 0, 0, j)
                    pt.run(dve, body, key=pt.masks)


def mix_phase(nc, A, affinity, w_out):
    with Phase(nc, "mix") as ph:
        ident = ph.sb("ident", [P, P])
        w_hi = ph.sb("w_hi", [P, KC, D], F32R)
        w_lo = ph.sb("w_lo", [P, KC, D], F32R)
        g_out = ph.sb("g_out", [P, KC])
        w_r = ph.sb("w_r", [P, KC, NE])
        g_ffn = ph.sb("g_ffn", [P, D])
        consts, g_loaded, w_hi_set, w_lo_set = (ph.sem(n) for n in ("consts", "g_loaded", "w_hi_set", "w_lo_set"))
        o3 = ph.sb("o3", [P, 2, 3, O_COLS])
        obc = ph.sb("obc", [P, 2, D_B + D_C])
        oa = ph.sb("oa", [P, 2, D_A])
        cT_hi = ph.sb("cT_hi", [P, 2, KC, P], F32R)
        cT_lo = ph.sb("cT_lo", [P, 2, KC, P], F32R)
        x = ph.sb("x", [P, 2, D])
        xn = ph.sb("xn", [P, 2, XN_COLS])
        xnT = ph.sb("xnT", [P, KC, P])
        junk = ph.sb("junk", [P, D], BF16)
        stat = ph.sb("stat", [P, 160])
        half = ph.sb("half", [P, 1])
        top, wts, wden = stat[:, 0:8], stat[:, 8:32], stat[:, 32:56]
        tot, rtot, wfin = stat[:, 56:64], stat[:, 64:72], stat[:, 72:96]
        ss_a, ms_a, rs_a = stat[:, 96:97], stat[:, 97:98], stat[:, 98:99]
        ss_y, ms_y, rs_y = stat[:, 100:101], stat[:, 101:102], stat[:, 102:103]
        rmax, rneg, rden, rrec, rexp = stat[:, 104:105], stat[:, 105:106], stat[:, 106:107], stat[:, 107:108], stat[:, 112:128]
        ps_c = ph.psum("ps_c", [P, KC, P])
        ps_y = ph.psum("ps_y", [P, 2, 512])
        ps_n = ph.psum("ps_n", [P, KC, P])
        ps_r = ph.psum("ps_r", [P, 512])
        names = """topped shifted weighted wden_sb tot_sb rtot_sb wfin_sb scaled3 added_a added_b sq_a ms_a rs_a
            oa_out cT_ps hi_sb lo_sb y_a y_b x1_a x1_b sq_y ms_y rs_y xn_sb nT_ps nT_sb r_ps rmax_sb rneg_sb
            rexp_sb rrec_sb aff_a aff_b half_set""".split()
        s = {n: ph.sem(n) for n in names}
        o_loaded = [ph.sem(f"o_loaded{u}") for u in range(2)]
        x_loaded = [ph.sem(f"x_loaded{u}") for u in range(2)]
        y_stored = [ph.sem(f"y_stored{u}") for u in range(2)]
        xn_stored = [ph.sem(f"xn_stored{u}") for u in range(2)]

        def loop(eng, body):
            body(0, True, False)
            with eng.Fori(1, PAIRS - 1) as i:
                body(i, False, False)
            body(PAIRS - 1, False, True)

        with nc.Block() as block:
            @block.sync
            def _(sp):
                def load_o(t, u):
                    ge(sp, s["added_b"], t - 1)
                    ge(sp, s["cT_ps"], t - 1)
                    for j in range(3):
                        sp.dma_start(o3[:, u, j, :], A[f"o{j}"][bass.ds(t * P, P), :]).then_inc(o_loaded[u], 16)
                    sp.dma_start(obc[:, u, :], A["obc"][bass.ds(t * P, P), :]).then_inc(o_loaded[u], 16)

                def load_x(t, u, n):
                    ge(sp, y_stored[u], 16 * n)
                    ge(sp, s["xn_sb"], t - 1)
                    sp.dma_start(x[:, u, :], A["x"][bass.ds(t * P, P), :]).then_inc(x_loaded[u], 16)

                def store_y(t, u):
                    sp.wait_ge(s["x1_b"], t + 1)
                    sp.dma_start(A["y"][bass.ds(t * P, P), :], x[:, u, :]).then_inc(y_stored[u], 16)

                def store_xn(t, u):
                    sp.wait_ge(s["aff_a"], t + 1)
                    sp.dma_start(A["xn"][bass.ds(t * P, P), :], xn[:, u, :]).then_inc(xn_stored[u], 16)

                def body(i, first, last):
                    next_last = isinstance(i, int) and i == PAIRS - 2
                    for u in range(2):
                        t = 2 * i + u
                        if not (first and u == 0):
                            store_y(t - 1, 1 - u)
                        if not (last and u):
                            load_x(t + 1, 1 - u, i + u)
                        if not last and not (next_last and u):
                            load_o(t + 3, 1 - u)
                        if not first:
                            store_xn(t - 2, u)
                sp.dma_start(g_out[:], A["g_out"]).then_inc(g_loaded, 16)
                load_o(0, 0)
                sp.dma_start(ident[:], A["ident"]).then_inc(consts, 16)
                load_o(1, 1)
                load_x(0, 0, 0)
                sp.dma_start(g_ffn[:], A["g_ffn"]).then_inc(consts, 16)
                sp.dma_start(w_r[:], A["w_router"].rearrange("(k p) e -> p k e", p=P)).then_inc(consts, 16)
                load_o(2, 0)
                body(0, True, False)
                with sp.Fori(1, PAIRS - 2) as i:
                    body(i, False, False)
                body(PAIRS - 2, False, False)
                body(PAIRS - 1, False, True)
                store_y(NT - 1, 1)
                for u in range(2):
                    store_xn(NT - 2 + u, u)
                for u in range(2):
                    sp.wait_ge(y_stored[u], 16 * PAIRS)
                    sp.wait_ge(xn_stored[u], 16 * PAIRS)

            @block.gpsimd
            def _(pool):
                nc.gpsimd.memset(half[:], -0.5).then_inc(s["half_set"], 1)
                pool.wait_ge(s["half_set"], 1)

                def join(t, u):
                    pool.wait_ge(s["scaled3"], t + 1)
                    ge(pool, s["oa_out"], t)
                    a, b, c = (o3[:, u, j, 0:D_A] for j in range(3))
                    nc.gpsimd.tensor_tensor(a, a, b, ALU.add).then_inc(s["added_a"], 1)
                    pool.wait_ge(s["added_a"], t + 1)
                    ge(pool, s["cT_ps"], t - 1)
                    nc.gpsimd.tensor_tensor(oa[:, u, :], a, c, ALU.add).then_inc(s["added_b"], 1)
                    pool.wait_ge(s["ms_a"], t + 1)
                    nc.gpsimd.tensor_tensor(rs_a, ms_a, half[:], ALU.pow).then_inc(s["rs_a"], 1)

                def norm(t):
                    pool.wait_ge(s["ms_y"], t + 1)
                    ge(pool, s["xn_sb"], t)
                    nc.gpsimd.tensor_tensor(rs_y, ms_y, half[:], ALU.pow).then_inc(s["rs_y"], 1)

                def body(i, first, last):
                    for u in range(2):
                        t = 2 * i + u
                        if not (first and u == 0):
                            norm(t - 1)
                        if not last:
                            join(t + 2, u)
                join(0, 0)
                join(1, 1)
                loop(pool, body)
                norm(NT - 1)

            @block.scalar
            def _(act):

                def weigh(t):
                    act.wait_ge(s["shifted"], t + 1)
                    nc.scalar.activation(wts, wts, ACT.Exp, scale=SCALE).then_inc(s["weighted"], 1)

                def join(t, u):
                    act.wait_ge(s["added_b"], t + 1)
                    ge(act, s["ms_a"], t)
                    nc.scalar.activation(junk[:, 0:D_A], oa[:, u, :], ACT.Square, accum_out=ss_a).then_inc(s["sq_a"], 1)
                    act.wait_ge(s["rs_a"], t + 1)
                    nc.scalar.activation(oa[:, u, :], oa[:, u, :], ACT.Copy, scale=rs_a).then_inc(s["oa_out"], 1)

                def hi(t, u):
                    act.wait_ge(s["cT_ps"], t + 1)
                    ge(act, s["y_b"], t - 1)
                    nc.scalar.activation(cT_hi[:, u, :, :], ps_c[:], ACT.Copy).then_inc(s["hi_sb"], 1)

                def square(t, u):
                    act.wait_ge(s["x1_b"], t + 1)
                    ge(act, s["ms_y"], t)
                    nc.scalar.activation(junk[:], x[:, u, :], ACT.Square, accum_out=ss_y).then_inc(s["sq_y"], 1)

                def out_n(t):
                    act.wait_ge(s["nT_ps"], t + 1)
                    ge(act, s["r_ps"], t)
                    nc.scalar.activation(xnT[:], ps_n[:], ACT.Copy).then_inc(s["nT_sb"], 1)

                def softmax(t):
                    act.wait_ge(s["rneg_sb"], t + 1)
                    ge(act, s["aff_b"], t)
                    nc.scalar.activation(rexp, ps_r[:, 0:NE], ACT.Exp, bias=rneg, accum_out=rden).then_inc(s["rexp_sb"], 1)

                def body(i, first, last):
                    for u in range(2):
                        t = 2 * i + u
                        if not (first and u == 0):
                            square(t - 1, 1 - u)
                        if not last:
                            weigh(t + 2)
                        if not first:
                            out_n(t - 2)
                        if not (last and u):
                            hi(t + 1, 1 - u)
                        if not first:
                            softmax(t - 2)
                        if not last:
                            join(t + 2, u)
                act.wait_ge(g_loaded, 16)
                for k in range(KC):
                    nc.scalar.activation(w_hi[:, k, :], w_out[:, k, :], ACT.Copy, scale=g_out[:, k:k + 1])\
                        .then_inc(w_hi_set, 1)
                weigh(0)
                join(0, 0)
                hi(0, 0)
                weigh(1)
                join(1, 1)
                loop(act, body)
                square(NT - 1, 1)
                for t in (NT - 2, NT - 1):
                    out_n(t)
                    softmax(t)

            @block.vector
            def _(dve):

                def heads(ap):
                    return ap.rearrange("p (j h) -> p j h", j=3)

                def over(ap):
                    return ap.rearrange("p (one h) -> p one h", one=1).broadcast_to([P, 3, HA])

                def join(t, u, n):
                    dve.wait_ge(o_loaded[u], 64 * n)
                    mj = o3[:, u, :, D_A:D_A + HA]
                    nc.vector.tensor_reduce(top, mj.rearrange("p j h -> p h j"), AX_X, ALU.max).then_inc(s["topped"], 1)
                    dve.wait_ge(s["topped"], t + 1)
                    ge(dve, s["wfin_sb"], t)
                    nc.vector.tensor_tensor(heads(wts), mj, over(top), ALU.subtract).then_inc(s["shifted"], 1)
                    dve.wait_ge(s["weighted"], t + 1)
                    nc.vector.tensor_tensor(heads(wden), heads(wts), o3[:, u, :, D_A + HA:], ALU.mult).then_inc(s["wden_sb"], 1)
                    dve.wait_ge(s["wden_sb"], t + 1)
                    nc.vector.tensor_reduce(tot, wden.rearrange("p (j h) -> p h j", j=3), AX_X, ALU.add).then_inc(s["tot_sb"], 1)
                    dve.wait_ge(s["tot_sb"], t + 1)
                    nc.vector.reciprocal(rtot, tot).then_inc(s["rtot_sb"], 1)
                    dve.wait_ge(s["rtot_sb"], t + 1)
                    nc.vector.tensor_tensor(heads(wfin), heads(wts), over(rtot), ALU.mult).then_inc(s["wfin_sb"], 1)
                    dve.wait_ge(s["wfin_sb"], t + 1)
                    for j in range(3):
                        v = o3[:, u, j, 0:D_A].rearrange("p (h c) -> p h c", h=HA)
                        by = wfin[:, j * HA:(j + 1) * HA].rearrange("p (h one) -> p h one", one=1).broadcast_to([P, HA, HD])
                        x_ = nc.vector.tensor_tensor(v, v, by, ALU.mult)
                    x_.then_inc(s["scaled3"], 1)

                def mean_a(t):
                    dve.wait_ge(s["sq_a"], t + 1)
                    ge(dve, s["oa_out"], t)
                    nc.vector.tensor_scalar(ms_a, ss_a, 1.0 / D_A, EPS, ALU.mult, ALU.add).then_inc(s["ms_a"], 1)

                def lo(t, u):
                    dve.wait_ge(s["hi_sb"], t + 1)
                    nc.vector.tensor_tensor(cT_lo[:, u, :, :], ps_c[:], cT_hi[:, u, :, :].bitcast(F32), ALU.subtract)\
                        .then_inc(s["lo_sb"], 1)

                def add_x(t, u, j, n):
                    if j == 0:
                        dve.wait_ge(x_loaded[u], 16 * n)
                    c = slice(j * 512, (j + 1) * 512)
                    dve.wait_ge(s["y_b" if j else "y_a"], t + 1)
                    nc.vector.tensor_tensor(x[:, u, c], x[:, u, c], ps_y[:, j, :], ALU.add).then_inc(s["x1_b" if j else "x1_a"], 1)

                def norm(t, u, n):
                    dve.wait_ge(s["sq_y"], t + 1)
                    ge(dve, s["rs_y"], t)
                    nc.vector.tensor_scalar(ms_y, ss_y, 1.0 / D, EPS, ALU.mult, ALU.add).then_inc(s["ms_y"], 1)
                    dve.wait_ge(s["rs_y"], t + 1)
                    ge(dve, xn_stored[u], 16 * n)
                    ge(dve, s["nT_ps"], t - 1)
                    nc.vector.scalar_tensor_tensor(out=xn[:, u, 0:D], in0=x[:, u, :], scalar=rs_y, in1=g_ffn[:],
                                                   op0=ALU.mult, op1=ALU.mult).then_inc(s["xn_sb"], 1)

                def softmax(t, u):
                    dve.wait_ge(s["r_ps"], t + 1)
                    nc.vector.tensor_reduce(rmax, ps_r[:, 0:NE], AX_X, ALU.max).then_inc(s["rmax_sb"], 1)
                    dve.wait_ge(s["rmax_sb"], t + 1)
                    ge(dve, s["rexp_sb"], t)
                    nc.vector.tensor_scalar(rneg, rmax, -1.0, None, ALU.mult).then_inc(s["rneg_sb"], 1)
                    dve.wait_ge(s["rexp_sb"], t + 1)
                    nc.vector.reciprocal(rrec, rden).then_inc(s["rrec_sb"], 1)
                    dve.wait_ge(s["rrec_sb"], t + 1)
                    nc.vector.tensor_scalar(xn[:, u, D:], rexp, rrec, None, ALU.mult).then_inc(s["aff_a"], 1)
                    nc.vector.tensor_scalar(affinity[:, bass.ds(t * NE, NE)], rexp, rrec, None, ALU.mult).then_inc(s["aff_b"], 1)

                def body(i, first, last):
                    for u in range(2):
                        t = 2 * i + u
                        past = not (first and u == 0)
                        if past:
                            add_x(t - 1, 1 - u, 1, None)
                        if past:
                            norm(t - 1, 1 - u, i - 1 + u)
                        if not last:
                            join(t + 2, u, i + 2)
                        add_x(t, u, 0, i + 1)
                        if not (last and u):
                            lo(t + 1, 1 - u)
                        if not first:
                            softmax(t - 2, u)
                        if not last:
                            mean_a(t + 2)
                for k in range(KC):
                    dve.wait_ge(w_hi_set, k + 1)
                    nc.vector.scalar_tensor_tensor(out=w_lo[:, k, :], in0=w_out[:, k, :], scalar=g_out[:, k:k + 1],
                                                   in1=w_hi[:, k, :].bitcast(F32), op0=ALU.mult,
                                                   op1=ALU.subtract).then_inc(w_lo_set, 1)
                join(0, 0, 1)
                mean_a(0)
                lo(0, 0)
                join(1, 1, 1)
                mean_a(1)
                dve.wait_ge(consts, 48)
                loop(dve, body)
                add_x(NT - 1, 1, 1, None)
                norm(NT - 1, 1, PAIRS - 1)
                for u in range(2):
                    softmax(NT - 2 + u, u)

            @block.tensor
            def _(pe):
                pe.wait_ge(consts, 48)

                def turn(t, u):
                    pe.wait_ge(s["oa_out"], t + 1)
                    ge(pe, s["lo_sb"], t)
                    for k in range(KC):
                        src = oa[:, u, k * P:(k + 1) * P] if k < 4 else obc[:, u, (k - 4) * P:(k - 3) * P]
                        x_ = nc.tensor.transpose(ps_c[:, k, :], src, ident[:])
                    x_.then_inc(s["cT_ps"], 1)

                def turn_n(t, u):
                    pe.wait_ge(s["xn_sb"], t + 1)
                    ge(pe, s["nT_sb"], t)
                    for k in range(KC):
                        x_ = nc.tensor.transpose(ps_n[:, k, :], xn[:, u, k * P:(k + 1) * P], ident[:])
                    x_.then_inc(s["nT_ps"], 1)

                def product(t, u, j):
                    ge(pe, s["x1_b" if j else "x1_a"], t)
                    n = 0
                    for k in range(KC):
                        for a, b in ((cT_lo, w_hi), (cT_hi, w_lo), (cT_hi, w_hi)):
                            x_ = nc.tensor.matmul(ps_y[:, j, :], a[:, u, k, :], b[:, k, j * 512:(j + 1) * 512],
                                                  start=(n == 0), stop=(n == 3 * KC - 1))
                            n += 1
                    x_.then_inc(s["y_b" if j else "y_a"], 1)

                def route(t):
                    pe.wait_ge(s["nT_sb"], t + 1)
                    ge(pe, s["rexp_sb"], t)
                    for k in range(KC):
                        x_ = nc.tensor.matmul(ps_r[:, 0:NE], xnT[:, k, :], w_r[:, k, :], start=(k == 0), stop=(k == KC - 1))
                    x_.then_inc(s["r_ps"], 1)

                def body(i, first, last):
                    for u in range(2):
                        t = 2 * i + u
                        pe.wait_ge(s["lo_sb"], t + 1)
                        product(t, u, 0)
                        if not first:
                            route(t - 2)
                        if not (last and u):
                            turn(t + 1, 1 - u)
                        product(t, u, 1)
                        if not (first and u == 0):
                            turn_n(t - 1, 1 - u)
                turn(0, 0)
                pe.wait_ge(w_lo_set, KC)
                loop(pe, body)
                route(NT - 2)
                turn_n(NT - 1, 1)
                route(NT - 1)


def choose_phase(nc, A, affinity, slots):
    B = 16
    EG = P // B
    COLS = EG * B * 2
    BLOCK = B * P + B
    with Phase(nc, "top") as ph:
        load = ph.sb("load", [P, P + 2 * NT + B])
        bits = ph.sb("bits", [P, BITS], I32)
        ones = ph.sb("ones", [P, P], BF16)
        tri = ph.sb("tri", [P, P], BF16)
        ids = ph.sb("ids", [P, 2 * NT], BF16)
        digits = ph.sb("digits", [P, B], BF16)
        ident = ph.sb("ident", [P, P])
        caps = ph.sb("caps", [P, 2, NE])
        thr = ph.sb("thr", [P, 2, NE], I32)
        cand = ph.sb("cand", [P, 2, NE], I32)
        kept = ph.sb("kept", [P, 2, NE], I32)
        hits = ph.sb("hits", [P, NT, NE], BF16)
        ties = ph.sb("ties", [P, NT, NE], BF16)
        chosen = ph.sb("chosen", [P, NT, NE], BF16)
        need = ph.sb("need", [P, 2, NE])
        sums = ph.sb("sums", [P, 2, NT, NE])
        rank = ph.sb("rank", [P, NT, NE])
        slot = ph.sb("slot", [P, NT * NE])
        slot_i = ph.sb("slot_i", [P, NT * NE], I32)
        part_i = ph.sb("part_i", [P, 2, NT * NE], I32)
        part = ph.sb("part", [P, 2, NT * NE])
        R = 4
        hot_a = ph.sb("hot_a", [P, R, NE, B], BF16)
        hot_b = ph.sb("hot_b", [P, R, NE * B], BF16)
        hot_id = ph.sb("hot_id", [P, R, NE * B, 2], BF16)
        lists = ph.sb("lists", [P, 2, 2, COLS])
        tokens = ph.sb("tokens", [P, 2, 2, EG * B])
        rows = ph.sb("rows", [ST * NE, P])
        ps_n = ph.psum("ps_n", [P, 2, 256])
        ps_w = ph.psum("ps_w", [P, 512])
        ps_s = ph.psum("ps_s", [P, 512])
        ps_l = [[ph.psum(f"ps_l{seq}{g}", [P, 512]) for g in range(2)] for seq in range(2)]
        ps_t = ph.psum("ps_t", [P, 512])
        names = """loaded made cand_set hit counted kept_set thr_set gt eq n_gt pre_ps need_sb run rank_sb ok tied sel
            sel_ps slot_sb int_sb parts_i parts a_set b_set id_set hot_used copied numbered written read turned
            slots_set""".split()
        s = {n: ph.sem(n) for n in names}
        MADE = 8
        STEP = 5
        assert BITS % STEP == 0
        tiles = (slice(0, NTP), slice(NTP, NT))

        def per_tile(ap, seq):
            n = tiles[seq].stop - tiles[seq].start
            return ap[:, seq:seq + 1, :].broadcast_to([P, n, NE])

        with nc.Block() as block:
            @block.sync
            def _(sp):
                sp.dma_start(load[:, 0:P], A["tri"]).then_inc(s["loaded"], 16)
                sp.dma_start(load[:, P:P + 2 * NT], A["ids"]).then_inc(s["loaded"], 16)
                sp.dma_start(load[:, P + 2 * NT:], A["digits"]).then_inc(s["loaded"], 16)
                sp.dma_start(ident[:], A["ident"]).then_inc(s["loaded"], 16)
                sp.dma_start(bits[:].bitcast(F32), A["bits"]).then_inc(s["loaded"], 16)
                for seq in range(2):
                    for g in range(2):
                        sp.wait_ge(s["numbered"], 2 * seq + g + 1)
                        sp.dma_start(A["lists"][seq, g, 0:P * P].rearrange("(p c) -> p c", c=P), tokens[:, seq, g, :])\
                            .then_inc(s["written"], 16)
                sp.wait_ge(s["written"], 16 * 4)
                for j in range(ST):
                    seq, a0 = min(j // 2, 1), j % 2 * EG
                    for g in range(2):
                        src = A["lists"][seq, g, 0:EG * BLOCK].rearrange("(e x) -> e x", x=BLOCK)[:, a0 * P:(a0 + EG) * P]
                        sp.dma_start(rows[j * NE + g * EG:j * NE + (g + 1) * EG, :].rearrange("e (a b) -> e a b", b=B),
                                     src.rearrange("e (a c) -> e a c", c=P)[:, :, 0:B]).then_inc(s["read"], 16)

            @block.tensor
            def _(pe):
                pe.wait_ge(s["made"], MADE)

                def count(what, bit=None):
                    for seq in range(2):
                        if bit is not None:
                            pe.wait_ge(s["hit"], 2 * bit + seq + 1)
                        t0, t1 = tiles[seq].start, tiles[seq].stop
                        for t in range(t0, t1):
                            x_ = nc.tensor.matmul(ps_n[:, seq, 0:NE], ones[:], what[:, t, :], start=(t == t0), stop=(t == t1 - 1))
                    return x_

                def prefix(what, done):
                    nc.tensor.matmul(ps_w[:, 0:NT * NE], tri[:], what[:].rearrange("p t e -> p (t e)"), start=True, stop=True)
                    nc.tensor.matmul(ps_s[:, 0:NT * NE], ones[:], what[:].rearrange("p t e -> p (t e)"), start=True, stop=True)\
                        .then_inc(done, 1)
                with pe.Fori(0, BITS // STEP) as i:
                    for k in range(STEP):
                        count(hits, STEP * i + k).then_inc(s["counted"], 1)
                pe.wait_ge(s["gt"], 1)
                count(hits).then_inc(s["n_gt"], 1)
                pe.wait_ge(s["eq"], 1)
                prefix(ties, s["pre_ps"])
                pe.wait_ge(s["sel"], 1)
                prefix(chosen, s["sel_ps"])
                def add(i, seq, first, last):
                    for r in range(R):
                        t = R * i + r
                        pe.wait_ge(s["a_set"], t + 1)
                        pe.wait_ge(s["id_set"], t + 1)
                        for g in range(2):
                            x_ = nc.tensor.matmul(ps_l[seq][g][:, 0:COLS],
                                                  hot_a[:, r, g * EG:(g + 1) * EG, :].rearrange("p e a -> p (e a)"),
                                                  hot_id[:, r, g * EG * B:(g + 1) * EG * B, :].rearrange("p n c -> p (n c)"),
                                                  start=first and r == 0, stop=last and r == R - 1)
                        x_.then_inc(s["hot_used"], 1)
                for seq in range(2):
                    n0, n1 = tiles[seq].start // R, tiles[seq].stop // R
                    add(n0, seq, True, False)
                    if n1 - n0 > 2:
                        with pe.Fori(n0 + 1, n1 - 1) as i:
                            add(i, seq, False, False)
                    add(n1 - 1, seq, False, True)
                pe.wait_ge(s["read"], 16 * 2 * ST)
                nc.tensor.transpose(ps_t[:, 0:ST * NE], rows[:], ident[0:ST * NE, 0:ST * NE]).then_inc(s["turned"], 1)

            @block.vector
            def _(dve):
                nc.vector.memset(ones[:], 1.0).then_inc(s["made"], 1)
                nc.vector.memset(thr[:], 0).then_inc(s["made"], 1)
                for seq in range(2):
                    nc.vector.memset(caps[:, seq, :], float(CAPS[seq])).then_inc(s["made"], 1)
                    nc.vector.memset(sums[:, 0, tiles[seq].start, :], 0.0).then_inc(s["made"], 1)
                dve.wait_ge(s["loaded"], 80)
                nc.vector.tensor_copy(tri[:], load[:, 0:P])
                nc.vector.tensor_copy(ids[:], load[:, P:P + 2 * NT]).then_inc(s["made"], 1)
                nc.vector.tensor_copy(digits[:], load[:, P + 2 * NT:]).then_inc(s["made"], 1)
                dve.wait_ge(s["made"], MADE)
                aff = affinity[:].rearrange("p (t e) -> p t e", e=NE)

                def compare(out, op, level, each=None):
                    for seq in range(2):
                        x_ = nc.vector.tensor_tensor(out[:, tiles[seq], :], aff[:, tiles[seq], :], per_tile(level, seq), op)
                        if each:
                            x_.then_inc(each, 1)
                    return x_

                def halve(b):
                    ge(dve, s["thr_set"], b)
                    nc.vector.tensor_tensor(cand[:].rearrange("p s e -> p (s e)"), thr[:].rearrange("p s e -> p (s e)"),
                                            bits[:, bass.ds(b, 1)].broadcast_to([P, 2 * NE]), ALU.bitwise_or).then_inc(s["cand_set"], 1)
                    dve.wait_ge(s["cand_set"], b + 1)
                    ge(dve, s["counted"], b)
                    compare(hits, ALU.is_ge, cand[:].bitcast(F32), s["hit"])
                    dve.wait_ge(s["counted"], b + 1)
                    nc.vector.tensor_tensor(kept[:], ps_n[:, :, 0:NE], caps[:], ALU.is_ge).then_inc(s["kept_set"], 1)
                    dve.wait_ge(s["kept_set"], b + 1)
                    nc.vector.memset(slot[:, 0:1], 0.0)
                    nc.vector.copy_predicated(thr[:], kept[:], cand[:]).then_inc(s["thr_set"], 1)
                for b in range(STEP):
                    halve(b)
                with dve.Fori(1, BITS // STEP) as i:
                    for k in range(STEP):
                        halve(STEP * i + k)

                dve.wait_ge(s["thr_set"], BITS)
                compare(hits, ALU.is_gt, thr[:].bitcast(F32)).then_inc(s["gt"], 1)
                compare(ties, ALU.is_equal, thr[:].bitcast(F32)).then_inc(s["eq"], 1)
                dve.wait_ge(s["n_gt"], 1)
                nc.vector.tensor_tensor(need[:], caps[:], ps_n[:, :, 0:NE], ALU.subtract).then_inc(s["need_sb"], 1)
                runs = [0]

                def ranks(done):
                    dve.wait_ge(done, 1)
                    ge(dve, s["run"], runs[0])
                    for k in tiles:
                        nc.vector.tensor_copy(sums[:, 0, k.start + 1:k.stop, :].rearrange("p t e -> p (t e)"),
                                              ps_s[:, k.start * NE:(k.stop - 1) * NE]).then_inc(s["run"], 1)
                        runs[0] += 1
                    at, d = 0, 1
                    while d < NTP:
                        dve.wait_ge(s["run"], runs[0])
                        for k in tiles:
                            mid = min(k.start + d, k.stop)
                            nc.vector.tensor_copy(sums[:, 1 - at, k.start:mid, :], sums[:, at, k.start:mid, :])\
                                .then_inc(s["run"], 1)
                            runs[0] += 1
                            if mid < k.stop:
                                nc.vector.tensor_tensor(sums[:, 1 - at, mid:k.stop, :], sums[:, at, mid:k.stop, :],
                                                        sums[:, at, k.start:k.stop - d, :], ALU.add).then_inc(s["run"], 1)
                                runs[0] += 1
                        at, d = 1 - at, 2 * d
                    dve.wait_ge(s["run"], runs[0])
                    nc.vector.tensor_tensor(rank[:].rearrange("p t e -> p (t e)"), sums[:, at, :, :].rearrange("p t e -> p (t e)"),
                                            ps_w[:, 0:NT * NE], ALU.add).then_inc(s["rank_sb"], 1)

                ranks(s["pre_ps"])
                dve.wait_ge(s["rank_sb"], 1)
                dve.wait_ge(s["need_sb"], 1)
                for seq in range(2):
                    nc.vector.tensor_tensor(rank[:, tiles[seq], :], rank[:, tiles[seq], :], per_tile(need, seq), ALU.is_le)\
                        .then_inc(s["ok"], 1)
                dve.wait_ge(s["ok"], 2)
                nc.vector.tensor_tensor(rank[:], rank[:], ties[:], ALU.mult).then_inc(s["tied"], 1)
                dve.wait_ge(s["tied"], 1)
                nc.vector.tensor_tensor(chosen[:], rank[:], hits[:], ALU.add).then_inc(s["sel"], 1)
                ranks(s["sel_ps"])
                dve.wait_ge(s["rank_sb"], 2)
                nc.vector.tensor_tensor(slot[:].rearrange("p (t e) -> p t e", e=NE), rank[:], chosen[:], ALU.mult)\
                    .then_inc(s["slot_sb"], 1)
                dve.wait_ge(s["slot_sb"], 1)

                nc.vector.tensor_scalar(slot_i[:], slot[:], -1.0, None, ALU.add).then_inc(s["int_sb"], 1)
                dve.wait_ge(s["int_sb"], 1)
                nc.vector.tensor_scalar(part_i[:, 0, :], slot_i[:], 4, None, ALU.arith_shift_right).then_inc(s["parts_i"], 1)
                nc.vector.tensor_scalar(part_i[:, 1, :], slot_i[:], B - 1, None, ALU.bitwise_and).then_inc(s["parts_i"], 1)
                dve.wait_ge(s["parts_i"], 2)
                nc.vector.tensor_copy(part[:], part_i[:]).then_inc(s["parts"], 1)
                dve.wait_ge(s["parts"], 1)

                def one_hots(i):
                    for r in range(R):
                        t = R * i + r
                        ge(dve, s["hot_used"], t - R + 1)
                        for which, hot, done in ((1, hot_b[:, r, :].rearrange("p (e b) -> p e b", b=B), s["b_set"]),
                                                 (0, hot_a[:, r, :, :], s["a_set"])):
                            digit = part[:, which, bass.ds(t * NE, NE)].rearrange("p (e one) -> p e one", one=1)
                            nc.vector.tensor_tensor(hot, digit.broadcast_to([P, NE, B]),
                                                    digits[:].rearrange("p (one b) -> p one b", one=1).broadcast_to([P, NE, B]),
                                                    ALU.is_equal).then_inc(done, 1)
                        dve.wait_ge(s["b_set"], t + 1)
                        nc.vector.tensor_tensor(hot_id[:, r, :, :],
                                                hot_b[:, r, :].rearrange("p (n one) -> p n one", one=1).broadcast_to([P, NE * B, 2]),
                                                ids[:, bass.ds(2 * t, 2)].rearrange("p (one c) -> p one c", one=1)
                                                .broadcast_to([P, NE * B, 2]), ALU.mult).then_inc(s["id_set"], 1)
                one_hots(0)
                with dve.Fori(1, NT // R) as i:
                    one_hots(i)
                for seq in range(2):
                    dve.wait_ge(s["hot_used"], tiles[seq].stop)
                    for g in range(2):
                        nc.vector.tensor_copy(lists[:, seq, g, :], ps_l[seq][g][:, 0:COLS]).then_inc(s["copied"], 1)
                        dve.wait_ge(s["copied"], 2 * seq + g + 1)
                        v = lists[:, seq, g, :].rearrange("p (n c) -> p n c", c=2)
                        nc.vector.scalar_tensor_tensor(out=tokens[:, seq, g, :], in0=v[:, :, 0], scalar=float(P), in1=v[:, :, 1],
                                                       op0=ALU.mult, op1=ALU.add).then_inc(s["numbered"], 1)
                dve.wait_ge(s["turned"], 1)
                nc.vector.tensor_copy(slots[:].rearrange("p j e -> p (j e)"), ps_t[:, 0:ST * NE]).then_inc(s["slots_set"], 1)


def expert_phase(nc, A, slots):
    S = ST * P
    UC = 256
    NU = D // UC
    UNITS = [(w, j) for j in range(NU) for w in ("w_gate", "w_up")] + [("w_down", j) for j in range(NU)]
    M = len(UNITS)
    RS, RW = 4, 3
    ROUNDS = 2 * ST
    assert M % RS == 0 and M % RW == 0
    with Phase(nc, "exp") as ph:
        ident = ph.sb("ident", [P, P])
        stage = ph.sb("stage", [P, RS, KC, UC])
        w_hi = ph.sb("w_hi", [P, RW, KC, UC], F32R)
        w_lo = ph.sb("w_lo", [P, RW, KC, UC], F32R)
        xe = ph.sb("xe", [P, 2, ST, XN_COLS])
        xT_hi = ph.sb("xT_hi", [P, KC, S], F32R)
        xT_lo = ph.sb("xT_lo", [P, KC, S], F32R)
        hT_hi = ph.sb("hT_hi", [P, KC, S], F32R)
        hT_lo = ph.sb("hT_lo", [P, KC, S], F32R)
        act_g = ph.sb("act_g", [P, 2, S])
        hid = ph.sb("hid", [P, 2, S])
        ye = ph.sb("ye", [P, ST, D])
        gates = ph.sb("gates", [P, 2, ST])
        ps_g = ph.psum("ps_g", [P, 2, 512])
        ps_u = ph.psum("ps_u", [P, 2, 512])
        ps_d = ph.psum("ps_d", [P, ST, 512])
        ps_t = ph.psum("ps_t", [P, 4, P])
        down_banks = [[ps_d[:, q, :] for q in range(ST)], [ps_g[:, 0, :], ps_g[:, 1, :], ps_u[:, 0, :]]]
        down_banks += [down_banks[0], [ps_u[:, 0, :], ps_u[:, 1, :], ps_t[:].rearrange("p a b -> p (a b)")]]
        first_banks = [ps_t[:]] + [ps_d[:, q, :].rearrange("p (k c) -> p k c", c=P) for q in range(ST)]
        consts = ph.sem("consts")
        loaded = [ph.sem(f"loaded{r}") for r in range(RS)]
        gathered = [ph.sem(f"gathered{u}") for u in range(2)]
        names = "w_hi_sb w_lo_sb unit_done xT_ps xT_hi_sb xT_lo_sb act_sb hid_sb h_hi_sb h_lo_sb scattered gate_sb y_out".split()
        s = {n: ph.sem(n) for n in names}

        def loop(eng, body):
            body(0, False)
            with eng.Fori(1, NE // 2 - 1) as i:
                body(i, False)
            body(NE // 2 - 1, True)

        WITHIN = {8: {2: 0, 5: 1}, 9: {2: 2, 5: 3}, 10: {2: 4, 5: 5}, 11: {}}

        def ahead(e, m, by, more):
            if m + by < M:
                return e, m + by
            return (e + 1, m + by - M) if more else None

        with nc.Block() as block:
            @block.sync
            def _(sp):
                sp.dma_start(ident[:], A["ident"]).then_inc(consts, 16)

                def load(e, m):
                    w, j = UNITS[m]
                    for half in (1, 0):
                        k = half * KC // 2
                        src = A[w][bass.ds(e, 1), k * P:k * P + D // 2, j * UC:(j + 1) * UC]
                        sp.dma_start(stage[:, m % RS, k:k + KC // 2, :], src.rearrange("o (k p) c -> p (o k) c", p=P))\
                            .then_inc(loaded[m % RS], 16)
                for m in range(RS):
                    if m == RW - 1:
                        sp.wait_ge(gathered[0], 16 * ST)
                    load(0, m)

                def body(i, last):
                    for u in range(2):
                        e = 2 * i + u
                        for m in range(M):
                            nxt = ahead(e, m, RS, not (last and u))
                            if nxt:
                                sp.wait_ge(s["w_lo_sb"], e * M + m + 1)
                                load(*nxt)
                loop(sp, body)

            @block.gpsimd
            def _(pool):
                def gather(e):
                    for j in range(ST):
                        nc.gpsimd.indirect_dma_start(xe[:, e % 2, j, :], None, A["xn"],
                                                     bass.IndirectOffsetOnAxis(ap=slots[:, j, e:e + 1], axis=0))\
                            .then_inc(gathered[e % 2], 16)
                def gate(e):
                    pool.wait_ge(gathered[e % 2], 16 * ST * (e // 2 + 1))
                    nc.gpsimd.tensor_copy(gates[:, e % 2, :], xe[:, e % 2, :, D + e]).then_inc(s["gate_sb"], 1)
                for e in range(2):
                    gather(e)
                    gate(e)
                for e in range(NE):
                    pool.wait_ge(s["y_out"], (e + 1) * NU)
                    if e:
                        pool.wait_ge(s["scattered"], 16 * ST * e)
                    for j in range(ST):
                        nc.gpsimd.indirect_dma_start(A["y"], bass.IndirectOffsetOnAxis(ap=slots[:, j, e:e + 1], axis=0),
                                                     ye[:, j, :], None, compute_op=ALU.add).then_inc(s["scattered"], 16)
                    if e + 2 < NE:
                        pool.wait_ge(s["xT_lo_sb"], ROUNDS * (e + 1))
                        pool.wait_ge(s["gate_sb"], e + 1)
                        gather(e + 2)
                        gate(e + 2)
                pool.wait_ge(s["scattered"], 16 * ST * NE)

            @block.scalar
            def _(act):
                def split(e, m):
                    act.wait_ge(loaded[m % RS], 32 * (e * (M // RS) + m // RS + 1))
                    nc.scalar.activation(w_hi[:, m % RW, :, :], stage[:, m % RS, :, :], ACT.Copy).then_inc(s["w_hi_sb"], 1)

                def hi_x(e, r, bank=ps_t[:]):
                    act.wait_ge(s["xT_ps"], e * ROUNDS + r + 1)
                    j, k = r // 2, r % 2 * 4
                    nc.scalar.activation(xT_hi[:, k:k + 4, j * P:(j + 1) * P], bank, ACT.Copy).then_inc(s["xT_hi_sb"], 1)

                def body(i, last):
                    for u in range(2):
                        e = 2 * i + u
                        more = not (last and u)
                        for m, (w, j) in enumerate(UNITS):
                            nxt = ahead(e, m, RW - 1, more)
                            if nxt:
                                ge(act, s["unit_done"], e * M + m)
                                split(*nxt)
                            if w == "w_gate":
                                act.wait_ge(s["unit_done"], e * M + m + 1)
                                ge(act, s["hid_sb"], e * NU + j)
                                nc.scalar.activation(act_g[:], ps_g[:, :, 0:S], ACT.Silu).then_inc(s["act_sb"], 1)
                            elif w == "w_up":
                                act.wait_ge(s["hid_sb"], e * NU + j + 1)
                                nc.scalar.activation(hT_hi[:, 2 * j:2 * j + 2, :], hid[:], ACT.Copy).then_inc(s["h_hi_sb"], 1)
                            else:
                                if more:
                                    for r in WITHIN[m].values():
                                        hi_x(e + 1, r)
                                act.wait_ge(s["unit_done"], e * M + m + 1)
                                ge(act, s["scattered"], 16 * ST * e)
                                if j == 0:
                                    act.wait_ge(s["gate_sb"], e + 1)
                                for q in range(ST):
                                    x_ = nc.scalar.activation(ye[:, q, j * UC:(j + 1) * UC], down_banks[j][q][:, 0:UC], ACT.Copy,
                                                              scale=gates[:, u, q:q + 1])
                                x_.then_inc(s["y_out"], 1)
                for m in range(RW - 1):
                    split(0, m)
                for r in range(ROUNDS):
                    hi_x(0, r, first_banks[r % len(first_banks)])
                loop(act, body)

            @block.vector
            def _(dve):
                def split(e, m):
                    dve.wait_ge(s["w_hi_sb"], e * M + m + 1)
                    nc.vector.tensor_tensor(w_lo[:, m % RW, :, :], stage[:, m % RS, :, :], w_hi[:, m % RW, :, :].bitcast(F32),
                                            ALU.subtract).then_inc(s["w_lo_sb"], 1)

                def lo_x(e, r, bank=ps_t[:]):
                    dve.wait_ge(s["xT_hi_sb"], e * ROUNDS + r + 1)
                    j, k = r // 2, r % 2 * 4
                    to = (slice(None), slice(k, k + 4), slice(j * P, (j + 1) * P))
                    nc.vector.tensor_tensor(xT_lo[to], bank, xT_hi[to].bitcast(F32), ALU.subtract).then_inc(s["xT_lo_sb"], 1)

                def body(i, last):
                    for u in range(2):
                        e = 2 * i + u
                        more = not (last and u)
                        for m, (w, j) in enumerate(UNITS):
                            nxt = ahead(e, m, RW - 1, more)
                            if nxt:
                                split(*nxt)
                            if w == "w_up":
                                dve.wait_ge(s["act_sb"], e * NU + j + 1)
                                dve.wait_ge(s["unit_done"], e * M + m + 1)
                                ge(dve, s["h_lo_sb"], e * NU + j)
                                nc.vector.tensor_tensor(hid[:], act_g[:], ps_u[:, :, 0:S], ALU.mult).then_inc(s["hid_sb"], 1)
                                dve.wait_ge(s["h_hi_sb"], e * NU + j + 1)
                                nc.vector.tensor_tensor(hT_lo[:, 2 * j:2 * j + 2, :], hid[:], hT_hi[:, 2 * j:2 * j + 2, :].bitcast(F32),
                                                        ALU.subtract).then_inc(s["h_lo_sb"], 1)
                            elif w == "w_down" and more:
                                for r in WITHIN[m].values():
                                    lo_x(e + 1, r)
                for m in range(RW - 1):
                    split(0, m)
                for r in range(ROUNDS):
                    lo_x(0, r, first_banks[r % len(first_banks)])
                loop(dve, body)

            @block.tensor
            def _(pe):
                pe.wait_ge(consts, 16)

                def turn(e, u, n, r, banks=(ps_t[:],)):
                    if r == 0:
                        pe.wait_ge(gathered[u], 16 * ST * n)
                    ge(pe, s["xT_lo_sb"], e * ROUNDS + r - len(banks) + 1)
                    j, k0 = r // 2, r % 2 * 4
                    for k in range(4):
                        x_ = nc.tensor.transpose(banks[r % len(banks)][:, k, :], xe[:, u, j, (k0 + k) * P:(k0 + k + 1) * P], ident[:])
                    x_.then_inc(s["xT_ps"], 1)

                def passes(slot, hi, lo):
                    return ((w_lo, hi), (w_hi, lo), (w_hi, hi))

                def body(i, last):
                    for u in range(2):
                        e = 2 * i + u
                        more = not (last and u)
                        for m, (w, j) in enumerate(UNITS):
                            pe.wait_ge(s["w_lo_sb"], e * M + m + 1)
                            if m == 0:
                                pe.wait_ge(s["xT_lo_sb"], ROUNDS * (e + 1))
                            if w != "w_down":
                                ps, free = (ps_g, "act_sb") if w == "w_gate" else (ps_u, "hid_sb")
                                ge(pe, s[free], e * NU + j)
                                if m == 1:
                                    ge(pe, s["y_out"], e * NU)
                                for f in range(2):
                                    n = 0
                                    for k in range(KC):
                                        for a, b in passes(m % RW, xT_hi, xT_lo):
                                            x_ = nc.tensor.matmul(ps[:, f, 0:S], a[:, m % RW, k, f * P:(f + 1) * P], b[:, k, :],
                                                                  start=(n == 0), stop=(n == 3 * KC - 1))
                                            n += 1
                            else:
                                if j == 0:
                                    ge(pe, s["y_out"], e * NU)
                                elif j == 1:
                                    pe.wait_ge(s["act_sb"], (e + 1) * NU)
                                    pe.wait_ge(s["hid_sb"], (e + 1) * NU)
                                else:
                                    pe.wait_ge(s["y_out"], e * NU + j - 1)
                                if j == NU - 1 and more:
                                    pe.wait_ge(s["xT_lo_sb"], ROUNDS * (e + 2))
                                for k in range(KC):
                                    if j == 0 and k % 2 == 0:
                                        pe.wait_ge(s["h_lo_sb"], e * NU + k // 2 + 1)
                                    for q in range(ST):
                                        rows = slice(q * P, (q + 1) * P)
                                        for n, (a, b) in enumerate(passes(m % RW, hT_hi, hT_lo)):
                                            x_ = nc.tensor.matmul(down_banks[j][q][:, 0:UC], b[:, k, rows], a[:, m % RW, k, :],
                                                                  start=(k == 0 and n == 0), stop=(k == KC - 1 and n == 2))
                                    if more and k in WITHIN[m]:
                                        turn(e + 1, 1 - u, i + 1 + u, WITHIN[m][k])
                            x_.then_inc(s["unit_done"], 1)
                for r in range(ROUNDS):
                    turn(0, 0, 1, r, first_banks)
                loop(pe, body)


def final_phase(nc, A):
    R = 4
    with Phase(nc, "fin") as ph:
        g = ph.sb("g", [P, D])
        y = ph.sb("y", [P, R, D])
        out = ph.sb("out", [P, R, D])
        stat = ph.sb("stat", [P, R, 4])
        half = ph.sb("half", [P, 1])
        g_loaded, half_set = ph.sem("g_loaded"), ph.sem("half_set")
        loaded = [ph.sem(f"loaded{r}") for r in range(R)]
        stored = [ph.sem(f"stored{r}") for r in range(R)]
        squared, meaned, powered, normed = (ph.sem(n) for n in ("squared", "meaned", "powered", "normed"))
        with nc.Block() as block:
            @block.sync
            def _(sp):
                sp.dma_start(g[:], A["g_final"]).then_inc(g_loaded, 16)
                for r in range(R):
                    sp.dma_start(y[:, r, :], A["y"][r * P:(r + 1) * P, :]).then_inc(loaded[r], 16)
                with sp.Fori(0, NT // R - 1) as i:
                    for r in range(R):
                        t = R * i + r
                        row = sp.snap((t + R) * P)
                        sp.wait_ge(normed, t + 1)
                        sp.dma_start(y[:, r, :], A["y"][bass.ds(row, P), :]).then_inc(loaded[r], 16)

            @block.scalar
            def _(act):
                def tiles_of(i):
                    for r in range(R):
                        t = R * i + r
                        act.wait_ge(loaded[r], 16 * (i + 1))
                        ge(act, stored[r], 16 * i)
                        nc.scalar.activation(out[:, r, :], y[:, r, :], ACT.Square, accum_out=stat[:, r, 0:1]).then_inc(squared, 1)
                tiles_of(0)
                with act.Fori(1, NT // R) as i:
                    tiles_of(i)

            @block.gpsimd
            def _(pool):
                nc.gpsimd.memset(half[:], -0.5).then_inc(half_set, 1)
                pool.wait_ge(half_set, 1)
                with pool.Fori(0, NT // R) as i:
                    for r in range(R):
                        t = R * i + r
                        pool.wait_ge(meaned, t + 1)
                        nc.gpsimd.tensor_tensor(stat[:, r, 2:3], stat[:, r, 1:2], half[:], ALU.pow).then_inc(powered, 1)
                        pool.wait_ge(normed, t + 1)
                        nc.gpsimd.dma_start(A["out"][bass.ds(t * P, P), :], out[:, r, :]).then_inc(stored[r], 16)
                for r in range(R):
                    pool.wait_ge(stored[r], 16 * (NT // R))

            @block.vector
            def _(dve):
                dve.wait_ge(g_loaded, 16)
                with dve.Fori(0, NT // R) as i:
                    for r in range(R):
                        t = R * i + r
                        dve.wait_ge(squared, t + 1)
                        nc.vector.tensor_scalar(stat[:, r, 1:2], stat[:, r, 0:1], 1.0 / D, EPS, ALU.mult, ALU.add).then_inc(meaned, 1)
                        dve.wait_ge(powered, t + 1)
                        nc.vector.scalar_tensor_tensor(out=out[:, r, :], in0=y[:, r, :], scalar=stat[:, r, 2:3], in1=g[:],
                                                       op0=ALU.mult, op1=ALU.mult).then_inc(normed, 1)


DRAM_IN = dict(x=(TOK, D), mem=(2 * MEM, D), w_in=(D, D_IN), w_mem_kv=(D, 2 * D_C), w_out=(D, D), w_router=(D, NE),
               w_gate=(NE, D, D), w_up=(NE, D, D), w_down=(NE, D, D), g_mix=(P, KC), g_mem=(P, KC), g_out=(P, KC),
               w_sT=(P, GB, P), b_sT=(P, GB), ln_g=(P, D_B), ln_b=(P, D_B), g_ffn=(P, D), g_final=(P, D),
               ident=(P, P), cossin=(TOK, 4 * HD // 2), masks=(P, 5, 2 * P), tri=(P, P), ids=(P, 2 * NT), digits=(P, 16),
               bits=(P, BITS))
SCRATCH = dict(qT=(P, HA // 2, TOK), kT=(P, HA // 2, TOK), v=(KV_ROWS, D_A), obc=(TOK, D_B + D_C), o0=(TOK, O_COLS), o1=(TOK, O_COLS),
               o2=(TOK, O_COLS), xn=(TOK, XN_COLS), y=(TOK, D), lists=(2, 2, P * P + P))


def build(nc, A, upto=99):
    with Phase(nc, "memory") as keep:
        kmT = keep.sb("kmT", [P, 2, 2, MEM])
        vm = keep.sb("vm", [P, 2, 2, D_C])
        w_hi = keep.sb("w_hi", [P, KC, D_IN], F32R)
        w_lo = keep.sb("w_lo", [P, KC, D_IN], F32R)
        memory_phase(nc, A, kmT, vm, w_hi, w_lo)
        if upto >= 1:
            project_phase(nc, A, kmT, vm, w_hi, w_lo)
    with Phase(nc, "route") as keep:
        slots = keep.sb("slots", [P, ST, NE], I32)
        affinity = keep.sb("affinity", [P, NT * NE])
        with Phase(nc, "out") as out:
            w_out = out.sb("w_out", [P, KC, D])
            if upto >= 2:
                attend_phase(nc, A, w_out)
            if upto >= 3:
                mix_phase(nc, A, affinity, w_out)
        if upto >= 4:
            choose_phase(nc, A, affinity, slots)
        if upto >= 5:
            expert_phase(nc, A, slots)
    if upto >= 6:
        final_phase(nc, A)


def constants():
    pos = np.concatenate([np.arange(s, dtype=np.float32) for s in SEQS])
    half = HD // 2
    inv = np.power(10000.0, -np.arange(half) * 2.0 / HD).astype(np.float32)
    ang = pos[:, None] * inv[None, :].astype(np.float32)
    cos, sin = np.cos(ang), np.sin(ang)
    cossin = np.concatenate([cos, cos, -sin, sin], axis=1).astype(np.float32)
    t, w = np.arange(P)[:, None], np.arange(2 * P)[None, :]
    band = np.abs(w - 64 - t) <= 64
    masks = np.zeros((P, 5, 2 * P), np.float32)
    masks[:, 0] = np.where(band & (w >= 64), 0, NEG)
    masks[:, 1] = np.where(band, 0, NEG)
    masks[:, 2] = np.where(band & (w < 64 + P), 0, NEG)
    masks[:, 3, :P] = np.where(np.abs(w[:, :P] - t) <= 64, 0, NEG)
    masks[:, 4, :P] = np.where(w[:, :P] // 64 == t // 64, 0, NEG)
    tri = (np.arange(P)[:, None] <= np.arange(P)[None, :]).astype(np.float32)
    ids = np.zeros((P, NT, 2), np.float32)
    ids[:, :, 0] = np.arange(NT)[None, :]
    ids[:, :, 1] = np.arange(P)[:, None]
    digits = np.broadcast_to(np.arange(16, dtype=np.float32), (P, 16))
    bits = (1 << np.arange(BITS - 1, -1, -1, dtype=np.int32)).astype(np.int32)
    return dict(ident=np.eye(P, dtype=np.float32), cossin=cossin, masks=masks, tri=tri, ids=ids.reshape(P, 2 * NT),
                digits=digits, bits=np.broadcast_to(bits.view(np.float32), (P, BITS)))


def lay_out(i):
    rows = lambda v: np.broadcast_to(np.asarray(v).reshape(1, -1), (P, v.size))
    cols = lambda v: np.asarray(v).reshape(KC, P).T
    a = {k: np.asarray(v) for k, v in i.items()}
    return dict(
        x=np.concatenate([a["x_prompt"][0], a["x_sample"][0]]), mem=np.concatenate([a["mem_prompt"][0], a["mem_sample"][0]]),
        w_in=a["w_in"][0], w_mem_kv=a["w_mem_kv"][0], w_out=a["w_out"][0], w_router=a["w_router"][0],
        w_gate=a["w_gate"][0], w_up=a["w_up"][0], w_down=a["w_down"][0],
        g_mix=cols(a["g_mix"]), g_mem=cols(a["g_mem"]), g_out=cols(a["g_out"]),
        w_sT=a["w_spatial"][0].transpose(2, 0, 1), b_sT=a["b_spatial"][0].T, ln_g=rows(a["ln_b_g"]), ln_b=rows(a["ln_b_b"]),
        g_ffn=rows(a["g_ffn"]), g_final=rows(a["g_final"]), **constants())


def kernel(**inputs):
    import concourse.bacc as bacc
    from concourse.bass_utils import run_bass_kernel_spmd

    nc = bacc.Bacc("TRN2", target_bir_lowering=False, num_devices=1)
    laid = lay_out(inputs)
    arrays, A = {}, {}
    for name, shape in DRAM_IN.items():
        arrays[f"in_{name}"] = np.ascontiguousarray(laid[name])
        A[name] = nc.dram_tensor(f"in_{name}", shape, F32, kind="ExternalInput").ap()
    for name, shape in SCRATCH.items():
        A[name] = nc.dram_tensor(f"scratch_{name}", shape, F32, kind="Internal").ap()
    A["out"] = nc.dram_tensor("out", (TOK, D), F32, kind="ExternalOutput").ap()
    build(nc, A)
    out = run_bass_kernel_spmd(nc, [arrays], core_ids=[0]).results[0]["out"]
    return out[None, :SEQS[0]], out[None, SEQS[0]:]
```
